# Optimizing a Trainium2 kernel written in Bass

```python
import math
import jax
import jax.numpy as jnp
from jax import lax
import numpy as np

D_MODEL = 1024
BATCH = 1
SEQ = 256
DEPTH = 1

GLA_HEADS = 4
GLA_DK = 128
GLA_DV = 256
GLA_RANK = 16
GLA_TAU = 16.0
GLA_CHUNK = 64
MOBA_HEADS = 8
MOBA_DH = 64
MOBA_BLOCK = 256
MOBA_TOPK = 3
MOBA_Q_CHUNK = 16
REL_BUCKETS = 32
REL_MAX_DIST = 128
D_FF = 2816
CONV_W = 3
EPS = 1e-6
N_BRANCHES = 2
NEG_INF = -1e30

GLA_QK_W = GLA_HEADS * GLA_DK
GLA_V_W = GLA_HEADS * GLA_DV
MOBA_W = MOBA_HEADS * MOBA_DH
IN_SPLITS = (GLA_QK_W, GLA_QK_W, GLA_V_W, GLA_V_W, GLA_RANK, MOBA_W, MOBA_W, MOBA_W, N_BRANCHES * D_MODEL)
D_IN = 2 * GLA_QK_W + 2 * GLA_V_W + GLA_RANK + 3 * MOBA_W + N_BRANCHES * D_MODEL


def rmsnorm(x, g):
    xf = x.astype(jnp.float32)
    y = xf * lax.rsqrt(jnp.mean(xf * xf, axis=-1, keepdims=True) + EPS)
    return (y * g.astype(jnp.float32)).astype(x.dtype)

def gla_chunked(q, k, v, log_a):
    B, T, H, DK = q.shape
    DV = v.shape[-1]
    C = GLA_CHUNK
    NC = T // C

    def to_chunks(t):
        return t.astype(jnp.float32).reshape(B, NC, C, H, t.shape[-1]).transpose(0, 3, 1, 2, 4)

    q, k, v, log_a = map(to_chunks, (q, k, v, log_a))
    q = q * (DK ** -0.5)
    b = jnp.cumsum(log_a, axis=3)
    b_last = b[:, :, :, -1:, :]
    q_dec = q * jnp.exp(b)
    k_dec = k * jnp.exp(-b)
    k_to_end = k * jnp.exp(b_last - b)
    causal = jnp.tril(jnp.ones((C, C), dtype=bool))
    attn = jnp.where(causal, jnp.einsum('bhnid,bhnjd->bhnij', q_dec, k_dec), 0.0)
    o_intra = jnp.einsum('bhnij,bhnjv->bhniv', attn, v)

    def step(S, inp):
        qc, kc, vc, dec = inp
        o = jnp.einsum('bhid,bhdv->bhiv', qc, S)
        S = S * dec[..., None] + jnp.einsum('bhjd,bhjv->bhdv', kc, vc)
        return S, o

    xs = (jnp.moveaxis(q_dec, 2, 0), jnp.moveaxis(k_to_end, 2, 0), jnp.moveaxis(v, 2, 0),
          jnp.moveaxis(jnp.exp(b_last[:, :, :, 0, :]), 2, 0))
    S0 = jnp.zeros((B, H, DK, DV), jnp.float32)
    _, o_inter = lax.scan(step, S0, xs)
    o = o_intra + jnp.moveaxis(o_inter, 0, 2)
    return o.transpose(0, 2, 3, 1, 4).reshape(B, T, H, DV)

def t5_bucket(rel):
    n = jnp.maximum(rel, 0)
    max_exact = REL_BUCKETS // 2
    nf = jnp.maximum(n, 1).astype(jnp.float32)
    large = max_exact + (jnp.log(nf / max_exact) / math.log(REL_MAX_DIST / max_exact)
                         * (REL_BUCKETS - max_exact)).astype(jnp.int32)
    large = jnp.minimum(large, REL_BUCKETS - 1)
    return jnp.where(n < max_exact, n, large)

def moba_attention(q, k, v, rel_bias):
    B, T, H, DH = q.shape
    NB = -(-T // MOBA_BLOCK)
    T_pad = NB * MOBA_BLOCK
    pad = ((0, 0), (0, T_pad - T), (0, 0), (0, 0))
    q, k, v = (jnp.pad(t, pad) for t in (q, k, v))
    QC = MOBA_Q_CHUNK
    NQ = T_pad // QC
    KSEL = min(MOBA_TOPK, NB)
    KB = KSEL * MOBA_BLOCK
    scale = DH ** -0.5
    k_blocks = k.transpose(0, 2, 1, 3).reshape(B, H, NB, MOBA_BLOCK, DH)
    v_blocks = v.transpose(0, 2, 1, 3).reshape(B, H, NB, MOBA_BLOCK, DH)
    k_mean = jnp.mean(k_blocks.astype(jnp.float32), axis=3)
    bias_tab = rel_bias.T.astype(jnp.float32)
    b_idx = jnp.arange(B)[:, None, None, None]
    h_idx = jnp.arange(H)[None, :, None, None]
    k_in_blk = jnp.arange(MOBA_BLOCK)
    q_chunks = q.transpose(0, 2, 1, 3).reshape(B, H, NQ, QC, DH).transpose(2, 0, 1, 3, 4)

    def one_chunk(args):
        qc, c = args
        q_pos = c * QC + jnp.arange(QC)
        q_blk = (c * QC) // MOBA_BLOCK
        gate = jnp.einsum('bhqd,bhnd->bhqn', qc.astype(jnp.float32), k_mean)
        gate = jnp.where(jnp.arange(NB) < q_blk, gate, -jnp.inf)
        _, sel = lax.top_k(gate, KSEL)
        sel_valid = jnp.repeat(sel < q_blk, MOBA_BLOCK, axis=-1)
        k_sel = k_blocks[b_idx, h_idx, sel].reshape(B, H, QC, KB, DH)
        v_sel = v_blocks[b_idx, h_idx, sel].reshape(B, H, QC, KB, DH)
        kpos_sel = (sel[..., None] * MOBA_BLOCK + k_in_blk).reshape(B, H, QC, KB)
        logit_sel = jnp.einsum('bhqd,bhqkd->bhqk', qc, k_sel).astype(jnp.float32) * scale
        logit_sel = logit_sel + bias_tab[h_idx, t5_bucket(q_pos[:, None] - kpos_sel)]
        logit_sel = jnp.where(sel_valid, logit_sel, NEG_INF)
        k_own = lax.dynamic_index_in_dim(k_blocks, q_blk, axis=2, keepdims=False)
        v_own = lax.dynamic_index_in_dim(v_blocks, q_blk, axis=2, keepdims=False)
        kpos_own = q_blk * MOBA_BLOCK + k_in_blk
        logit_own = jnp.einsum('bhqd,bhkd->bhqk', qc, k_own).astype(jnp.float32) * scale
        logit_own = logit_own + bias_tab[:, t5_bucket(q_pos[:, None] - kpos_own[None, :])]
        logit_own = jnp.where(kpos_own[None, :] <= q_pos[:, None], logit_own, NEG_INF)
        p = jax.nn.softmax(jnp.concatenate([logit_sel, logit_own], axis=-1), axis=-1).astype(v.dtype)
        return (jnp.einsum('bhqk,bhqkd->bhqd', p[..., :KB], v_sel)
                + jnp.einsum('bhqk,bhkd->bhqd', p[..., KB:], v_own))

    o = lax.map(one_chunk, (q_chunks, jnp.arange(NQ)))
    o = o.transpose(1, 0, 3, 2, 4).reshape(B, T_pad, H * DH)
    return o[:, :T]

def causal_dwconv(u, w, b):
    out = lax.conv_general_dilated(u, w[:, None, :].astype(u.dtype), window_strides=(1,),
                                   padding=[(CONV_W - 1, 0)], dimension_numbers=('NWC', 'WIO', 'NWC'),
                                   feature_group_count=u.shape[-1])
    return out + b.astype(u.dtype)

def hybrid_layer(x, rel_bias, norm_mix, w_in, w_lr_up, b_forget, gla_out_norm, w_branch_gla,
                 w_branch_moba, w_out, norm_ffn, w_up, conv_w, conv_b, w_down):
    B, T, _ = x.shape
    h = rmsnorm(x, norm_mix)
    proj = h @ w_in
    points = [int(p) for p in np.cumsum(IN_SPLITS)[:-1]]
    qa, ka, va, ra, a_lr, qb, kb, vb, gates = jnp.split(proj, points, axis=-1)
    log_a = jax.nn.log_sigmoid((a_lr @ w_lr_up + b_forget).astype(jnp.float32)) / GLA_TAU
    oa = gla_chunked(qa.reshape(B, T, GLA_HEADS, GLA_DK), ka.reshape(B, T, GLA_HEADS, GLA_DK),
                     va.reshape(B, T, GLA_HEADS, GLA_DV), log_a.reshape(B, T, GLA_HEADS, GLA_DK))
    oa = oa * lax.rsqrt(jnp.mean(oa * oa, axis=-1, keepdims=True) + EPS)
    oa = (oa.reshape(B, T, GLA_V_W) * gla_out_norm.astype(jnp.float32)).astype(x.dtype) * jax.nn.silu(ra)
    ob = moba_attention(qb.reshape(B, T, MOBA_HEADS, MOBA_DH), kb.reshape(B, T, MOBA_HEADS, MOBA_DH),
                        vb.reshape(B, T, MOBA_HEADS, MOBA_DH), rel_bias)
    g_a, g_b = jnp.split(jax.nn.sigmoid(gates), 2, axis=-1)
    mixed = g_a * (oa @ w_branch_gla) + g_b * (ob @ w_branch_moba)
    x = x + mixed @ w_out
    h = rmsnorm(x, norm_ffn)
    u = causal_dwconv(h @ w_up, conv_w, conv_b)
    a, bval = jnp.split(u, 2, axis=-1)
    return x + (jax.nn.silu(a) * bval) @ w_down

def first_inputs(seed: int = 0) -> dict:
    key = jax.random.key(seed)
    ks = jax.random.split(key, 16)

    def nrm(k, shape, scale):
        return jax.random.normal(k, shape, jnp.float32) * scale

    return {
        'x': nrm(ks[0], (BATCH, SEQ, D_MODEL), 1.0),
        'rel_bias': nrm(ks[1], (REL_BUCKETS, MOBA_HEADS), 0.5),
        'norm_mix': 1.0 + nrm(ks[2], (DEPTH, D_MODEL), 0.05),
        'w_in': nrm(ks[3], (DEPTH, D_MODEL, D_IN), D_MODEL ** -0.5),
        'w_lr_up': nrm(ks[4], (DEPTH, GLA_RANK, GLA_QK_W), GLA_RANK ** -0.5),
        'b_forget': 1.0 + nrm(ks[5], (DEPTH, GLA_QK_W), 0.5),
        'gla_out_norm': 1.0 + nrm(ks[6], (DEPTH, GLA_V_W), 0.05),
        'w_branch_gla': nrm(ks[7], (DEPTH, GLA_V_W, D_MODEL), GLA_V_W ** -0.5),
        'w_branch_moba': nrm(ks[8], (DEPTH, MOBA_W, D_MODEL), MOBA_W ** -0.5),
        'w_out': nrm(ks[9], (DEPTH, D_MODEL, D_MODEL), D_MODEL ** -0.5),
        'norm_ffn': 1.0 + nrm(ks[10], (DEPTH, D_MODEL), 0.05),
        'w_up': nrm(ks[11], (DEPTH, D_MODEL, 2 * D_FF), D_MODEL ** -0.5),
        'conv_w': nrm(ks[12], (DEPTH, CONV_W, 2 * D_FF), CONV_W ** -0.5),
        'conv_b': nrm(ks[13], (DEPTH, 2 * D_FF), 0.02),
        'w_down': nrm(ks[14], (DEPTH, D_FF, D_MODEL), D_FF ** -0.5),
        'norm_final': 1.0 + nrm(ks[15], (D_MODEL,), 0.05),
    }

def first_block(x, rel_bias, norm_mix, w_in, w_lr_up, b_forget, gla_out_norm, w_branch_gla,
              w_branch_moba, w_out, norm_ffn, w_up, conv_w, conv_b, w_down, norm_final):
    for l in range(DEPTH):
        x = hybrid_layer(x, rel_bias, norm_mix[l], w_in[l], w_lr_up[l], b_forget[l], gla_out_norm[l],
                         w_branch_gla[l], w_branch_moba[l], w_out[l], norm_ffn[l], w_up[l], conv_w[l],
                         conv_b[l], w_down[l])
    return rmsnorm(x, norm_final)


DEPTH_2 = 2

GRID_W = 64
CTX_LEN = 256
N_MIXERS = 2
N_CONV_LAYERS = (DEPTH_2 + 1) // 2
N_ATTN_LAYERS = DEPTH_2 // 2
CONV_WIDTH = 31
HEAD_DIM = 64
N_HEADS = D_MODEL // HEAD_DIM
N_KV_HEADS = N_HEADS // 4
GQA_GROUP = N_HEADS // N_KV_HEADS
QKV_DIM = (N_HEADS + 2 * N_KV_HEADS) * HEAD_DIM
WINDOW = 128
BLOCK = 128
ROPE_BASE = 10000.0
FFN_CONV_WIDTH = 3
NEG = -1e30


def rmsnorm_2(x, g):
    xf = x.astype(jnp.float32)
    y = xf * lax.rsqrt(jnp.mean(xf * xf, axis=-1, keepdims=True) + EPS)
    return (y * g.astype(jnp.float32)).astype(x.dtype)

def layernorm(x, g, b):
    xf = x.astype(jnp.float32)
    mu = jnp.mean(xf, axis=-1, keepdims=True)
    var = jnp.mean(jnp.square(xf - mu), axis=-1, keepdims=True)
    y = (xf - mu) * lax.rsqrt(var + EPS)
    return (y * g.astype(jnp.float32) + b.astype(jnp.float32)).astype(x.dtype)

def modulate(x, shift, scale):
    return x * (1.0 + scale) + shift

def dwconv(x, w, b):
    k = w.shape[0]
    pad = (k - 1) // 2
    y = lax.conv_general_dilated(x, w[:, None, :], window_strides=(1,), padding=[(pad, pad)],
                                 dimension_numbers=('NWC', 'WIO', 'NWC'),
                                 feature_group_count=x.shape[-1])
    return y + b

def axial_rope_tables(seq_len):
    rows = seq_len // GRID_W
    row = jnp.broadcast_to(jnp.arange(rows)[:, None], (rows, GRID_W)).reshape(-1).astype(jnp.float32)
    col = jnp.broadcast_to(jnp.arange(GRID_W)[None, :], (rows, GRID_W)).reshape(-1).astype(jnp.float32)
    n_freq = HEAD_DIM // 4
    inv = ROPE_BASE ** (-jnp.arange(n_freq, dtype=jnp.float32) / n_freq)
    ang = jnp.concatenate([row[:, None] * inv, col[:, None] * inv], axis=-1)
    return jnp.cos(ang), jnp.sin(ang)

def apply_rope(x, cos, sin):
    xf = x.astype(jnp.float32)
    half = HEAD_DIM // 2
    x1, x2 = xf[..., :half], xf[..., half:]
    c = cos[None, :, None, :]
    s = sin[None, :, None, :]
    return jnp.concatenate([x1 * c - x2 * s, x2 * c + x1 * s], axis=-1).astype(x.dtype)

def conformer_conv(h, w_pw1, b_pw1, w_dw, b_dw, ln_g, ln_b, w_pw2, b_pw2):
    u = h @ w_pw1 + b_pw1
    a, g = jnp.split(u, 2, axis=-1)
    v = a * jax.nn.sigmoid(g)
    v = dwconv(v, w_dw, b_dw)
    v = jax.nn.silu(layernorm(v, ln_g, ln_b))
    return v @ w_pw2 + b_pw2

def conv_ffn(h, w_up, w_dw, b_dw, w_down):
    u = dwconv(h @ w_up, w_dw, b_dw)
    a, b = jnp.split(u, 2, axis=-1)
    return (jax.nn.silu(a) * b) @ w_down

def split_qkv(h, w_qkv):
    bsz, length, _ = h.shape
    qkv = h @ w_qkv
    q = qkv[..., :N_HEADS * HEAD_DIM].reshape(bsz, length, N_HEADS, HEAD_DIM)
    k = qkv[..., N_HEADS * HEAD_DIM:(N_HEADS + N_KV_HEADS) * HEAD_DIM].reshape(bsz, length, N_KV_HEADS, HEAD_DIM)
    v = qkv[..., (N_HEADS + N_KV_HEADS) * HEAD_DIM:].reshape(bsz, length, N_KV_HEADS, HEAD_DIM)
    return q, k, v

def sink_logits(sink, bsz, nq):
    s = sink.astype(jnp.float32).reshape(N_KV_HEADS, GQA_GROUP)[None, :, :, None, None]
    return jnp.broadcast_to(s, (bsz, N_KV_HEADS, GQA_GROUP, nq, 1))

def window_attention(h_lat, h_ctx, w_qkv, w_o, sink, cos, sin, with_ctx_out):
    bsz, seq, _ = h_lat.shape
    scale = HEAD_DIM ** -0.5
    qc, kc, vc = split_qkv(h_ctx, w_qkv)
    q, k, v = split_qkv(h_lat, w_qkv)
    q = apply_rope(q, cos, sin) * scale
    k = apply_rope(k, cos, sin)
    q = q.reshape(bsz, seq, N_KV_HEADS, GQA_GROUP, HEAD_DIM)
    nb = seq // BLOCK
    k_pad = jnp.pad(k, ((0, 0), (BLOCK, BLOCK), (0, 0), (0, 0)))
    v_pad = jnp.pad(v, ((0, 0), (BLOCK, BLOCK), (0, 0), (0, 0)))
    q_blocks = jnp.moveaxis(q.reshape(bsz, nb, BLOCK, N_KV_HEADS, GQA_GROUP, HEAD_DIM), 1, 0)
    s_sink_lat = sink_logits(sink, bsz, BLOCK)

    def block_fn(args):
        i, qb = args
        kb = lax.dynamic_slice_in_dim(k_pad, i * BLOCK, 3 * BLOCK, axis=1)
        vb = lax.dynamic_slice_in_dim(v_pad, i * BLOCK, 3 * BLOCK, axis=1)
        qpos = i * BLOCK + jnp.arange(BLOCK)
        kpos = i * BLOCK - BLOCK + jnp.arange(3 * BLOCK)
        valid = (jnp.abs(qpos[:, None] - kpos[None, :]) <= WINDOW) & (kpos[None, :] >= 0) & (kpos[None, :] < seq)
        s_band = jnp.einsum('bqhgd,bkhd->bhgqk', qb, kb).astype(jnp.float32)
        s_band = jnp.where(valid[None, None, None], s_band, NEG)
        s_ctx = jnp.einsum('bqhgd,bkhd->bhgqk', qb, kc).astype(jnp.float32)
        p = jax.nn.softmax(jnp.concatenate([s_band, s_ctx, s_sink_lat], axis=-1), axis=-1)
        p_band = p[..., :3 * BLOCK].astype(vb.dtype)
        p_ctx = p[..., 3 * BLOCK:3 * BLOCK + CTX_LEN].astype(vc.dtype)
        o = jnp.einsum('bhgqk,bkhd->bqhgd', p_band, vb) + jnp.einsum('bhgqk,bkhd->bqhgd', p_ctx, vc)
        return o

    o_blocks = lax.map(block_fn, (jnp.arange(nb), q_blocks))
    o_lat = jnp.moveaxis(o_blocks, 0, 1).reshape(bsz, seq, N_HEADS * HEAD_DIM) @ w_o

    o_ctx = None
    if with_ctx_out:
        qcs = (qc * scale).reshape(bsz, CTX_LEN, N_KV_HEADS, GQA_GROUP, HEAD_DIM)
        s_c = jnp.einsum('bqhgd,bkhd->bhgqk', qcs, kc).astype(jnp.float32)
        p_c = jax.nn.softmax(jnp.concatenate([s_c, sink_logits(sink, bsz, CTX_LEN)], axis=-1), axis=-1)
        oc = jnp.einsum('bhgqk,bkhd->bqhgd', p_c[..., :CTX_LEN].astype(vc.dtype), vc)
        o_ctx = oc.reshape(bsz, CTX_LEN, N_HEADS * HEAD_DIM) @ w_o
    return o_lat, o_ctx

def second_inputs(seed: int = 0) -> dict:
    key = jax.random.key(seed)
    ks = jax.random.split(key, 32)
    D = D_MODEL

    def nrm(k, shape, scale):
        return jax.random.normal(k, shape, jnp.float32) * scale

    return {
        'x': nrm(ks[0], (BATCH, SEQ, D), 1.0),
        'c': nrm(ks[1], (BATCH, D), 1.0),
        'ctx': nrm(ks[2], (BATCH, CTX_LEN, D), 1.0),
        'c_ctx': nrm(ks[3], (D,), 1.0),
        'ada_w': nrm(ks[4], (DEPTH_2, D, 6 * D), 0.02),
        'ada_b': nrm(ks[5], (DEPTH_2, 6 * D), 0.02),
        'norm1_g': 1.0 + nrm(ks[6], (DEPTH_2, D), 0.05),
        'norm2_g': 1.0 + nrm(ks[7], (DEPTH_2, D), 0.05),
        'final_g': 1.0 + nrm(ks[8], (D,), 0.05),
        'conv_w_pw1': nrm(ks[9], (N_CONV_LAYERS, D, 2 * D), D ** -0.5),
        'conv_b_pw1': nrm(ks[10], (N_CONV_LAYERS, 2 * D), 0.02),
        'conv_w_dw': nrm(ks[11], (N_CONV_LAYERS, CONV_WIDTH, D), CONV_WIDTH ** -0.5),
        'conv_b_dw': nrm(ks[12], (N_CONV_LAYERS, D), 0.02),
        'conv_ln_g': 1.0 + nrm(ks[13], (N_CONV_LAYERS, D), 0.05),
        'conv_ln_b': nrm(ks[14], (N_CONV_LAYERS, D), 0.02),
        'conv_w_pw2': nrm(ks[15], (N_CONV_LAYERS, D, D), D ** -0.5),
        'conv_b_pw2': nrm(ks[16], (N_CONV_LAYERS, D), 0.02),
        'attn_w_qkv': nrm(ks[17], (N_ATTN_LAYERS, D, QKV_DIM), D ** -0.5),
        'attn_w_o': nrm(ks[18], (N_ATTN_LAYERS, N_HEADS * HEAD_DIM, D), (N_HEADS * HEAD_DIM) ** -0.5),
        'attn_sink': nrm(ks[19], (N_ATTN_LAYERS, N_HEADS), 1.0),
        'ffn_w_up': nrm(ks[20], (DEPTH_2, D, 2 * D_FF), D ** -0.5),
        'ffn_w_dw': nrm(ks[21], (DEPTH_2, FFN_CONV_WIDTH, 2 * D_FF), FFN_CONV_WIDTH ** -0.5),
        'ffn_b_dw': nrm(ks[22], (DEPTH_2, 2 * D_FF), 0.02),
        'ffn_w_down': nrm(ks[23], (DEPTH_2, D_FF, D), D_FF ** -0.5),
    }

def second_block(x, c, ctx, c_ctx, ada_w, ada_b, norm1_g, norm2_g, final_g,
              conv_w_pw1, conv_b_pw1, conv_w_dw, conv_b_dw, conv_ln_g, conv_ln_b, conv_w_pw2, conv_b_pw2,
              attn_w_qkv, attn_w_o, attn_sink,
              ffn_w_up, ffn_w_dw, ffn_b_dw, ffn_w_down):
    cos, sin = axial_rope_tables(x.shape[1])
    sc = jax.nn.silu(c)
    scc = jax.nn.silu(c_ctx)
    h_lat = x
    h_ctx = ctx
    for i in range(DEPTH_2):
        last = i == DEPTH_2 - 1
        mod_lat = (sc @ ada_w[i] + ada_b[i])[:, None, :]
        mod_ctx = scc @ ada_w[i] + ada_b[i]
        sh1, sc1, g1, sh2, sc2, g2 = jnp.split(mod_lat, 6, axis=-1)
        csh1, csc1, cg1, csh2, csc2, cg2 = jnp.split(mod_ctx, 6, axis=-1)
        a_lat = modulate(rmsnorm_2(h_lat, norm1_g[i]), sh1, sc1)
        j = i // N_MIXERS
        if i % N_MIXERS == 0:
            y_lat = conformer_conv(a_lat, conv_w_pw1[j], conv_b_pw1[j], conv_w_dw[j], conv_b_dw[j],
                                   conv_ln_g[j], conv_ln_b[j], conv_w_pw2[j], conv_b_pw2[j])
            if not last:
                a_ctx = modulate(rmsnorm_2(h_ctx, norm1_g[i]), csh1, csc1)
                y_ctx = conformer_conv(a_ctx, conv_w_pw1[j], conv_b_pw1[j], conv_w_dw[j], conv_b_dw[j],
                                       conv_ln_g[j], conv_ln_b[j], conv_w_pw2[j], conv_b_pw2[j])
        else:
            a_ctx = modulate(rmsnorm_2(h_ctx, norm1_g[i]), csh1, csc1)
            y_lat, y_ctx = window_attention(a_lat, a_ctx, attn_w_qkv[j], attn_w_o[j], attn_sink[j],
                                            cos, sin, not last)
        h_lat = h_lat + g1 * y_lat
        b_lat = modulate(rmsnorm_2(h_lat, norm2_g[i]), sh2, sc2)
        h_lat = h_lat + g2 * conv_ffn(b_lat, ffn_w_up[i], ffn_w_dw[i], ffn_b_dw[i], ffn_w_down[i])
        if not last:
            h_ctx = h_ctx + cg1 * y_ctx
            b_ctx = modulate(rmsnorm_2(h_ctx, norm2_g[i]), csh2, csc2)
            h_ctx = h_ctx + cg2 * conv_ffn(b_ctx, ffn_w_up[i], ffn_w_dw[i], ffn_b_dw[i], ffn_w_down[i])
    return rmsnorm_2(h_lat, final_g)


def setup_inputs(seed=0):
    out = dict(first_inputs(seed))
    for name, value in second_inputs(seed + 1).items():
        if name != "x":
            out[name + "_2"] = value
    return out


def reference(
    x, rel_bias, norm_mix, w_in, w_lr_up, b_forget, gla_out_norm, w_branch_gla, w_branch_moba,
    w_out, norm_ffn, w_up, conv_w, conv_b, w_down, norm_final, c_2, ctx_2, c_ctx_2, ada_w_2,
    ada_b_2, norm1_g_2, norm2_g_2, final_g_2, conv_w_pw1_2, conv_b_pw1_2, conv_w_dw_2,
    conv_b_dw_2, conv_ln_g_2, conv_ln_b_2, conv_w_pw2_2, conv_b_pw2_2, attn_w_qkv_2, attn_w_o_2,
    attn_sink_2, ffn_w_up_2, ffn_w_dw_2, ffn_b_dw_2, ffn_w_down_2,
):
    x = first_block(
        x, rel_bias, norm_mix, w_in, w_lr_up, b_forget, gla_out_norm, w_branch_gla,
        w_branch_moba, w_out, norm_ffn, w_up, conv_w, conv_b, w_down, norm_final,
    )
    return second_block(
        x, c_2, ctx_2, c_ctx_2, ada_w_2, ada_b_2, norm1_g_2, norm2_g_2, final_g_2, conv_w_pw1_2,
        conv_b_pw1_2, conv_w_dw_2, conv_b_dw_2, conv_ln_g_2, conv_ln_b_2, conv_w_pw2_2,
        conv_b_pw2_2, attn_w_qkv_2, attn_w_o_2, attn_sink_2, ffn_w_up_2, ffn_w_dw_2, ffn_b_dw_2,
        ffn_w_down_2,
    )


_drawn_inputs = setup_inputs


def setup_inputs(seed=0):
    import zlib

    import numpy as np

    out = dict(_drawn_inputs(seed))
    spreads = {}
    factors = {'gla_out_norm': 2.974,
     'conv_b': 3.764,
     'norm1_g_2': 4.141,
     'conv_b_pw1_2': 8.0,
     'conv_b_dw_2': 7.011,
     'conv_ln_g_2': 3.887,
     'conv_ln_b_2': 8.0,
     'conv_b_pw2_2': 6.732,
     'attn_sink_2': 64.0,
     'ffn_b_dw_2': 5.431}
    for name, (base, spread) in spreads.items():
        noise = np.random.default_rng([zlib.crc32(name.encode()), seed]).standard_normal(out[name].shape)
        drawn = base * np.exp(spread * noise) if base else spread * noise
        out[name] = jnp.asarray(drawn.astype(out[name].dtype))
    for name, factor in factors.items():
        out[name] = (out[name] * factor).astype(out[name].dtype)
    return out
```

```python
from contextlib import ExitStack

import numpy as np

import concourse.bass as bass
from concourse import mybir

F32 = mybir.dt.float32
F32R = mybir.dt.float32r
ACT = mybir.ActivationFunctionType
ALU = mybir.AluOpType
AX = mybir.AxisListType

P = 128
T = 256
D = 1024
KT = D // P
EPS = 1e-6
SLAB = 2048
SLABC = 256
RING = 3

H_GLA, DK, DV, CHUNK, RANK, TAU = 4, 128, 256, 64, 16, 16.0
NCH = T // CHUNK
H_MOBA, DH = 8, 64
BUCKETS, MAX_DIST = 32, 128
NEG = -1e30
D_FF = 2816
NJ = D_FF // SLABC
FT = D_FF // P
TAPS = 3
CONV_TAPS = 31
PADC = (CONV_TAPS - 1) // 2
H2, HKV, WINDOW, GRID_W, ROPE_BASE = 16, 4, 128, 64, 10000.0
GLA_W, V_W, MOBA_W = H_GLA * DK, H_GLA * DV, H_MOBA * DH


def columns():
    at, n = {}, 0
    for name, k in [
        ("norm_mix", KT), ("gla_out_norm", KT), ("norm_ffn", KT), ("norm_final", KT),
        ("ffn_w0", TAPS * 2 * FT), ("ffn_w1", TAPS * 2 * FT), ("ffn_w2", TAPS * 2 * FT),
        ("ffn_b0", 2 * FT), ("ffn_b1", 2 * FT), ("ffn_b2", 2 * FT),
        ("norm1_0", KT), ("norm1_1", KT), ("norm2_0", KT), ("norm2_1", KT), ("final_g", KT),
        ("pw1_b", 2 * KT), ("dw_w", CONV_TAPS * KT), ("dw_b", KT), ("ln_g", KT), ("ln_b", KT), ("pw2_b", KT),
        ("ada_b0", 48), ("ada_b1", 48), ("cond", 2 * KT), ("sink", H2),
    ]:
        at[name] = (n, k)
        n += k
    return at, n


def stored():
    at, n = {}, 0
    for name, k in [("mix", 27), ("moba", 2), ("gla", 4), ("out", 4), ("ffn0", 3 * NJ), ("ada0", 24), ("ada1", 24),
                    ("pw1", 8), ("pw2", 4), ("ffn1", 3 * NJ), ("qkv", 6), ("wo", 4), ("ffn2", 3 * NJ)]:
        at[name] = (n, k)
        n += k
    return at, n


class Slab:

    def __init__(self, c, n=0, j=0):
        self.c, self.n, self.j = c, n, j

    def __add__(self, k):
        return Slab(self.c + k, self.n, self.j)

    @property
    def slot(self):
        return self.c % RING

    def number(self):
        return self.c + 3 * self.n * self.j

    def landings(self):
        return 16 * (self.c // RING + 1) + 16 * self.n * self.j


class Tally:

    def __init__(self, sem):
        self.sem, self.n, self.j, self.per, self.n0 = sem, 0, None, 0, 0

    def mark(self, ins):
        ins.then_inc(self.sem, 1)
        self.n += 1
        return self.value()

    def value(self):
        return self.n if self.j is None else self.n + self.per * self.j

    def enter(self, j, per):
        self.j, self.per, self.n0 = j, per, self.n

    def leave(self, times):
        assert self.n - self.n0 == self.per, (self.n, self.n0, self.per)
        self.n, self.j = self.n0 + self.per * times, None


def build(nc, io, PLAN):
    COL, NCOL = columns()
    STORE, _ = stored()
    ctx = ExitStack()
    with ctx:
        def sb(name, shape, dt=F32):
            return ctx.enter_context(nc.sbuf_tensor(name, shape, dt))

        def sem(name):
            return ctx.enter_context(nc.semaphore(name))

        BASE, total = {}, 0
        for name, use in PLAN:
            BASE[use] = total
            total += STORE[name][1]
        TOTAL = total

        ps = ctx.enter_context(nc.psum_tensor("ps", [P, 8, 512], F32))
        raw = sb("raw", [P, RING, SLAB])
        whi = sb("whi", [P, RING, SLAB], F32R)
        wlo = sb("wlo", [P, RING, SLAB], F32R)
        xlat = sb("xlat", [P, KT, T])
        h_hi = sb("h_hi", [P, KT, T], F32R)
        h_lo = sb("h_lo", [P, KT, T], F32R)
        g_hi = sb("g_hi", [P, KT, T], F32R)
        g_lo = sb("g_lo", [P, KT, T], F32R)
        m_hi = sb("m_hi", [P, 2, 2, T], F32R)
        m_lo = sb("m_lo", [P, 2, 2, T], F32R)
        cva = sb("cva", [P, 2, 2, T])
        cvb = sb("cvb", [P, 2, 2, T])
        bufA = sb("bufA", [P, SLAB])
        bufB = sb("bufB", [P, SLAB])
        gates = sb("gates", [P, 2 * KT, T])
        sra = sb("sra", [P, KT, T])
        mqk = sb("mqk", [P, 2, 4, T])
        mv = sb("mv", [P, 2, MOBA_W])
        state = sb("state", [P, 2, H_GLA, DV])
        brev = sb("brev", [P, H_MOBA, T])
        cols = sb("cols", [P, NCOL])
        ones = sb("ones", [P, P])
        onesv = sb("onesv", [P, P])
        consts = sb("consts", [P, 3, P])
        rstd = sb("rstd", [P, 2, T])
        tiny = sb("tiny", [P, 64])
        mod = sb("mod", [P, 2, 6 * KT, 2])
        amod = sb("amod", [P, 7, KT])
        sel = sb("sel", [4, 2])
        relb = sb("relb", [BUCKETS + 1, H_MOBA])
        epsc = sb("epsc", [P, 1])

        qa, ka = gates[:, 0:4, :], gates[:, 4:8, :]
        va = gates[:, 8:16, :].rearrange("p a t -> p (a t)").rearrange("p (s n) -> p s n", s=2)
        wlr, alr = mv[0:RANK + 1, 0, :], mv[0:RANK + 1, 1, 0:T]
        xctx = brev
        g_flat = gates[:, :, :].rearrange("p a t -> p (a t)")
        VP = T + 2 * PADC
        vpad = g_flat[:, 0:KT * VP].rearrange("p (t n) -> p t n", t=KT)
        late = KT * VP
        rope_cs = g_flat[:, late:late + 2 * T].rearrange("p (a t) -> p a t", a=2)
        rot = g_flat[:, late + 2 * T:late + 2 * T + P]
        wmask = g_flat[:, late + 2 * T + P:late + 2 * T + 3 * P].rearrange("p (a k) -> p a k", a=2)
        modrow = mv[0:4, :, :].rearrange("p a n -> p (a n)")[:, 0:RING * SLABC].rearrange("p (k n) -> p k n", k=RING)
        cond = g_hi[:, :, 0:P]
        q_raw, q_rot = sra, mqk[:, :, :, :].rearrange("p a b t -> p (a b) t")
        k_raw = mv[:, 0, :].rearrange("p (a t) -> p a t", a=2)
        k_all = state[:, 0, :, :].rearrange("p h v -> p (h v)").rearrange("p (a n) -> p a n", a=2)
        v_all = state[:, 1, :, :]
        eye, rev, cum = (consts[:, i, :] for i in range(3))

        def col(name, i=0):
            c = COL[name][0]
            return cols[:, c + i:c + i + 1]

        s_cols, s_consts, s_small, s_x = sem("cols_landed"), sem("consts_landed"), sem("small_landed"), sem("x_landed")
        s_memset, s_relb = sem("memsets_done"), sem("later_keys_set")
        landed = [sem(f"slab_landed{i}") for i in range(RING)]
        hi_done, lo_done, slab_done = sem("slab_hi_done"), sem("slab_lo_done"), sem("slab_used")
        act_order, dve_order, pool_order = sem("act_order"), sem("dve_order"), sem("pool_order")
        sq_done, ms_done, std_done, y_done = sem("squares_done"), sem("means_done"), sem("std_done"), sem("normed")
        xhi_done, xlo_done = sem("act_hi_done"), sem("act_lo_done")
        mix_drained = sem("mix_drained")
        z_done, la_done, b_done, blast = sem("z_done"), sem("la_done"), sem("b_done"), sem("blast_done")
        exps_done, dec_done = sem("exps_done"), sem("decayed_done")
        attn_done, attn_sb, attn_masked = sem("attn_done"), sem("attn_copied"), sem("attn_masked")
        kteT_done, kteT_sb = sem("kteT_done"), sem("kteT_copied")
        kv_done, state_done = sem("kv_done"), sem("state_done")
        o_done, o_sq, o_sb, oms_done, ostd_done = sem("o_done"), sem("o_squared"), sem("o_copied"), sem("o_means_done"), sem("o_std_done")
        oa_done, oahi_done, oalo_done = sem("oa_done"), sem("oa_hi_done"), sem("oa_lo_done")
        tab_done, tab_sb, tab_out, brev_in = sem("bias_row_done"), sem("bias_row_copied"), sem("bias_row_stored"), sem("bias_landed")
        sc_done, sub_done, e_done, p_done = sem("scores_done"), sem("scores_less_max"), sem("exp_done"), sem("probs_done")
        pt_done, pt_sb, ob_done, obhi_done, oblo_done = sem("probsT_done"), sem("probsT_copied"), sem("ob_done"), sem("ob_hi_done"), sem("ob_lo_done")
        br_drained, mixed_done, mxhi_done, mxlo_done = sem("branch_drained"), sem("mixed_done"), sem("mixed_hi_done"), sem("mixed_lo_done")
        x_ready = sem("residual_ready")
        tap0, conv_out, silu_done, mid_f, mid_hi, mid_lo = sem("tap0_done"), sem("conv_done"), sem("silu_done"), sem("mid_done"), sem("mid_hi_done"), sem("mid_lo_done")
        s_ctx, s_late, s_sel = sem("context_landed"), sem("tables_landed"), sem("sel_landed")
        cond_f, cond_zero, cond_hi, cond_lo = sem("cond_done"), sem("cond_cleared"), sem("cond_hi_done"), sem("cond_lo_done")
        row_done, modT_done, mod_done, amod_done = sem("mod_rows_done"), sem("mod_turned"), sem("mod_done"), sem("amod_done")
        sg_done, v_done, pads_done, dw_done = sem("sigmoid_done"), sem("glu_done"), sem("pads_cleared"), sem("dwconv_done")
        mu_done, cen_done, lsq_done, var_done = sem("ln_mean_done"), sem("ln_centred"), sem("ln_squared"), sem("ln_var_done")
        lstd_done, lnorm_done, act_done = sem("ln_std_done"), sem("ln_normed"), sem("ln_silu_done")
        chi_done, clo_done = sem("conv_act_hi_done"), sem("conv_act_lo_done")
        kv_sb, krot_done, k_ready = sem("kv_copied"), sem("k_turned"), sem("k_roped")
        q_sb, qrot_done, q_ready = sem("q_copied"), sem("q_turned"), sem("q_roped")
        ws_done, wmax_done, we_done, wp_done = sem("window_scores"), sem("window_max"), sem("window_exp"), sem("window_probs")
        wt_done, wt_sb, wo_done, wohi_done, wolo_done = (sem("window_probsT"), sem("window_probsT_copied"), sem("window_out"),
                                                        sem("window_out_hi"), sem("window_out_lo"))
        out_ready, out_stored = sem("out_ready"), sem("out_stored")

        MODULATED = [(0, 1, 1, "norm1_0"), (0, 4, 1, "norm2_0"), (0, 1, 0, "norm1_0"), (0, 4, 0, "norm2_0"),
                     (1, 1, 1, "norm1_1"), (1, 1, 0, "norm1_1"), (1, 4, 0, "norm2_1")]

        def flat(a):
            names = "abc"[:len(a.shape) - 1]
            return a.rearrange(f"p {' '.join(names)} -> p ({' '.join(names)})")

        def place(h, r):
            return h % 2 * 4 + h // 2 if r == 0 else h % 2 * 2 + h % 4 // 2

        def pt_of(r):
            return [state[:, 1, :, :], cva[:, :, :, :], cvb[:, :, :, :]][r]

        def down_slab(b0, j):
            return b0 + 3 * j + 4

        def ffn_v(f):
            return (0, 1, 1, 2)[f]

        block = ctx.enter_context(nc.Block())

        def turned(act, n):
            b = n % 2
            act.wait_ge(wt_done, n + 1)
            if n >= 2:
                act.wait_ge(wo_done, n - 1)
            act.activation(bufB[:, 1024 * b:1024 * b + 1024], ps[:, 4:6, :], ACT.Copy).then_inc(wt_sb, 1)
            if n % 2:
                act.wait_ge(wo_done, n + 1)
                i = n // 2
                act.activation(g_hi[:, i, :], ps[:, 6 + i % 2, 0:T], ACT.Copy).then_inc(wohi_done, 1)

        def ffn_act(act, hi, order, f, use):
            b0 = BASE[use]
            centre = 2 if f == 0 else 1

            def tap(half, j, par, jj):
                buf = (cva, cvb)[half]
                for m in range(2):
                    t = 2 * j + m + half * FT
                    c = COL[f"ffn_w{ffn_v(f)}"][0] + centre * 2 * FT
                    b = COL[f"ffn_b{ffn_v(f)}"][0]
                    ins = act.activation(buf[:, par, m, :], ps[:, 2 * par + half, m * T:m * T + T], ACT.Identity,
                                         scale=cols[:, bass.ds(c + t, 1)], bias=cols[:, bass.ds(b + t, 1)])
                ins.then_inc(tap0, 1)

            def up(g, j, par, first, jj):
                hi(g + RING)
                act.wait_ge(slab_done, g.number() + 1)
                if not first:
                    act.wait_ge(mid_f, f * NJ + j - 1)
                tap(0, j, par, jj)
                hi(g + (RING + 1))
                act.wait_ge(slab_done, g.number() + 2)
                if not first:
                    act.wait_ge(mid_lo, f * NJ + j - 1)
                tap(1, j, par, jj)
                act.wait_ge(conv_out, f * 2 * NJ + 2 * j + 1)
                act.activation(cva[:, par, :, :], cva[:, par, :, :], ACT.Silu).then_inc(silu_done, 1)

            def split(j, par, first):
                act.wait_ge(mid_f, f * NJ + j + 1)
                if not first:
                    act.wait_ge(slab_done, down_slab(b0, j - 2) + 1)
                act.activation(m_hi[:, par, :, :], cvb[:, par, :, :], ACT.Copy).then_inc(mid_hi, 1)

            up(Slab(b0), 0, 0, True, 0)
            split(0, 0, True)
            up(Slab(b0 + 2), 1, 1, True, 0)
            hi(Slab(b0 + 4 + RING))
            split(1, 1, True)
            with act.Fori(0, 4) as jj:
                for u in range(2):
                    g = Slab(b0 + 5 + 3 * u, 2, jj)
                    up(g, 2 * jj + 2 + u, u, False, jj)
                    hi(g + (2 + RING))
                    split(2 * jj + 2 + u, u, False)
            g = Slab(b0 + 29)
            up(g, 10, 0, False, 0)
            hi(g + (2 + RING))
            split(10, 0, False)
            hi(g + (3 + RING))

        def ffn_dve(dve, lo, order, f, use):
            b0 = BASE[use]
            shifted = [(0, 2, -2), (1, 1, -1)] if f == 0 else [(0, 1, -1), (2, 0, 1)]

            def taps(half, j, par):
                buf = (cva, cvb)[half]
                c0 = COL[f"ffn_w{ffn_v(f)}"][0]
                dve.wait_ge(tap0, f * 2 * NJ + 2 * j + half + 1)
                for i, (k, first, shift) in enumerate(shifted):
                    n = T - abs(shift)
                    src = first + shift
                    for m in range(2):
                        w = cols[:, bass.ds(c0 + k * 2 * FT + half * FT + m + 2 * j, 1)]
                        out = buf[:, par, m, first:first + n]
                        ins = dve.scalar_tensor_tensor(out, ps[:, 2 * par + half, m * T + src:m * T + src + n], w, out,
                                                       ALU.mult, ALU.add)
                        if i == 0:
                            order.mark(ins)
                    if i == 0:
                        dve.wait_ge(dve_order, order.value())
                ins.then_inc(conv_out, 1)

            def up(g, j, par):
                lo(g + RING)
                taps(0, j, par)
                lo(g + (RING + 1))
                taps(1, j, par)
                dve.wait_ge(silu_done, f * NJ + j + 1)
                dve.wait_ge(conv_out, f * 2 * NJ + 2 * j + 2)
                dve.tensor_tensor(cvb[:, par, :, :], cva[:, par, :, :], cvb[:, par, :, :], ALU.mult).then_inc(mid_f, 1)

            def split(j, par):
                dve.wait_ge(mid_hi, f * NJ + j + 1)
                dve.tensor_tensor(m_lo[:, par, :, :], cvb[:, par, :, :], m_hi[:, par, :, :].bitcast(F32), ALU.subtract)\
                   .then_inc(mid_lo, 1)

            up(Slab(b0), 0, 0)
            split(0, 0)
            up(Slab(b0 + 2), 1, 1)
            lo(Slab(b0 + 4 + RING))
            split(1, 1)
            with dve.Fori(0, 4) as jj:
                order.enter(jj, 8)
                for u in range(2):
                    g = Slab(b0 + 5 + 3 * u, 2, jj)
                    up(g, 2 * jj + 2 + u, u)
                    lo(g + (2 + RING))
                    split(2 * jj + 2 + u, u)
                order.leave(4)
            g = Slab(b0 + 29)
            up(g, 10, 0)
            lo(g + (2 + RING))
            split(10, 0)
            lo(g + (3 + RING))

        def ffn_pe(pe, features, mm3, f, use):
            b0 = BASE[use]
            H = (h_hi, h_lo)

            def up(g, j, par, first):
                for half in range(2):
                    if not first:
                        pe.wait_ge(conv_out, f * 2 * NJ + 2 * j + half - 3)
                    features(g + half, 2 * par + half, H)

            def down(g, j, par, first=False):
                pe.wait_ge(lo_done, g.number() + 1)
                pe.wait_ge(mid_lo, f * NJ + j + 1)
                w = [a[:, g.slot, :].rearrange("p (k n) -> p k n", k=2) for a in (whi, wlo)]
                for m in range(KT):
                    for k in range(2):
                        ins = mm3(ps[:, 4 + m // 2, (m % 2) * T:(m % 2) * T + T], [a[:, k, m * P:m * P + P] for a in w],
                                  [m_hi[:, par, k, :], m_lo[:, par, k, :]], start=(first and k == 0 and m % 2 == 0))
                ins.then_inc(slab_done, 1)

            up(Slab(b0), 0, 0, True)
            up(Slab(b0 + 2), 1, 1, True)
            down(Slab(b0 + 4), 0, 0, True)
            with pe.Fori(0, 4) as jj:
                for u in range(2):
                    g = Slab(b0 + 5 + 3 * u, 2, jj)
                    up(g, 2 * jj + 2 + u, u, False)
                    down(g + 2, 2 * jj + 1 + u, 1 - u)
            up(Slab(b0 + 29), 10, 0, False)
            down(Slab(b0 + 31), 9, 1)
            down(Slab(b0 + 32), 10, 0)
        @block.sync
        def _(sp):
            sp.dma_start(xlat[:, :, :], io["xT"]).then_inc(s_x, 16)

            def load(name, first, k, g):
                if g.c >= RING:
                    sp.wait_ge(lo_done, (g + -RING).number() + 1)
                src = STORE[name][0] + first + k
                sp.dma_start(raw[:, g.slot, :], io["w"][bass.ds(src, 1)]).then_inc(landed[g.slot], 16)

            for name, use in PLAN:
                count = STORE[name][1]
                head = min(count, RING) if BASE[use] == 0 else 0
                for k in range(head):
                    load(name, 0, k, Slab(BASE[use] + k))
                if use == PLAN[0][1]:
                    sp.dma_start(cols[:, :], io["cols"]).then_inc(s_cols, 16)
                    sp.dma_start(consts[:, :, :], io["consts"]).then_inc(s_consts, 16)
                    sp.dma_start(relb[0:BUCKETS, :], io["rel_bias"]).then_inc(s_small, 16)
                    sp.dma_start(sra[0:BUCKETS + 1, 0:2, :], io["onehot"]).then_inc(s_small, 16)
                    sp.dma_start(sel[:, :], io["sel"]).then_inc(s_sel, 16)
                    sp.dma_start(wlr[0:RANK, :], io["w_lr_up"]).then_inc(s_small, 16)
                    sp.dma_start(wlr[RANK:RANK + 1, :], io["b_forget"]).then_inc(s_small, 16)
                times = (count - head) // RING
                if times:
                    with sp.Fori(0, times) as j:
                        for k in range(RING):
                            load(name, head + k, 3 * j, Slab(BASE[use] + head + k, 1, j))
                for k in range(head + RING * times, count):
                    load(name, 0, k, Slab(BASE[use] + k))
                if use == "ffn0":
                    sp.wait_ge(sc_done, 3)
                    sp.dma_start(xctx[:, :, :], io["ctxT"]).then_inc(s_ctx, 16)
                    sp.wait_ge(br_drained, 6)
                    sp.dma_start(g_flat[:, late:late + 2 * T + 3 * P], io["tables"]).then_inc(s_late, 16)
            sp.wait_ge(out_ready, 1)
            sp.dma_start(io["out"], xlat[:, :, :]).then_inc(out_stored, 16)
            sp.wait_ge(out_stored, 16)

        @block.gpsimd
        def _(pool):
            pool.memset(ones[:, :], 1.0 / D).then_inc(s_memset, 1)
            pool.memset(onesv[:, :], 1.0 / DV).then_inc(s_memset, 1)
            pool.memset(epsc[:, :], EPS).then_inc(s_memset, 1)
            pool.memset(alr, 1.0).then_inc(s_memset, 1)
            pool.wait_ge(tab_sb, 1)
            pool.dma_start(io["scratch"], state[0:H_MOBA, 0, 0:2, :].rearrange("p a t -> p (a t)")).then_inc(tab_out, 16)
            pool.wait_ge(tab_out, 16)
            pool.dma_start(brev[:, :, :], bass.AP(io["scratch"].tensor, 0, [[1, P], [512, H_MOBA], [1, T]]))\
                .then_inc(brev_in, 16)
            attn = bufA[:, 0:1024].rearrange("p (a i) -> p a i", i=P)
            pool.wait_ge(attn_sb, 1)
            pool.affine_select(out=attn, in_=attn, compare_op=ALU.is_ge, fill=0.0, base=0,
                               pattern=[[0, 8], [1, P]], channel_multiplier=-1).then_inc(pool_order, 1)
            pool.wait_ge(pool_order, 1)
            pool.memset(attn[0:CHUNK, :, CHUNK:P], 0.0).then_inc(attn_masked, 1)

        @block.scalar
        def _(act):
            order = Tally(act_order)

            def hi(g):
                if isinstance(g.j, int) and g.c >= TOTAL:
                    return
                act.wait_ge(landed[g.slot], g.landings())
                if g.c >= RING:
                    act.wait_ge(slab_done, (g + -RING).number() + 1)
                act.activation(whi[:, g.slot, :], raw[:, g.slot, :], ACT.Copy).then_inc(hi_done, 1)

            def norm_squares(n, x):
                for i in range(2):
                    act.activation(bufB[:, 1024 * i:1024 * i + 1024], x[:, 4 * i:4 * i + 4, :], ACT.Square)\
                       .then_inc(sq_done, 1)
                act.wait_ge(ms_done, n + 1)
                act.activation(rstd[:, 0, :], ps[:, 4, 0:T], ACT.Sqrt, bias=epsc[:, :]).then_inc(std_done, 1)

            def split_hi(n, y, out=h_hi, shift=None):
                for t in range(0, KT, 2):
                    act.wait_ge(y_done, KT * n + t + 2)
                    if shift is None:
                        ins = act.activation(out[:, t:t + 2, :], y[:, t * T:t * T + 2 * T], ACT.Copy)
                    else:
                        for m in (t, t + 1):
                            ins = act.activation(out[:, m, :], y[:, m * T:m * T + T], ACT.Identity, bias=shift(m))
                    ins.then_inc(xhi_done, 1)

            act.wait_ge(s_memset, 4)
            act.wait_ge(s_cols, 16)
            act.wait_ge(s_x, 16)
            norm_squares(0, xlat)
            for k in range(RING):
                hi(Slab(k))
            split_hi(0, bufA)

            def drain(g, out, func=ACT.Copy, scale=1.0, rows=P):
                bank = ps[0:rows, g % 4, 0:out.shape[-1] if len(out.shape) == 2 else 512]
                act.activation(out, bank, func, scale=scale).then_inc(mix_drained, 1)

            b0 = BASE["mix"]
            for g in range(27):
                hi(Slab(b0 + g + RING))
                act.wait_ge(slab_done, b0 + g + 1)
                if g == 0:
                    act.wait_ge(s_memset, 4)
                    drain(g, alr[0:RANK, :], rows=RANK)
                elif g < 3:
                    drain(g, ka[:, 2 * (g - 1):2 * g, :])
                elif g < 5:
                    drain(g, qa[:, 2 * (g - 3):2 * (g - 3) + 2, :], scale=DK ** -0.5)
                elif g < 9:
                    drain(g, va[:, :, (g - 5) * SLABC:(g - 4) * SLABC])
                elif g < 11:
                    drain(g, mqk[:, 1, 2 * (g - 9):2 * (g - 9) + 2, :])
                elif g < 13:
                    drain(g, mqk[:, 0, 2 * (g - 11):2 * (g - 11) + 2, :], scale=DH ** -0.5)
                elif g < 15:
                    drain(g, mv[:, :, (g - 13) * SLABC:(g - 12) * SLABC])
                elif g < 19:
                    if g == 15:
                        act.wait_ge(tab_done, 1)
                    drain(g, sra[:, 2 * (g - 15):2 * (g - 15) + 2, :], ACT.Silu)
                else:
                    if g == 19:
                        act.wait_ge(o_done, 1)
                    drain(g, gates[:, 2 * (g - 19):2 * (g - 19) + 2, :], ACT.Sigmoid)
                if g == 2:
                    act.wait_ge(z_done, 1)
                    lz = bufB[:, 0:1024]
                    order.mark(act.activation(lz, ps[:, 4:6, :], ACT.Abs))
                    act.wait_ge(act_order, order.value())
                    order.mark(act.activation(lz, lz, ACT.Exp, scale=-1.0))
                    act.wait_ge(act_order, order.value())
                    act.activation(lz, lz, ACT.Ln, bias=1.0).then_inc(la_done, 1)
                if g == 4:
                    act.wait_ge(blast, 2)
                    act.activation(bufA[:, 0:1024], ps[:, 6:8, :], ACT.Exp).then_inc(exps_done, 1)
                    act.activation(bufA[:, 1024:2048], ps[:, 6:8, :], ACT.Exp, scale=-1.0).then_inc(exps_done, 1)
                    act.activation(tiny[:, 16:32], tiny[:, 0:16], ACT.Exp).then_inc(exps_done, 1)
                    act.activation(bufB[:, 0:1024], bufB[:, 0:1024], ACT.Exp).then_inc(exps_done, 1)
                if g == 8:
                    act.wait_ge(attn_done, 1)
                    act.activation(bufA[:, 0:1024], ps[:, 4:6, :], ACT.Copy).then_inc(attn_sb, 1)
                    act.wait_ge(kteT_done, 1)
                    act.activation(bufB[:, 1024:2048], ps[:, 6:8, :], ACT.Copy).then_inc(kteT_sb, 1)
                if g == 13:
                    act.wait_ge(o_done, 1)
                    act.activation(bufB[:, :], ps[:, 4:8, :], ACT.Square).then_inc(o_sq, 1)
                if g == 14:
                    act.wait_ge(oms_done, 1)
                    act.activation(bufB[:, 0:1024], ps[:, 4:6, :], ACT.Sqrt, bias=epsc[:, :]).then_inc(ostd_done, 1)
                if g == 19:
                    for i in range(2):
                        act.wait_ge(oa_done, KT)
                        act.activation(g_hi[:, 4 * i:4 * i + 4, :], bufA[:, 1024 * i:1024 * i + 1024], ACT.Copy)\
                           .then_inc(oahi_done, 1)
                if g in (17, 20, 23):
                    r = (g - 17) // 3
                    act.wait_ge(sub_done, r + 1)
                    act.activation(state[:, 0, :, :], state[:, 0, :, :], ACT.Exp).then_inc(e_done, 1)
                if g in (18, 21, 24):
                    r = (g - 18) // 3
                    act.wait_ge(pt_done, r + 1)
                    act.activation(pt_of(r), ps[:, 6:8, :], ACT.Copy).then_inc(pt_sb, 1)
            act.wait_ge(ob_done, 1)
            act.activation(m_hi[:, :, :, :], ps[:, 4:6, :], ACT.Copy).then_inc(obhi_done, 1)

            for i in range(10):
                hi(Slab(BASE["moba"] + i + RING))
                act.wait_ge(slab_done, BASE["moba"] + i + 1)
                if 2 <= i < 6:
                    act.wait_ge(mixed_done, i - 1)
                    act.activation(h_hi[:, 2 * (i - 2):2 * (i - 2) + 2, :], bufA[:, 512 * (i - 2):512 * (i - 1)], ACT.Copy)\
                       .then_inc(mxhi_done, 1)
            act.wait_ge(x_ready, 4)
            norm_squares(1, xlat)
            split_hi(1, bufA)
            ffn_act(act, hi, order, 0, "ffn0")
            act.wait_ge(x_ready, 8)
            norm_squares(2, xlat)

            act.activation(tiny[:, 0:16], cols[:, COL["cond"][0]:COL["cond"][0] + 2 * KT], ACT.Silu).then_inc(cond_f, 1)
            act.wait_ge(cond_f, 1)
            act.wait_ge(cond_zero, 1)
            for s in range(2):
                act.activation(cond[:, :, 2 * s], tiny[:, 8 * s:8 * s + 8], ACT.Copy).then_inc(cond_hi, 1)
            for layer in range(2):
                b0 = BASE[f"ada{layer}"]
                with act.Fori(0, 8) as j:
                    for k in range(RING):
                        g = Slab(b0 + k, 1, j)
                        hi(g + RING)
                        act.wait_ge(slab_done, g.number() + 1)
                        act.activation(modrow[:, k, :], ps[0:4, k, 0:SLABC], ACT.Copy).then_inc(row_done, 1)

            def conformer(q, use1, use2):
                b0 = BASE[use1]
                for j in range(4):
                    hi(Slab(b0 + 2 * j + RING))
                    hi(Slab(b0 + 2 * j + 1 + RING))
                    act.wait_ge(slab_done, b0 + 2 * j + 2)
                    if j >= 2:
                        act.wait_ge(v_done, 4 * q + j - 1)
                    for m in range(2):
                        ins = act.activation(cva[:, j % 2, m, :], ps[:, 2 * (j % 2) + 1, m * T:m * T + T], ACT.Sigmoid,
                                             bias=col("pw1_b", KT + 2 * j + m))
                    ins.then_inc(sg_done, 1)
                for i in range(2):
                    act.wait_ge(cen_done, q + 1)
                    act.activation(bufB[:, 1024 * i:1024 * i + 1024], bufA[:, 1024 * i:1024 * i + 1024], ACT.Square)\
                       .then_inc(lsq_done, 1)
                act.wait_ge(var_done, q + 1)
                act.activation(rstd[:, 0, :], ps[:, 5, 0:T], ACT.Sqrt, bias=epsc[:, :]).then_inc(lstd_done, 1)
                act.wait_ge(lnorm_done, q + 1)
                for t in range(KT):
                    act.activation(bufB[:, t * T:t * T + T], bufA[:, t * T:t * T + T], ACT.Silu,
                                   scale=col("ln_g", t), bias=col("ln_b", t)).then_inc(act_done, 1)
                for t in range(0, KT, 2):
                    act.wait_ge(act_done, KT * q + t + 2)
                    act.activation(g_hi[:, t:t + 2, :], bufB[:, t * T:t * T + 2 * T], ACT.Copy).then_inc(chi_done, 1)
                for i in range(4):
                    hi(Slab(BASE[use2] + i + RING))

            def shift_of(layer, i, s):
                return lambda t: mod[:, layer, i * KT + t, s:s + 1]

            act.wait_ge(s_ctx, 16)
            norm_squares(3, xctx)
            split_hi(3, bufA, shift=shift_of(0, 0, 1))
            conformer(0, "pw1_ctx", "pw2_ctx")
            act.wait_ge(x_ready, 12)
            norm_squares(4, xctx)
            split_hi(4, bufA, shift=shift_of(0, 3, 1))
            ffn_act(act, hi, order, 1, "ffn_ctx")
            act.wait_ge(x_ready, 16)
            norm_squares(5, xlat)
            split_hi(5, bufA, shift=shift_of(0, 0, 0))
            conformer(1, "pw1_lat", "pw2_lat")
            act.wait_ge(x_ready, 20)
            norm_squares(6, xlat)
            split_hi(6, bufA, shift=shift_of(0, 3, 0))
            ffn_act(act, hi, order, 2, "ffn_lat")
            act.wait_ge(x_ready, 24)
            norm_squares(7, xctx)
            split_hi(7, bufA, shift=shift_of(1, 0, 1))
            norm_squares(8, xlat)
            split_hi(8, bufA, out=g_hi, shift=shift_of(1, 0, 0))

            b0 = BASE["qkv"]
            for i in range(6):
                hi(Slab(b0 + i + RING))
                act.wait_ge(slab_done, b0 + i + 1)
                if i == 0:
                    act.activation(k_raw, ps[:, 0, :], ACT.Copy).then_inc(kv_sb, 1)
                    act.activation(k_all[:, :, T:2 * T], ps[:, 1, :].rearrange("p (a t) -> p a t", a=2), ACT.Copy).then_inc(kv_sb, 1)
                elif i == 1:
                    act.activation(v_all, ps[:, 2:4, :], ACT.Copy).then_inc(kv_sb, 1)
                else:
                    act.activation(q_raw[:, 2 * (i - 2):2 * (i - 2) + 2, :], ps[:, i - 2, :], ACT.Copy, scale=DH ** -0.5).then_inc(q_sb, 1)
            for n in range(H2):
                u, b = n % 2, n % 2
                pr = bufA[:, 1024 * b:1024 * b + 1024].rearrange("p (s k) -> p s k", s=2)
                act.wait_ge(wmax_done, n + 1)
                if n >= 2:
                    act.wait_ge(wt_done, n - 1)
                for s in range(2):
                    act.activation(pr[:, s, :], ps[:, 2 * b + s, :], ACT.Exp, bias=tiny[:, 8 * b + 2:8 * b + 3] if s == 0 else tiny[:, 8 * b + 3:8 * b + 4],
                                   accum_out=tiny[:, 16 + 8 * b + s:17 + 8 * b + s])
                act.activation(tiny[:, 16 + 8 * b + 2:16 + 8 * b + 4], tiny[:, 8 * b + 4:8 * b + 6], ACT.Exp).then_inc(we_done, 1)
                if n >= 1:
                    turned(act, n - 1)
            turned(act, H2 - 1)
            for i in range(4):
                hi(Slab(BASE["wo"] + i + RING))
            act.wait_ge(x_ready, 28)
            norm_squares(9, xlat)
            split_hi(9, bufA, shift=shift_of(1, 3, 0))
            ffn_act(act, hi, order, 3, "ffn2")
            act.wait_ge(x_ready, 32)
            norm_squares(10, xlat)

        @block.vector
        def _(dve):
            order = Tally(dve_order)

            def lo(g):
                if isinstance(g.j, int) and g.c >= TOTAL:
                    return
                dve.wait_ge(hi_done, g.number() + 1)
                dve.tensor_tensor(wlo[:, g.slot, :], raw[:, g.slot, :], whi[:, g.slot, :].bitcast(F32), ALU.subtract)\
                   .then_inc(lo_done, 1)

            def norm_scale(n, x, gains, y):
                dve.wait_ge(std_done, n + 1)
                order.mark(dve.reciprocal(rstd[:, 1, :], rstd[:, 0, :]))
                dve.wait_ge(dve_order, order.value())
                for t in range(KT):
                    dve.scalar_tensor_tensor(y[:, t * T:t * T + T], x[:, t, :], gains(t), rstd[:, 1, :],
                                             ALU.mult, ALU.mult).then_inc(y_done, 1)

            def split_lo(n, y, out=(h_hi, h_lo), shift=None):
                for t in range(0, KT, 2):
                    dve.wait_ge(xhi_done, KT // 2 * n + t // 2 + 1)
                    if shift is None:
                        ins = dve.tensor_tensor(out[1][:, t:t + 2, :], y[:, t * T:t * T + 2 * T],
                                                out[0][:, t:t + 2, :].bitcast(F32), ALU.subtract)
                    else:
                        for m in (t, t + 1):
                            ins = dve.scalar_tensor_tensor(out[1][:, m, :], y[:, m * T:m * T + T], shift(m),
                                                           out[0][:, m, :].bitcast(F32), ALU.add, ALU.subtract)
                    ins.then_inc(xlo_done, 1)

            dve.memset(relb[BUCKETS:BUCKETS + 1, :], NEG).then_inc(s_relb, 1)
            dve.wait_ge(tab_done, 1)
            dve.tensor_copy(state[0:H_MOBA, 0, 0:2, :], ps[0:H_MOBA, 5, :]).then_inc(tab_sb, 1)
            norm_scale(0, xlat, lambda t: col("norm_mix", t), bufA)
            for k in range(RING):
                lo(Slab(k))
            split_lo(0, bufA)

            b0 = BASE["mix"]
            E1, E2, E3 = bufA[:, 0:1024], bufA[:, 1024:2048], bufB[:, 0:1024]
            heads = lambda a: a.rearrange("p (h t) -> p h t", t=T)
            for g in range(27):
                lo(Slab(b0 + g + RING))
                if g == 2:
                    dve.wait_ge(la_done, 1)
                    dve.scalar_tensor_tensor(bufB[:, 1024:2048], ps[:, 4:6, :].rearrange("p a n -> p (a n)"), 0.0,
                                             bufB[:, 0:1024], ALU.min, ALU.subtract).then_inc(la_done, 1)
                if g == 4:
                    dve.wait_ge(b_done, 1)
                    bT = ps[:, 6:8, :].rearrange("p a (h c i) -> p (a h c) i", h=2, c=NCH)
                    dve.tensor_copy(tiny[:, 0:16], bT[:, :, CHUNK - 1]).then_inc(blast, 1)
                    dve.wait_ge(blast, 1)
                    dve.scalar_tensor_tensor(E3.rearrange("p (c i) -> p c i", i=CHUNK), bT, -1.0,
                                             tiny[:, 0:16, None].to_broadcast([P, 16, CHUNK]),
                                             ALU.mult, ALU.add).then_inc(blast, 1)
                    dve.wait_ge(exps_done, 1)
                    dve.tensor_tensor(qa, qa, heads(E1), ALU.mult).then_inc(dec_done, 1)
                    dve.wait_ge(exps_done, 2)
                    dve.tensor_tensor(heads(E2), ka, heads(E2), ALU.mult).then_inc(dec_done, 1)
                    dve.wait_ge(exps_done, 4)
                    dve.tensor_tensor(heads(E3), ka, heads(E3), ALU.mult).then_inc(dec_done, 1)
                if g == 10:
                    dve.wait_ge(tab_out, 16)
                    dve.wait_ge(kv_done, 1)
                    dve.tensor_copy(ka, ps[:, 4:6, :].rearrange("p a (h v) -> p (a h) v", v=DV)).then_inc(state_done, 1)
                    dve.wait_ge(state_done, 1)
                    for n in (1, 2):
                        if n == 2:
                            dve.wait_ge(kv_done, 2)
                        for h in range(H_GLA):
                            prev = ka[:, h, :] if n == 1 else state[:, 0, h, :]
                            bank = (6 if n == 1 else 4) + h // 2
                            if n == 2:
                                dve.wait_ge(state_done, 2 + h)
                            c = 16 + h * NCH + n
                            dve.scalar_tensor_tensor(state[:, n - 1, h, :], prev, tiny[:, c:c + 1],
                                                     ps[:, bank, (h % 2) * DV:(h % 2) * DV + DV], ALU.mult, ALU.add)\
                               .then_inc(state_done, 1)
                if g == 13:
                    dve.wait_ge(o_sq, 1)
                    dve.tensor_copy(bufA[:, :], ps[:, 4:8, :].rearrange("p a n -> p (a n)")).then_inc(o_sb, 1)
                if g == 14:
                    dve.wait_ge(ostd_done, 1)
                    order.mark(dve.reciprocal(bufB[:, 0:1024], bufB[:, 0:1024]))
                    dve.wait_ge(dve_order, order.value())
                    dve.wait_ge(o_sb, 1)
                    o = bufA[:, :].rearrange("p (h d t) -> p h d t", h=H_GLA, d=2)
                    order.mark(dve.tensor_tensor(
                        o, o, heads(bufB[:, 0:1024])[:, :, None, :].to_broadcast([P, H_GLA, 2, T]), ALU.mult))
                if g == 18:
                    dve.wait_ge(dve_order, order.value())
                    dve.wait_ge(mix_drained, 19)
                    for t in range(KT):
                        o = bufA[:, t * T:t * T + T]
                        dve.scalar_tensor_tensor(o, o, col("gla_out_norm", t), sra[:, t, :], ALU.mult, ALU.mult)\
                           .then_inc(oa_done, 1)
                if g == 19:
                    for i in range(2):
                        dve.wait_ge(oahi_done, i + 1)
                        dve.tensor_tensor(g_lo[:, 4 * i:4 * i + 4, :], bufA[:, 1024 * i:1024 * i + 1024],
                                          g_hi[:, 4 * i:4 * i + 4, :].bitcast(F32), ALU.subtract).then_inc(oalo_done, 1)
                if g in (16, 19, 22):
                    r = (g - 16) // 3
                    n = 8 if r == 0 else 4
                    sc = ps[:, 4:6, :].rearrange("p a (h k) -> p (a h) k", h=n // 2)
                    pr = state[:, 0, :, :].rearrange("p h v -> p (h v)").rearrange("p (h k) -> p h k", h=n)
                    dve.wait_ge(sc_done, r + 1)
                    order.mark(dve.tensor_reduce(tiny[:, 32:32 + n], sc, AX.X, ALU.max))
                    dve.wait_ge(dve_order, order.value())
                    if r:
                        dve.wait_ge(pt_done, r)
                    dve.tensor_tensor(pr, sc, tiny[:, 32:32 + n, None].to_broadcast([P, n, 1024 // n]), ALU.subtract)\
                       .then_inc(sub_done, 1)
                if g in (17, 20, 23):
                    dve.wait_ge(e_done, r + 1)
                    order.mark(dve.tensor_reduce(tiny[:, 40:40 + n], pr, AX.X, ALU.add))
                    dve.wait_ge(dve_order, order.value())
                    order.mark(dve.reciprocal(tiny[:, 48:48 + n], tiny[:, 40:40 + n]))
                    dve.wait_ge(dve_order, order.value())
                    dve.tensor_tensor(pr, pr, tiny[:, 48:48 + n, None].to_broadcast([P, n, 1024 // n]), ALU.mult)\
                       .then_inc(p_done, 1)
            dve.wait_ge(obhi_done, 1)
            dve.tensor_tensor(m_lo[:, :, :, :].rearrange("p a b t -> p (a b t)"), ps[:, 4:6, :].rearrange("p a n -> p (a n)"),
                              m_hi[:, :, :, :].bitcast(F32).rearrange("p a b t -> p (a b t)"), ALU.subtract)\
               .then_inc(oblo_done, 1)

            for i in range(10):
                lo(Slab(BASE["moba"] + i + RING))
                dve.wait_ge(slab_done, BASE["moba"] + i + 1)
                if i < 2:
                    dve.wait_ge(mix_drained, 27)
                    dve.tensor_tensor(bufB[:, 1024 * i:1024 * i + 1024], ps[:, 2 * i:2 * i + 2, :].rearrange("p a n -> p (a n)"),
                                      gates[:, KT + 4 * i:KT + 4 * i + 4, :].rearrange("p a t -> p (a t)"), ALU.mult)\
                       .then_inc(br_drained, 1)
                elif i < 6:
                    k = i - 2
                    mix = bufA[:, 512 * k:512 * k + 512]
                    dve.tensor_tensor(mix, ps[:, k, :], gates[:, 2 * k:2 * k + 2, :].rearrange("p a t -> p (a t)"), ALU.mult)\
                       .then_inc(br_drained, 1)
                    dve.wait_ge(br_drained, i + 1)
                    dve.tensor_tensor(mix, mix, bufB[:, 512 * k:512 * k + 512], ALU.add).then_inc(mixed_done, 1)
                    dve.wait_ge(mxhi_done, k + 1)
                    dve.tensor_tensor(h_lo[:, 2 * k:2 * k + 2, :].rearrange("p a t -> p (a t)"), mix,
                                      h_hi[:, 2 * k:2 * k + 2, :].bitcast(F32).rearrange("p a t -> p (a t)"), ALU.subtract)\
                       .then_inc(mxlo_done, 1)
                else:
                    k = i - 6
                    x = xlat[:, 2 * k:2 * k + 2, :].rearrange("p a t -> p (a t)")
                    dve.tensor_tensor(x, ps[:, k, :], x, ALU.add).then_inc(x_ready, 1)
            norm_scale(1, xlat, lambda t: col("norm_ffn", t), bufA)
            split_lo(1, bufA)
            ffn_dve(dve, lo, order, 0, "ffn0")
            dve.wait_ge(slab_done, BASE["ffn0"] + 3 * NJ)
            for q in range(4):
                x = xlat[:, 2 * q:2 * q + 2, :].rearrange("p a t -> p (a t)")
                dve.tensor_tensor(x, ps[:, 4 + q, :], x, ALU.add).then_inc(x_ready, 1)
            norm_scale(2, xlat, lambda t: col("norm_final", t), xlat[:, :, :].rearrange("p a t -> p (a t)"))

            dve.memset(cond.bitcast(F32), 0.0).then_inc(cond_zero, 1)
            dve.wait_ge(cond_hi, 2)
            for s in range(2):
                dve.tensor_tensor(cond[:, :, 2 * s + 1], tiny[:, 8 * s:8 * s + 8], cond[:, :, 2 * s].bitcast(F32), ALU.subtract)\
                   .then_inc(cond_lo, 1)
            for layer in range(2):
                b0, c0 = BASE[f"ada{layer}"], COL[f"ada_b{layer}"][0]
                with dve.Fori(0, 8) as j:
                    for k in range(RING):
                        lo(Slab(b0 + k + RING, 1, j))
                    dve.wait_ge(modT_done, 8 * layer + j + 1)
                    dve.tensor_tensor(mod[:, layer, bass.ds(6 * j, 6), :], ps[:, 3, 0:12].rearrange("p (a s) -> p a s", s=2),
                                      cols[:, bass.ds(6 * j + c0, 6), None].to_broadcast([P, 6, 2]), ALU.add).then_inc(mod_done, 1)
            dve.wait_ge(mod_done, 16)
            for i, (layer, which, s, gain) in enumerate(MODULATED):
                dve.scalar_tensor_tensor(amod[:, i, :], mod[:, layer, which * KT:which * KT + KT, s], 1.0,
                                         cols[:, COL[gain][0]:COL[gain][0] + KT], ALU.add, ALU.mult).then_inc(amod_done, 1)
            dve.wait_ge(amod_done, len(MODULATED))
            dve.memset(vpad[:, :, 0:PADC], 0.0).then_inc(pads_done, 1)
            dve.memset(vpad[:, :, PADC + T:VP], 0.0).then_inc(pads_done, 1)
            dve.wait_ge(pads_done, 2)

            def gain_of(i):
                return lambda t: amod[:, i, t:t + 1]

            def shift_of(layer, i, s):
                return lambda t: mod[:, layer, i * KT + t, s:s + 1]

            def gated_residual(x, gate):
                for t in range(KT):
                    ins = dve.scalar_tensor_tensor(x[:, t, :], ps[:, 4 + t // 2, (t % 2) * T:(t % 2) * T + T], gate(t), x[:, t, :],
                                                   ALU.mult, ALU.add)
                    if t % 2:
                        ins.then_inc(x_ready, 1)

            def conformer(q, use1, use2, x, gate):
                b0 = BASE[use1]
                for j in range(4):
                    lo(Slab(b0 + 2 * j + RING))
                    lo(Slab(b0 + 2 * j + 1 + RING))
                    dve.wait_ge(sg_done, 4 * q + j + 1)
                    for m in range(2):
                        ins = dve.scalar_tensor_tensor(vpad[:, 2 * j + m, PADC:PADC + T], ps[:, 2 * (j % 2), m * T:m * T + T],
                                                       col("pw1_b", 2 * j + m), cva[:, j % 2, m, :], ALU.add, ALU.mult)
                    ins.then_inc(v_done, 1)
                dve.wait_ge(v_done, 4 * q + 4)
                acc = bufA[:, :].rearrange("p (t n) -> p t n", t=KT)
                n0 = order.value()
                for t in range(KT):
                    order.mark(dve.tensor_scalar(acc[:, t, :], vpad[:, t, 0:T], col("dw_w", t), col("dw_b", t), ALU.mult, ALU.add))
                with dve.Fori(0, CONV_TAPS - 1) as k:
                    order.enter(k, KT)
                    for t in range(KT):
                        dve.wait_ge(dve_order, n0 + KT * k + t + 1)
                        w = cols[:, bass.ds(KT * k + (COL["dw_w"][0] + KT + t), 1)]
                        order.mark(dve.scalar_tensor_tensor(acc[:, t, :], vpad[:, t, bass.ds(k + 1, T)], w, acc[:, t, :],
                                                            ALU.mult, ALU.add))
                    order.leave(CONV_TAPS - 1)
                dve.wait_ge(dve_order, order.value())
                dve.sem_inc(dw_done, 1)
                wide = lambda a: a[:, None, :].to_broadcast([P, KT, T])
                dve.wait_ge(mu_done, q + 1)
                dve.tensor_tensor(acc, acc, wide(ps[:, 4, 0:T]), ALU.subtract).then_inc(cen_done, 1)
                dve.wait_ge(lstd_done, q + 1)
                order.mark(dve.reciprocal(rstd[:, 1, :], rstd[:, 0, :]))
                dve.wait_ge(dve_order, order.value())
                dve.tensor_tensor(acc, acc, wide(rstd[:, 1, :]), ALU.mult).then_inc(lnorm_done, 1)
                for t in range(0, KT, 2):
                    dve.wait_ge(chi_done, 4 * q + t // 2 + 1)
                    dve.tensor_tensor(g_lo[:, t:t + 2, :], bufB[:, t * T:t * T + 2 * T], g_hi[:, t:t + 2, :].bitcast(F32),
                                      ALU.subtract).then_inc(clo_done, 1)
                for i in range(4):
                    lo(Slab(BASE[use2] + i + RING))
                    dve.wait_ge(slab_done, BASE[use2] + i + 1)
                    for m in range(2):
                        t = 2 * i + m
                        order.mark(dve.tensor_scalar(bufA[:, t * T:t * T + T], ps[:, i, m * T:m * T + T], col("pw2_b", t), gate(t),
                                                     ALU.add, ALU.mult))
                    dve.wait_ge(dve_order, order.value())
                    dve.tensor_tensor(x[:, 2 * i:2 * i + 2, :], x[:, 2 * i:2 * i + 2, :], bufA[:, 512 * i:512 * i + 512], ALU.add)\
                       .then_inc(x_ready, 1)

            def ffn(f, use, x, gate):
                ffn_dve(dve, lo, order, f, use)
                dve.wait_ge(slab_done, BASE[use] + 3 * NJ)
                gated_residual(x, gate)

            norm_scale(3, xctx, gain_of(0), bufA)
            split_lo(2, bufA, shift=shift_of(0, 0, 1))
            conformer(0, "pw1_ctx", "pw2_ctx", xctx, shift_of(0, 2, 1))
            norm_scale(4, xctx, gain_of(1), bufA)
            split_lo(3, bufA, shift=shift_of(0, 3, 1))
            ffn(1, "ffn_ctx", xctx, shift_of(0, 5, 1))
            norm_scale(5, xlat, gain_of(2), bufA)
            split_lo(4, bufA, shift=shift_of(0, 0, 0))
            conformer(1, "pw1_lat", "pw2_lat", xlat, shift_of(0, 2, 0))
            norm_scale(6, xlat, gain_of(3), bufA)
            split_lo(5, bufA, shift=shift_of(0, 3, 0))
            ffn(2, "ffn_lat", xlat, shift_of(0, 5, 0))
            norm_scale(7, xctx, gain_of(4), bufA)
            split_lo(6, bufA, shift=shift_of(1, 0, 1))
            norm_scale(8, xlat, gain_of(5), bufA)
            split_lo(7, bufA, out=(g_hi, g_lo), shift=shift_of(1, 0, 0))

            b0 = BASE["qkv"]
            cos, sin = (rope_cs[:, i:i + 1, :].to_broadcast([P, 2, T]) for i in range(2))

            def rope(out, raw_, bank, done):
                order.mark(dve.tensor_tensor(out, ps[:, bank, :].rearrange("p (a t) -> p a t", a=2), sin, ALU.mult))
                order.mark(dve.tensor_tensor(raw_, raw_, cos, ALU.mult))
                dve.wait_ge(dve_order, order.value())
                dve.tensor_tensor(out, out, raw_, ALU.add).then_inc(done, 1)

            dve.wait_ge(s_late, 16)
            for i in range(6):
                lo(Slab(b0 + i + RING))
                if i == 1:
                    dve.wait_ge(krot_done, 1)
                    rope(k_all[:, :, 0:T], k_raw, 4, k_ready)
                if i >= 3:
                    dve.wait_ge(qrot_done, i - 2)
                    rope(q_rot[:, 2 * (i - 3):2 * (i - 3) + 2, :], q_raw[:, 2 * (i - 3):2 * (i - 3) + 2, :], 4 + (i - 2) % 4, q_ready)
            dve.wait_ge(qrot_done, 4)
            rope(q_rot[:, 6:8, :], q_raw[:, 6:8, :], 4, q_ready)

            def probs(n):
                b = n % 2
                c = 16 + 8 * b
                dve.wait_ge(we_done, n + 1)
                order.mark(dve.tensor_tensor(tiny[:, c + 4:c + 6], tiny[:, c:c + 2], tiny[:, c + 2:c + 4], ALU.add))
                dve.wait_ge(dve_order, order.value())
                order.mark(dve.reciprocal(tiny[:, c + 6:c + 8], tiny[:, c + 4:c + 6]))
                dve.wait_ge(dve_order, order.value())
                for s in range(2):
                    pr = bufA[:, 1024 * b + 512 * s:1024 * b + 512 * s + 512]
                    ins = dve.tensor_scalar(pr, pr, tiny[:, c + 6 + s:c + 7 + s], None, ALU.mult)
                ins.then_inc(wp_done, 1)

            def out_lo(i):
                dve.wait_ge(wohi_done, i + 1)
                dve.tensor_tensor(g_lo[:, i, :], ps[:, 6 + i % 2, 0:T], g_hi[:, i, :].bitcast(F32), ALU.subtract).then_inc(wolo_done, 1)

            for n in range(H2):
                b = n % 2
                c = 8 * b
                dve.wait_ge(ws_done, n + 1)
                if n >= 2:
                    dve.wait_ge(we_done, n - 1)
                order.mark(dve.tensor_reduce(tiny[:, c:c + 2], ps[:, 2 * b:2 * b + 2, :], AX.X, ALU.max))
                dve.wait_ge(dve_order, order.value())
                sink = col("sink", n)
                order.mark(dve.tensor_scalar(tiny[:, c + 2:c + 4], tiny[:, c:c + 2], sink, -1.0, ALU.max, ALU.mult))
                dve.wait_ge(dve_order, order.value())
                dve.tensor_scalar(tiny[:, c + 4:c + 6], tiny[:, c + 2:c + 4], sink, None, ALU.add).then_inc(wmax_done, 1)
                if n >= 1:
                    probs(n - 1)
                if n >= 4 and n % 2 == 0:
                    out_lo(n // 2 - 2)
            probs(H2 - 1)
            out_lo(6)
            out_lo(7)
            for i in range(4):
                lo(Slab(BASE["wo"] + i + RING))
                dve.wait_ge(slab_done, BASE["wo"] + i + 1)
                for m in range(2):
                    t = 2 * i + m
                    ins = dve.scalar_tensor_tensor(xlat[:, t, :], ps[:, i, m * T:m * T + T], mod[:, 1, 2 * KT + t, 0:1], xlat[:, t, :],
                                                   ALU.mult, ALU.add)
                ins.then_inc(x_ready, 1)
            norm_scale(9, xlat, gain_of(6), bufA)
            split_lo(8, bufA, shift=shift_of(1, 3, 0))
            ffn(3, "ffn2", xlat, shift_of(1, 5, 0))
            norm_scale(10, xlat, lambda t: col("final_g", t), xlat[:, :, :].rearrange("p a t -> p (a t)"))
            dve.wait_ge(y_done, KT * 11)
            dve.sem_inc(out_ready, 1)

        @block.tensor
        def _(pe):
            def mm3(out, w, x, start=False, stop=False):
                pe.matmul(out, w[0], x[0], start=start, stop=False, skip_group_check=True)
                pe.matmul(out, w[0], x[1], start=False, stop=False, skip_group_check=True)
                return pe.matmul(out, w[1], x[0], start=False, stop=stop, skip_group_check=True)

            def weights(g, pattern, **k):
                return (whi[:, g.slot, :].rearrange(pattern, **k), wlo[:, g.slot, :].rearrange(pattern, **k))

            def features(g, bank, x, kts=KT, tiles=2):
                pe.wait_ge(lo_done, g.number() + 1)
                w = weights(g, "p (k n) -> p k n", k=kts)
                for m in range(tiles):
                    for k in range(kts):
                        ins = mm3(ps[:, bank + m // 2, (m % 2) * T:(m % 2) * T + T],
                                  [a[:, k, m * P:m * P + P] for a in w], [a[:, k, :] for a in x],
                                  start=(k == 0 and m % 2 == 0), stop=(k == kts - 1))
                ins.then_inc(slab_done, 1)

            def tokens(g, bank, x):
                pe.wait_ge(lo_done, g.number() + 1)
                w = weights(g, "p (k n) -> p k n", k=KT)
                for s in range(2):
                    for k in range(KT):
                        ins = mm3(ps[:, bank, s * T:s * T + T], [a[:, k, s * P:s * P + P] for a in x],
                                  [a[:, k, :] for a in w], start=(k == 0 and s == 0), stop=(k == KT - 1))
                ins.then_inc(slab_done, 1)

            def means(n, sq):
                for t in range(KT):
                    if t % 4 == 0:
                        pe.wait_ge(sq_done, 2 * n + t // 4 + 1)
                    ins = pe.matmul(ps[:, 4, 0:T], ones[:, :], sq[:, t * T:t * T + T], start=(t == 0), stop=(t == KT - 1))
                ins.then_inc(ms_done, 1)

            H, G = (h_hi, h_lo), (g_hi, g_lo)
            pe.wait_ge(s_memset, 4)
            pe.wait_ge(s_relb, 1)
            pe.wait_ge(s_small, 64)
            pe.matmul(ps[0:H_MOBA, 5, :], relb[:, :], sra[0:BUCKETS + 1, 0:2, :], start=True, stop=True).then_inc(tab_done, 1)
            means(0, bufB)
            pe.wait_ge(s_consts, 16)
            pe.wait_ge(xlo_done, KT // 2)

            b0 = BASE["mix"]
            for g in range(27):
                if g >= 4:
                    pe.wait_ge(mix_drained, g - 3)
                if g == 0:
                    features(Slab(b0), 0, H, tiles=1)
                elif 5 <= g < 9 or 13 <= g < 15:
                    tokens(Slab(b0 + g), g % 4, H)
                else:
                    features(Slab(b0 + g), g % 4, H)
                if g == 2:
                    pe.wait_ge(mix_drained, 1)
                    pe.wait_ge(tab_sb, 1)
                    for s in range(2):
                        ins = pe.matmul(ps[:, 4 + s, :], alr[:, s * P:s * P + P], wlr, start=True, stop=True)
                    ins.then_inc(z_done, 1)
                if g == 4:
                    pe.wait_ge(la_done, 2)
                    for h in range(H_GLA):
                        for s in range(2):
                            la = bufB[:, 1024 + s * 512 + h * DK:1024 + s * 512 + h * DK + DK]
                            c = (h % 2) * T + s * P
                            ins = pe.matmul(ps[:, 6 + h // 2, c:c + P], la, cum, start=(h % 2 == 0 and s == 0),
                                            stop=True, skip_group_check=True)
                    ins.then_inc(b_done, 1)
                if g == 8:
                    pe.wait_ge(dec_done, 2)
                    for h in range(H_GLA):
                        for s in range(2):
                            a = h * 2 + s
                            ins = pe.matmul(ps[:, 4 + a // 4, (a % 4) * P:(a % 4) * P + P],
                                            bufA[:, 1024 + h * T + s * P:1024 + h * T + s * P + P],
                                            qa[:, h, s * P:s * P + P], start=(a % 4 == 0), stop=True, skip_group_check=True)
                    ins.then_inc(attn_done, 1)
                    pe.wait_ge(dec_done, 3)
                    for h in range(H_GLA):
                        for s in range(2):
                            ins = pe.transpose(ps[:, 6 + s, h * DK:h * DK + DK], bufB[:, h * T + s * P:h * T + s * P + P], eye)
                    ins.then_inc(kteT_done, 1)
                if g in (10, 11):
                    pe.wait_ge(attn_sb, 1)
                    pe.wait_ge(kteT_sb, 1)
                    if g == 11:
                        pe.wait_ge(state_done, 1)
                    for n in (0, 1) if g == 10 else (2,):
                        s, r0 = n // 2, (n % 2) * CHUNK
                        for h in range(H_GLA):
                            bank = (4, 6, 4)[n] + h // 2
                            k = bufB[r0:r0 + CHUNK, 1024 + s * 512 + h * DK:1024 + s * 512 + h * DK + DK]
                            ins = pe.matmul(ps[:, bank, (h % 2) * DV:(h % 2) * DV + DV], k,
                                            va[r0:r0 + CHUNK, s, h * DV:h * DV + DV],
                                            start=(h % 2 == 0), stop=True, skip_group_check=True)
                    ins.then_inc(kv_done, 1)
                if g == 12:
                    pe.wait_ge(attn_masked, 1)
                    pe.wait_ge(state_done, 9)
                    for h in range(H_GLA):
                        for d in range(2):
                            c = d * T
                            for s in range(2):
                                a = h * 2 + s
                                pe.matmul(ps[:, 4 + h, c + s * P:c + s * P + P],
                                          va[:, s, h * DV + d * P:h * DV + d * P + P], bufA[:, a * P:a * P + P],
                                          start=(d == 0 and s == 0), stop=False, skip_group_check=True)
                            for n in range(1, NCH):
                                S = ka[:, h, :] if n == 1 else state[:, n - 2, h, :]
                                ins = pe.matmul(ps[:, 4 + h, c + n * CHUNK:c + n * CHUNK + CHUNK], S[:, d * P:d * P + P],
                                                qa[:, h, n * CHUNK:n * CHUNK + CHUNK], start=False, stop=(n == NCH - 1),
                                                skip_group_check=True)
                    ins.then_inc(o_done, 1)
                if g == 14:
                    pe.wait_ge(o_sq, 1)
                    pe.wait_ge(o_sb, 1)
                    for h in range(H_GLA):
                        for d in range(2):
                            c = (h * 2 + d) * T
                            ins = pe.matmul(ps[:, 4 + h // 2, (h % 2) * T:(h % 2) * T + T], onesv[:, :], bufB[:, c:c + T],
                                            start=(h % 2 == 0 and d == 0), stop=(d == 1), skip_group_check=True)
                    ins.then_inc(oms_done, 1)
                if g in (18, 21, 24):
                    r = (g - 18) // 3
                    pe.wait_ge(p_done, r + 1)
                    if r:
                        pe.wait_ge(pt_sb, r)
                    pr = state[:, 0, :, :].rearrange("p h v -> p (h v)")
                    for a in range(8):
                        ins = pe.transpose(ps[:, 6 + a // 4, (a % 4) * P:(a % 4) * P + P], pr[:, a * P:a * P + P], eye)
                    ins.then_inc(pt_done, 1)
                if g in (15, 18, 21):
                    r = (g - 15) // 3
                    if r == 0:
                        pe.wait_ge(ostd_done, 1)
                        pe.wait_ge(brev_in, 16)
                        pe.wait_ge(mix_drained, 15)
                    else:
                        pe.wait_ge(sub_done, r)
                    n = P if r == 0 else T
                    for h in range(8) if r == 0 else range(4 * r - 4, 4 * r):
                        i = place(h, r) * n
                        out = ps[:, 4 + i // 512, i % 512:i % 512 + n]
                        r0, q0 = (h % 2) * DH, 0 if r == 0 else P
                        pe.matmul(out, mqk[r0:r0 + DH, 0, h // 2, q0:q0 + P], mqk[r0:r0 + DH, 1, h // 2, 0:n],
                                  start=(i % 512 == 0), stop=False, skip_group_check=True)
                        ins = pe.matmul(out, rev, brev[:, h, T - n:T], start=False, stop=True, skip_group_check=True)
                    ins.then_inc(sc_done, 1)
                if g == 25:
                    pe.wait_ge(pt_sb, 3)
                    for h in range(H_MOBA):
                        r0, bank, c = (h % 2) * DH, 4 + h // 4, (h // 2 % 2) * T
                        for q in range(2):
                            out = ps[r0:r0 + DH, bank, c + q * P:c + q * P + P]
                            for k in range(q + 1):
                                pt = pt_of(0) if q == 0 else pt_of(1 + h // 4)
                                a = place(h, 0) if q == 0 else place(h, 1) * 2 + k
                                pt = flat(pt)[:, a * P:a * P + P]
                                ins = pe.matmul(out, mv[:, k, h * DH:h * DH + DH], pt,
                                                start=(h % 4 < 2 and q == 0), stop=(k == q), skip_group_check=True)
                    ins.then_inc(ob_done, 1)

            M = [a[:, :, :, :].rearrange("p a b t -> p (a b) t") for a in (m_hi, m_lo)]
            for i in range(10):
                g = Slab(BASE["moba"] + i)
                if i < 2:
                    pe.wait_ge(oblo_done, 1)
                    pe.wait_ge(mix_drained, 27)
                    features(g, 2 * i, M, kts=4, tiles=4)
                elif i < 6:
                    pe.wait_ge(oalo_done, 2)
                    pe.wait_ge(br_drained, 1 if i < 4 else 2)
                    features(g, i - 2, G)
                else:
                    pe.wait_ge(br_drained, i - 3)
                    pe.wait_ge(mxlo_done, 4)
                    features(g, i - 6, H)
            pe.wait_ge(x_ready, 4)
            means(1, bufB)
            pe.wait_ge(xlo_done, KT)
            ffn_pe(pe, features, mm3, 0, "ffn0")
            means(2, bufB)

            pe.wait_ge(cond_lo, 2)
            pe.wait_ge(s_sel, 16)
            for layer in range(2):
                with pe.Fori(0, 8) as j:
                    for k in range(RING):
                        g = Slab(BASE[f"ada{layer}"] + k, 1, j)
                        pe.wait_ge(lo_done, g.number() + 1)
                        w = weights(g, "p (k n) -> p k n", k=KT)
                        for t in range(KT):
                            for part in range(2):
                                ins = pe.matmul(ps[:, k, 0:SLABC], cond[:, t, :], w[part][:, t, :], start=(t == 0 and part == 0),
                                                stop=(t == KT - 1 and part == 1))
                        ins.then_inc(slab_done, 1)
                    pe.wait_ge(row_done, 24 * layer + 3 * j + 3)
                    for k in range(RING):
                        for m in range(2):
                            c = (2 * k + m) * 2
                            ins = pe.matmul(ps[:, 3, c:c + 2], modrow[:, k, m * P:m * P + P], sel[:, :], start=(c == 0), stop=True,
                                            skip_group_check=True)
                    ins.then_inc(modT_done, 1)
                    pe.wait_ge(mod_done, 8 * layer + j + 1)

            def conformer(q, use1, use2):
                for j in range(4):
                    for half in range(2):
                        if j >= 2:
                            pe.wait_ge(v_done, 4 * q + j - 1)
                        features(Slab(BASE[use1] + 2 * j + half), 2 * (j % 2) + half, H)
                pe.wait_ge(dw_done, q + 1)
                for t in range(KT):
                    ins = pe.matmul(ps[:, 4, 0:T], ones[:, :], bufA[:, t * T:t * T + T], start=(t == 0), stop=(t == KT - 1))
                ins.then_inc(mu_done, 1)
                for t in range(KT):
                    pe.wait_ge(lsq_done, 2 * q + t // 4 + 1)
                    ins = pe.matmul(ps[:, 5, 0:T], ones[:, :], bufB[:, t * T:t * T + T], start=(t == 0), stop=(t == KT - 1))
                ins.then_inc(var_done, 1)
                pe.wait_ge(clo_done, 4 * q + 4)
                for i in range(4):
                    features(Slab(BASE[use2] + i), i, G)

            def split_ready(n):
                pe.wait_ge(xlo_done, KT // 2 * (n + 1))

            means(3, bufB)
            split_ready(2)
            conformer(0, "pw1_ctx", "pw2_ctx")
            means(4, bufB)
            split_ready(3)
            ffn_pe(pe, features, mm3, 1, "ffn_ctx")
            means(5, bufB)
            split_ready(4)
            conformer(1, "pw1_lat", "pw2_lat")
            means(6, bufB)
            split_ready(5)
            ffn_pe(pe, features, mm3, 2, "ffn_lat")
            means(7, bufB)
            means(8, bufB)
            split_ready(7)

            b0 = BASE["qkv"]

            def both(g, product):
                pe.wait_ge(lo_done, g.number() + 1)
                w = weights(g, "p (k n) -> p k n", k=KT)
                for bank, x in enumerate((G, H)):
                    for m in range(2):
                        for k in range(KT):
                            xs, ws = [a[:, k, :] for a in x], [a[:, k, :] for a in w]
                            a, b = ([v[:, m * P:m * P + P] for v in ws], xs) if product == "k" else ([v[:, m * P:m * P + P] for v in xs], ws)
                            ins = mm3(ps[:, bank + (0 if product == "k" else 2), m * T:m * T + T], a, b, start=(k == 0 and m == 0))
                ins.then_inc(slab_done, 1)

            def turn(raw_, bank, done):
                for a in range(2):
                    ins = pe.matmul(ps[:, bank, a * T:a * T + T], rot, raw_[:, a, :], start=(a == 0), stop=True, skip_group_check=True)
                ins.then_inc(done, 1)

            pe.wait_ge(s_late, 16)
            both(Slab(b0), "k")
            both(Slab(b0 + 1), "v")
            pe.wait_ge(kv_sb, 1)
            turn(k_raw, 4, krot_done)
            for i in range(4):
                pe.wait_ge(kv_sb, 2 if i < 2 else 3)
                features(Slab(b0 + 2 + i), i, G)
                if i >= 1:
                    pe.wait_ge(q_sb, i)
                    if i == 4:
                        pe.wait_ge(q_ready, 1)
                    turn(q_raw[:, 2 * i - 2:2 * i, :], 4 + i % 4, qrot_done)
            pe.wait_ge(q_sb, 4)
            pe.wait_ge(k_ready, 1)
            turn(q_raw[:, 6:8, :], 4, qrot_done)

            def wscores(n):
                i, u, b = n // 2, n % 2, n % 2
                r0 = u * DH
                pe.wait_ge(q_ready, 4 if n == 0 else i // 2 + 1)
                if n >= 2:
                    pe.wait_ge(we_done, n - 1)
                for s in range(2):
                    pe.matmul(ps[:, 2 * b + s, :], q_rot[r0:r0 + DH, i, s * P:s * P + P], k_all[r0:r0 + DH, i // 4, :],
                              start=True, stop=False, skip_group_check=True)
                    c = P if s == 0 else 0
                    ins = pe.matmul(ps[:, 2 * b + s, c:c + P], eye, wmask[:, s, :], start=False, stop=True, skip_group_check=True)
                ins.then_inc(ws_done, 1)

            def wturn(n):
                b = n % 2
                pe.wait_ge(wp_done, n + 1)
                if n >= 1:
                    pe.wait_ge(wt_sb, n)
                for k in range(4):
                    for s in range(2):
                        a = 2 * k + s
                        ins = pe.transpose(ps[:, 4 + a // 4, (a % 4) * P:(a % 4) * P + P],
                                           bufA[:, 1024 * b + 512 * s + k * P:1024 * b + 512 * s + k * P + P], eye)
                ins.then_inc(wt_done, 1)

            def wout(n):
                i, u, b = n // 2, n % 2, n % 2
                kv = 2 * (i // 4) + u
                pe.wait_ge(wt_sb, n + 1)
                if n >= 4:
                    pe.wait_ge(wolo_done, i - 1)
                for k in range(4):
                    ins = pe.matmul(ps[u * DH:u * DH + DH, 6 + i % 2, 0:T], v_all[:, k, kv * DH:kv * DH + DH],
                                    bufB[:, 1024 * b + k * T:1024 * b + k * T + T], start=(k == 0), stop=(k == 3), skip_group_check=True)
                ins.then_inc(wo_done, 1)

            wscores(0)
            for n in range(H2):
                if n + 1 < H2:
                    wscores(n + 1)
                wturn(n)
                if n >= 1:
                    wout(n - 1)
            wout(H2 - 1)
            pe.wait_ge(wolo_done, KT)
            for i in range(4):
                features(Slab(BASE["wo"] + i), i, G)
            means(9, bufB)
            split_ready(8)
            ffn_pe(pe, features, mm3, 3, "ffn2")
            means(10, bufB)


def kernel(**inputs):
    import concourse.bacc as bacc
    from concourse.bass_utils import run_bass_kernel_spmd as run

    a = {k: np.asarray(v) for k, v in inputs.items()}
    COL, NCOL = columns()
    STORE, n_slabs = stored()

    def tiles(v):
        return np.ascontiguousarray(np.asarray(v).reshape(-1, P).T)

    w = np.zeros((n_slabs, P, SLAB), np.float32)

    def put(name, i, block):
        k = block.shape[0] // P
        w[STORE[name][0] + i] = block.reshape(k, P, -1).transpose(1, 0, 2).reshape(P, SLAB)

    def put_columns(name, i, mat, c0):
        put(name, i, mat[:, c0:c0 + SLABC])

    def put_ffn(name, up, down):
        ups = [0] + [3 * j - 1 for j in range(1, NJ)]
        for j, i in enumerate(ups):
            put_columns(name, i, up, j * SLABC)
            put_columns(name, i + 1, up, D_FF + j * SLABC)
            put(name, 3 * NJ - 1 if j == NJ - 1 else 3 * j + 4, down[j * SLABC:(j + 1) * SLABC])

    win = a["w_in"][0]
    o_qa, o_ka, o_va, o_ra = 0, GLA_W, 2 * GLA_W, 2 * GLA_W + V_W
    o_lr = o_ra + V_W
    o_qb = o_lr + RANK
    o_kb, o_vb, o_g = o_qb + MOBA_W, o_qb + 2 * MOBA_W, o_qb + 3 * MOBA_W
    lr = np.zeros((D, SLABC), np.float32)
    lr[:, 0:RANK] = win[:, o_lr:o_lr + RANK]
    put("mix", 0, lr)
    i = 1
    for c0, width in [(o_ka, GLA_W), (o_qa, GLA_W), (o_va, V_W), (o_kb, MOBA_W), (o_qb, MOBA_W), (o_vb, MOBA_W),
                      (o_ra, V_W), (o_g, 2 * D)]:
        for c in range(c0, c0 + width, SLABC):
            put_columns("mix", i, win, c)
            i += 1
    for i in range(2):
        put("moba", i, a["w_branch_moba"][0][:, i * 512:(i + 1) * 512])
    for i in range(4):
        put_columns("gla", i, a["w_branch_gla"][0], i * SLABC)
        put_columns("out", i, a["w_out"][0], i * SLABC)
    put_ffn("ffn0", a["w_up"][0], a["w_down"][0])
    for layer in range(2):
        for i in range(24):
            put_columns(f"ada{layer}", i, a["ada_w_2"][layer], i * SLABC)
        put_ffn(f"ffn{layer + 1}", a["ffn_w_up_2"][layer], a["ffn_w_down_2"][layer])
    for j in range(4):
        put_columns("pw1", 2 * j, a["conv_w_pw1_2"][0], j * SLABC)
        put_columns("pw1", 2 * j + 1, a["conv_w_pw1_2"][0], D + j * SLABC)
        put_columns("pw2", j, a["conv_w_pw2_2"][0], j * SLABC)
    pairs = [(h, h + 4) for g in (0, 8) for h in range(g, g + 4)]
    by_pair = np.concatenate([np.arange(h * DH, (h + 1) * DH) for p in pairs for h in p])
    wqkv = a["attn_w_qkv_2"][0]
    put_columns("qkv", 0, wqkv, H2 * DH)
    put_columns("qkv", 1, wqkv, (H2 + HKV) * DH)
    wq, wo = wqkv[:, :H2 * DH][:, by_pair], a["attn_w_o_2"][0][by_pair]
    for i in range(4):
        put_columns("qkv", 2 + i, wq, i * SLABC)
        put_columns("wo", i, wo, i * SLABC)

    cols = np.zeros((P, NCOL), np.float32)

    def put_cols(name, v):
        c, k = COL[name]
        cols[:, c:c + k] = tiles(v)

    put_cols("norm_mix", a["norm_mix"][0])
    put_cols("gla_out_norm", a["gla_out_norm"][0])
    put_cols("norm_ffn", a["norm_ffn"][0])
    put_cols("norm_final", a["norm_final"])
    put_cols("ffn_w0", a["conv_w"][0])
    put_cols("ffn_b0", a["conv_b"][0])
    for layer in range(2):
        put_cols(f"ffn_w{layer + 1}", a["ffn_w_dw_2"][layer])
        put_cols(f"ffn_b{layer + 1}", a["ffn_b_dw_2"][layer])
        put_cols(f"norm1_{layer}", a["norm1_g_2"][layer])
        put_cols(f"norm2_{layer}", a["norm2_g_2"][layer])
        put_cols(f"ada_b{layer}", a["ada_b_2"][layer])
    put_cols("final_g", a["final_g_2"])
    for name, key in [("pw1_b", "conv_b_pw1_2"), ("dw_w", "conv_w_dw_2"), ("dw_b", "conv_b_dw_2"), ("ln_g", "conv_ln_g_2"),
                      ("ln_b", "conv_ln_b_2"), ("pw2_b", "conv_b_pw2_2")]:
        put_cols(name, a[key][0])
    put_cols("cond", np.concatenate([a["c_2"][0], a["c_ctx_2"]]))
    c, k = COL["sink"]
    cols[:, c:c + k] = a["attn_sink_2"][0][[h for p in pairs for h in p]][None, :]

    eye = np.eye(P, dtype=np.float32)
    tok = np.arange(P)
    cum = ((tok[:, None] <= tok[None, :]) & (tok[:, None] // CHUNK == tok[None, :] // CHUNK)) / TAU
    consts = np.stack([eye, eye[::-1], cum.astype(np.float32)], axis=1)
    dist = T - 1 - np.arange(2 * T)
    half = BUCKETS // 2
    far = half + (np.log(np.maximum(dist, 1).astype(np.float32) / half) / np.float32(np.log(MAX_DIST / half))
                  * (BUCKETS - half)).astype(np.int32)
    bucket = np.where(dist < half, dist, np.minimum(far, BUCKETS - 1))
    bucket = np.where(dist < 0, BUCKETS, bucket)
    onehot = (np.arange(BUCKETS + 1)[:, None] == bucket[None, :]).astype(np.float32)

    pos = np.arange(T)
    freqs = (np.float32(ROPE_BASE) ** (-np.arange(DH // 4, dtype=np.float32) / (DH // 4))).astype(np.float32)
    angle = np.concatenate([(pos // GRID_W).astype(np.float32)[:, None] * freqs, (pos % GRID_W).astype(np.float32)[:, None] * freqs], axis=1)
    rope = [np.tile(f(angle).T.astype(np.float32), (4, 1)) for f in (np.cos, np.sin)]
    rot = np.zeros((P, P), np.float32)
    for h in (0, DH):
        for d in range(DH // 2):
            rot[h + DH // 2 + d, h + d] = -1.0
            rot[h + d, h + DH // 2 + d] = 1.0
    outside = [np.where(tok[None, :] > tok[:, None], NEG, 0.0), np.where(tok[None, :] < tok[:, None], NEG, 0.0)]
    tables = np.concatenate(rope + [rot] + outside, axis=1).astype(np.float32)
    sel = np.array([[1, 0], [1, 0], [0, 1], [0, 1]], np.float32)

    arrays = {
        "tables": tables, "sel": sel,
        "ctxT": np.ascontiguousarray(a["ctx_2"][0].T.reshape(KT, P, T).transpose(1, 0, 2)),
        "w": w, "cols": cols, "consts": np.ascontiguousarray(consts), "onehot": onehot.reshape(BUCKETS + 1, 2, T),
        "xT": np.ascontiguousarray(a["x"][0].T.reshape(KT, P, T).transpose(1, 0, 2)),
        "rel_bias": a["rel_bias"], "w_lr_up": a["w_lr_up"][0], "b_forget": a["b_forget"],
    }
    arrays = {f"{k}_dram": np.ascontiguousarray(v) for k, v in arrays.items()}

    nc = bacc.Bacc("TRN2", target_bir_lowering=False, num_devices=1)
    io = {k[:-5]: nc.dram_tensor(k, v.shape, F32, kind="ExternalInput").ap() for k, v in arrays.items()}
    io["out"] = nc.dram_tensor("out_dram", (P, KT, T), F32, kind="ExternalOutput").ap()
    io["scratch"] = nc.dram_tensor("bias_rows", (H_MOBA, 512), F32, kind="Internal").ap()
    build(nc, io, RUN_ORDER)
    got = run(nc, [arrays], core_ids=[0]).results[0]["out_dram"]
    return np.ascontiguousarray(got.transpose(2, 1, 0).reshape(1, T, D))


RUN_ORDER = [("mix", "mix"), ("moba", "moba"), ("gla", "gla"), ("out", "out"), ("ffn0", "ffn0"),
             ("ada0", "ada0"), ("ada1", "ada1"), ("pw1", "pw1_ctx"), ("pw2", "pw2_ctx"), ("ffn1", "ffn_ctx"),
             ("pw1", "pw1_lat"), ("pw2", "pw2_lat"), ("ffn1", "ffn_lat"), ("qkv", "qkv"), ("wo", "wo"), ("ffn2", "ffn2")]
```

```python
from contextlib import ExitStack

import numpy as np

import concourse.bass as bass
from concourse import mybir

F32 = mybir.dt.float32
F32R = mybir.dt.float32r
ACT = mybir.ActivationFunctionType
ALU = mybir.AluOpType
AX = mybir.AxisListType

P = 128
T = 256
D = 1024
KT = D // P
EPS = 1e-6
SLAB = 2048
SLABC = 256
RING = 3

H_GLA, DK, DV, CHUNK, RANK, TAU = 4, 128, 256, 64, 16, 16.0
NCH = T // CHUNK
H_MOBA, DH = 8, 64
BUCKETS, MAX_DIST = 32, 128
NEG = -1e30
D_FF = 2816
NJ = D_FF // SLABC
FT = D_FF // P
TAPS = 3
CONV_TAPS = 31
PADC = (CONV_TAPS - 1) // 2
H2, HKV, WINDOW, GRID_W, ROPE_BASE = 16, 4, 128, 64, 10000.0
GLA_W, V_W, MOBA_W = H_GLA * DK, H_GLA * DV, H_MOBA * DH


def columns():
    at, n = {}, 0
    for name, k in [
        ("norm_mix", KT), ("gla_out_norm", KT), ("norm_ffn", KT), ("norm_final", KT),
        ("ffn_w0", TAPS * 2 * FT), ("ffn_w1", TAPS * 2 * FT), ("ffn_w2", TAPS * 2 * FT),
        ("ffn_b0", 2 * FT), ("ffn_b1", 2 * FT), ("ffn_b2", 2 * FT),
        ("norm1_0", KT), ("norm1_1", KT), ("norm2_0", KT), ("norm2_1", KT), ("final_g", KT),
        ("pw1_b", 2 * KT), ("dw_w", CONV_TAPS * KT), ("dw_b", KT), ("ln_g", KT), ("ln_b", KT), ("pw2_b", KT),
        ("ada_b0", 48), ("ada_b1", 48), ("cond", 2 * KT), ("sink", H2),
    ]:
        at[name] = (n, k)
        n += k
    return at, n


N_MIX, N_ADA = 27, 6 * D // SLABC

ADA_FIRST = 3
LEAD = [("ada", i) for i in range(ADA_FIRST)]
for _g in range(N_MIX):
    LEAD.append(("mix", _g))
    if ADA_FIRST + _g < N_ADA:
        LEAD.append(("ada", ADA_FIRST + _g))
AT = {item: n for n, item in enumerate(LEAD)}

RUN_ORDER = [
    ("lead", "lead", 0, len(LEAD)), ("moba", "moba", 0, 2), ("gla", "gla", 0, 4),
    ("pw1_ctx_a", "pw1", 0, 2), ("out", "out", 0, 4), ("pw1_ctx_b", "pw1", 2, 6), ("ffn0", "ffn0", 0, 3 * NJ),
    ("ada_a", "ada1", 0, 6), ("pw2_ctx", "pw2", 0, 4), ("pw1_lat", "pw1", 0, 8), ("ffn_ctx", "ffn1", 0, 3 * NJ),
    ("ada_b", "ada1", 6, 6), ("pw2_lat", "pw2", 0, 4), ("ada_c", "ada1", 12, 6), ("ffn_lat", "ffn1", 0, 3 * NJ),
    ("ada_d", "ada1", 18, 6), ("qkv", "qkv", 0, 6), ("wo", "wo", 0, 4), ("ffn2", "ffn2", 0, 3 * NJ),
]


def stored():
    at, n = {}, 0
    for _, name, first, k in RUN_ORDER:
        at[name] = max(at.get(name, 0), first + k)
    out = {}
    for name, k in at.items():
        out[name] = (n, k)
        n += k
    return out, n


def stream():
    at, n = {}, 0
    for use, _, _, k in RUN_ORDER:
        at[use] = n
        n += k
    return at, n


def pool_words(use):
    return 1920 if use in ("ffn0", "ffn_ctx") else 1024


class Slab:

    def __init__(self, c, n=0, j=0):
        self.c, self.n, self.j = c, n, j

    def __add__(self, k):
        return Slab(self.c + k, self.n, self.j)

    @property
    def slot(self):
        return self.c % RING

    def number(self):
        return self.c + 3 * self.n * self.j

    def landings(self):
        return 16 * (self.c // RING + 1) + 16 * self.n * self.j


class Tally:

    def __init__(self, sem):
        self.sem, self.n, self.j, self.per, self.n0 = sem, 0, None, 0, 0

    def mark(self, ins):
        ins.then_inc(self.sem, 1)
        self.n += 1

    def value(self):
        return self.n if self.j is None else self.n + self.per * self.j

    def enter(self, j, per):
        self.j, self.per, self.n0 = j, per, self.n

    def leave(self, times):
        assert self.n - self.n0 == self.per, (self.n, self.n0, self.per)
        self.n, self.j = self.n0 + self.per * times, None


def build(nc, io):
    COL, NCOL = columns()
    STORE, _ = stored()
    BASE, TOTAL = stream()
    ctx = ExitStack()
    with ctx:
        def sb(name, shape, dt=F32):
            return ctx.enter_context(nc.sbuf_tensor(name, shape, dt))

        def sem(name):
            return ctx.enter_context(nc.semaphore(name))

        ps = ctx.enter_context(nc.psum_tensor("ps", [P, 8, 512], F32))
        raw = sb("raw", [P, RING, SLAB])
        whi = sb("whi", [P, RING, SLAB], F32R)
        wlo = sb("wlo", [P, RING, SLAB], F32R)
        xlat = sb("xlat", [P, KT, T])
        h_hi = sb("h_hi", [P, KT, T], F32R)
        h_lo = sb("h_lo", [P, KT, T], F32R)
        g_hi = sb("g_hi", [P, KT, T], F32R)
        g_lo = sb("g_lo", [P, KT, T], F32R)
        m_hi = sb("m_hi", [P, 2, 2, T], F32R)
        m_lo = sb("m_lo", [P, 2, 2, T], F32R)
        cnd = sb("cnd", [P, 4 * KT + P - 4], F32R)
        cva = sb("cva", [P, 2, 2, T])
        cvb = sb("cvb", [P, 2, 2, T])
        bufA = sb("bufA", [P, SLAB])
        bufB = sb("bufB", [P, SLAB])
        gates = sb("gates", [P, 2 * KT, T])
        sra = sb("sra", [P, KT, T])
        mqk = sb("mqk", [P, 2, 4, T])
        mv = sb("mv", [P, 2, MOBA_W])
        state = sb("state", [P, 2, H_GLA, DV])
        brev = sb("brev", [P, H_MOBA, T])
        cols = sb("cols", [P, NCOL])
        ones = sb("ones", [P, P])
        consts = sb("consts", [P, 3, P])
        rstd = sb("rstd", [P, 2, T])
        tiny = sb("tiny", [P, 64])
        relb = sb("relb", [BUCKETS + 1, H_MOBA])
        epsc = sb("epsc", [P, 1])
        mod = sb("mod", [P, 2, 6 * KT, 2])
        amod = sb("amod", [P, 7, KT])
        sel = sb("sel", [4, 2])

        def flat(a):
            names = "abc"[:len(a.shape) - 1]
            return a.rearrange(f"p {' '.join(names)} -> p ({' '.join(names)})")

        qa, ka = gates[:, 0:4, :], gates[:, 4:8, :]
        va = flat(gates[:, 8:16, :]).rearrange("p (s n) -> p s n", s=2)
        wlr, alr = mv[0:RANK + 1, 0, :], mv[0:RANK + 1, 1, 0:T]
        eye, rev, cum = (consts[:, i, :] for i in range(3))
        modrow = cvb[0:4, 1, :, :]
        lstd = cvb[:, 0, :, :]
        xctx = brev
        g_flat = flat(gates[:, :, :])
        VP = T + 2 * PADC
        vpad = g_flat[:, 0:KT * VP].rearrange("p (t n) -> p t n", t=KT)
        acc = sra
        late = KT * VP
        rope_cs = g_flat[:, late:late + 2 * T].rearrange("p (a t) -> p a t", a=2)
        rot = g_flat[:, late + 2 * T:late + 2 * T + P]
        wmask = g_flat[:, late + 2 * T + P:late + 2 * T + 3 * P].rearrange("p (a k) -> p a k", a=2)
        ctx_sq, ctx_y = flat(mqk[:, :, :, :]), flat(sra[:, :, :])
        q_raw, q_rot = sra, mqk[:, :, :, :].rearrange("p a b t -> p (a b) t")
        k_raw = mv[:, 0, :].rearrange("p (a t) -> p a t", a=2)
        k_all = flat(state[:, 0, :, :]).rearrange("p (a n) -> p a n", a=2)
        v_all = state[:, 1, :, :]

        def col(name, i=0):
            c = COL[name][0]
            return cols[:, c + i:c + i + 1]

        MODULATED = [(0, 1, 1, "norm1_0"), (0, 4, 1, "norm2_0"), (0, 1, 0, "norm1_0"), (0, 4, 0, "norm2_0"),
                     (1, 1, 1, "norm1_1"), (1, 1, 0, "norm1_1"), (1, 4, 0, "norm2_1")]

        def gain_of(i):
            return lambda t: amod[:, i, t:t + 1]

        def shift_of(layer, i, s):
            return lambda t: mod[:, layer, i * KT + t, s:s + 1]

        s_cols, s_consts, s_small, s_x = sem("cols_landed"), sem("consts_landed"), sem("small_landed"), sem("x_landed")
        s_ctx, s_late = sem("context_landed"), sem("tables_landed")
        s_memset, s_relb = sem("memsets_done"), sem("later_keys_set")
        landed = [sem(f"slab_landed{i}") for i in range(RING)]
        hi_done, slab_done = sem("slab_hi_done"), sem("slab_used")
        lo_done, lo2_done = sem("slab_lo_done_by_vector"), sem("slab_lo_done_by_gpsimd")
        dve_order, act_order, pool_order = sem("dve_order"), sem("act_order"), sem("pool_order")
        sq_done, ms_done, std_done, y_done = sem("squares_done"), sem("means_done"), sem("std_done"), sem("normed")
        xhi_done, xlo_done = sem("act_hi_done"), sem("act_lo_done")
        mix_drained = sem("mix_drained")
        z_done, la_done, b_done, blast = sem("z_done"), sem("la_done"), sem("b_done"), sem("blast_done")
        exps_done, dec_done = sem("exps_done"), sem("decayed_done")
        attn_done, attn_sb, attn_masked = sem("attn_done"), sem("attn_copied"), sem("attn_masked")
        kteT_done, kteT_sb = sem("kteT_done"), sem("kteT_copied")
        kv_done, state_done = sem("kv_done"), sem("state_done")
        o_done, o_sq, o_sb, oms_done, ostd_done = sem("o_done"), sem("o_squared"), sem("o_copied"), sem("o_means_done"), sem("o_std_done")
        oa_done, oahi_done, oalo_done = sem("oa_done"), sem("oa_hi_done"), sem("oa_lo_done")
        tab_done, tab_sb, tab_out, brev_in = sem("bias_row_done"), sem("bias_row_copied"), sem("bias_row_stored"), sem("bias_landed")
        sc_done, sub_done, e_done, p_done = sem("scores_done"), sem("scores_less_max"), sem("exp_done"), sem("probs_done")
        pt_done, pt_sb, ob_done, obhi_done, oblo_done = sem("probsT_done"), sem("probsT_copied"), sem("ob_done"), sem("ob_hi_done"), sem("ob_lo_done")
        br_drained, mixed_done, mxhi_done, mxlo_done = sem("branch_drained"), sem("mixed_done"), sem("mixed_hi_done"), sem("mixed_lo_done")
        x_ready = sem("residual_ready")
        tap0, conv_out, silu_done, mid_f, mid_hi, mid_lo = sem("tap0_done"), sem("conv_done"), sem("silu_done"), sem("mid_done"), sem("mid_hi_done"), sem("mid_lo_done")
        cond_f, cond_zero, cond_hi, cond_lo = sem("cond_done"), sem("cond_cleared"), sem("cond_hi_done"), sem("cond_lo_done")
        row_done, modT_done, mod_done, amod_done = sem("mod_rows_done"), sem("mod_turned"), sem("mod_done"), sem("amod_done")
        sg_done, v_done, pads_done, dw_done = sem("sigmoid_done"), sem("glu_done"), sem("pads_cleared"), sem("dwconv_done")
        mu_done, cen_done, lsq_done, var_done = sem("ln_mean_done"), sem("ln_centred"), sem("ln_squared"), sem("ln_var_done")
        lstd_done, lnorm_done, act_done = sem("ln_std_done"), sem("ln_normed"), sem("ln_silu_done")
        chi_done, clo_done = sem("conv_act_hi_done"), sem("conv_act_lo_done")
        kv_sb, krot_done, k_ready = sem("kv_copied"), sem("k_turned"), sem("k_roped")
        q_sb, qrot_done, q_ready = sem("q_copied"), sem("q_turned"), sem("q_roped")
        ws_done, wmax_done, we_done, wp_done = sem("window_scores"), sem("window_max"), sem("window_exp"), sem("window_probs")
        wt_done, wt_sb, wo_done, wohi_done, wolo_done = (sem("window_probsT"), sem("window_probsT_copied"), sem("window_out"),
                                                        sem("window_out_hi"), sem("window_out_lo"))
        out_ready, out_stored = sem("out_ready"), sem("out_stored")

        def place(h, r):
            return h % 2 * 4 + h // 2 if r == 0 else h % 2 * 2 + h % 4 // 2

        def pt_of(r):
            return [state[:, 1, :, :], cva[:, :, :, :], cvb[:, :, :, :]][r]

        def down_slab(b0, j):
            return b0 + 3 * j + 4

        def use_of(c):
            return [use for use, _, _, _ in RUN_ORDER if BASE[use] <= c][-1]

        def ffn_v(f):
            return (0, 1, 1, 2)[f]

        block = ctx.enter_context(nc.Block())

        def ffn_act(act, hi, f, use):
            b0 = BASE[use]
            centre = 2 if f == 0 else 1
            c, b = COL[f"ffn_w{ffn_v(f)}"][0] + centre * 2 * FT, COL[f"ffn_b{ffn_v(f)}"][0]

            def tap(half, j, par):
                buf = (cva, cvb)[half]
                for m in range(2):
                    t = 2 * j + (m + half * FT)
                    ins = act.activation(buf[:, par, m, :], ps[:, 2 * par + half, m * T:m * T + T], ACT.Identity,
                                         scale=cols[:, bass.ds(t + c, 1)], bias=cols[:, bass.ds(t + b, 1)])
                ins.then_inc(tap0, 1)

            def up(g, j, par, first):
                hi(g + RING)
                act.wait_ge(slab_done, g.number() + 1)
                if not first:
                    act.wait_ge(mid_f, j + (f * NJ - 1))
                tap(0, j, par)
                hi(g + (RING + 1))
                act.wait_ge(slab_done, g.number() + 2)
                if not first:
                    act.wait_ge(mid_lo, j + (f * NJ - 1))
                tap(1, j, par)
                act.wait_ge(conv_out, 2 * j + (f * 2 * NJ + 1))
                act.activation(cva[:, par, :, :], cva[:, par, :, :], ACT.Silu).then_inc(silu_done, 1)

            def split(j, par, first):
                act.wait_ge(mid_f, j + (f * NJ + 1))
                if not first:
                    act.wait_ge(slab_done, down_slab(b0, j - 2) + 1)
                act.activation(m_hi[:, par, :, :], cvb[:, par, :, :], ACT.Copy).then_inc(mid_hi, 1)

            up(Slab(b0), 0, 0, True)
            split(0, 0, True)
            up(Slab(b0 + 2), 1, 1, True)
            hi(Slab(b0 + 4 + RING))
            split(1, 1, True)
            with act.Fori(0, 4) as jj:
                for u in range(2):
                    g = Slab(b0 + 5 + 3 * u, 2, jj)
                    up(g, 2 * jj + (2 + u), u, False)
                    hi(g + (2 + RING))
                    split(2 * jj + (2 + u), u, False)
            g = Slab(b0 + 3 * NJ - 4)
            up(g, NJ - 1, 0, False)
            hi(g + (2 + RING))
            split(NJ - 1, 0, False)
            hi(g + (3 + RING))

        def ffn_dve(dve, lo, order, f, use, host=None):
            b0 = BASE[use]
            shifted = [(0, 2, -2), (1, 1, -1)] if f == 0 else [(0, 1, -1), (2, 0, 1)]
            c0 = COL[f"ffn_w{ffn_v(f)}"][0]

            def taps(half, j, par):
                buf = (cva, cvb)[half]
                dve.wait_ge(tap0, 2 * j + (f * 2 * NJ + half + 1))
                for i, (k, first, shift) in enumerate(shifted):
                    n = T - abs(shift)
                    src = first + shift
                    for m in range(2):
                        w = cols[:, bass.ds(2 * j + (c0 + k * 2 * FT + half * FT + m), 1)]
                        out = buf[:, par, m, first:first + n]
                        ins = dve.scalar_tensor_tensor(out, ps[:, 2 * par + half, m * T + src:m * T + src + n], w, out,
                                                       ALU.mult, ALU.add)
                        if i == 0:
                            order.mark(ins)
                    if i == 0:
                        dve.wait_ge(dve_order, order.value())
                ins.then_inc(conv_out, 1)

            def pair(g, j, par, down):
                lo(g + RING)
                taps(0, j, par)
                if host and down:
                    host(j, 0)
                lo(g + (RING + 1))
                taps(1, j, par)
                dve.wait_ge(silu_done, j + (f * NJ + 1))
                dve.wait_ge(conv_out, 2 * j + (f * 2 * NJ + 2))
                dve.tensor_tensor(cvb[:, par, :, :], cva[:, par, :, :], cvb[:, par, :, :], ALU.mult).then_inc(mid_f, 1)
                if host and down:
                    host(j, 1)
                if down:
                    lo(g + (2 + RING))
                dve.wait_ge(mid_hi, j + (f * NJ + 1))
                dve.tensor_tensor(m_lo[:, par, :, :], cvb[:, par, :, :], m_hi[:, par, :, :].bitcast(F32), ALU.subtract)\
                   .then_inc(mid_lo, 1)
                if host and down:
                    host(j, 2)

            pair(Slab(b0), 0, 0, False)
            pair(Slab(b0 + 2), 1, 1, True)
            with dve.Fori(0, 4) as jj:
                order.enter(jj, 8 + (6 * KT if host else 0))
                for u in range(2):
                    pair(Slab(b0 + 5 + 3 * u, 2, jj), 2 * jj + (2 + u), u, True)
                order.leave(4)
            g = Slab(b0 + 3 * NJ - 4)
            pair(g, NJ - 1, 0, True)
            lo(g + (3 + RING))

        def ffn_pe(pe, features, mm3, f, use, split, free):
            b0 = BASE[use]
            G = (g_hi, g_lo)

            def up(g, j, par, first):
                for half in range(2):
                    if not first:
                        pe.wait_ge(conv_out, 2 * j + (f * 2 * NJ + half - 3))
                    features(g + half, 2 * par + half, G, split=split if first and j == 0 and half == 0 else None)

            def down(g, j, par, first=False):
                pe.wait_ge(lo_done, g.number() + 1)
                pe.wait_ge(lo2_done, g.number() + 1)
                pe.wait_ge(mid_lo, j + (f * NJ + 1))
                w = [a[:, g.slot, :].rearrange("p (k n) -> p k n", k=2) for a in (whi, wlo)]
                for m in range(KT):
                    for k in range(2):
                        ins = mm3(ps[:, 4 + m // 2, (m % 2) * T:(m % 2) * T + T], [a[:, k, m * P:m * P + P] for a in w],
                                  [m_hi[:, par, k, :], m_lo[:, par, k, :]], start=(first and k == 0 and m % 2 == 0))
                ins.then_inc(slab_done, 1)

            pe.wait_ge(*free[0])
            up(Slab(b0), 0, 0, True)
            pe.wait_ge(*free[1])
            up(Slab(b0 + 2), 1, 1, True)
            down(Slab(b0 + 4), 0, 0, True)
            with pe.Fori(0, 4) as jj:
                for u in range(2):
                    g = Slab(b0 + 5 + 3 * u, 2, jj)
                    up(g, 2 * jj + (2 + u), u, False)
                    down(g + 2, 2 * jj + (1 + u), 1 - u)
            up(Slab(b0 + 3 * NJ - 4), NJ - 1, 0, False)
            down(Slab(b0 + 3 * NJ - 2), NJ - 2, 1)
            down(Slab(b0 + 3 * NJ - 1), NJ - 1, 0)

        @block.sync
        def _(sp):
            def load(name, first, g):
                if g.c >= RING:
                    sp.wait_ge(lo_done, (g + -RING).number() + 1)
                    sp.wait_ge(lo2_done, (g + -RING).number() + 1)
                sp.dma_start(raw[:, g.slot, :], io["w"][bass.ds(STORE[name][0] + first, 1)]).then_inc(landed[g.slot], 16)

            def run(use, name, first, k0, k1):
                times = (k1 - k0) // RING
                if times > 1:
                    with sp.Fori(0, times) as j:
                        for k in range(RING):
                            load(name, 3 * j + (first + k0 + k), Slab(BASE[use] + k0 + k, 1, j))
                    k0 += RING * times
                for k in range(k0, k1):
                    load(name, first + k, Slab(BASE[use] + k))

            sp.dma_start(xlat[:, :, :], io["xT"]).then_inc(s_x, 16)
            sp.dma_start(cols[:, :], io["cols"]).then_inc(s_cols, 16)
            for use, name, first, count in RUN_ORDER:
                if use == "lead":
                    run(use, name, first, 0, RING)
                    sp.dma_start(relb[0:BUCKETS, :], io["rel_bias"]).then_inc(s_small, 16)
                    sp.dma_start(sra[0:BUCKETS + 1, 0:2, :], io["onehot"]).then_inc(s_small, 16)
                    sp.dma_start(sel[:, :], io["sel"]).then_inc(s_small, 16)
                    sp.dma_start(wlr[0:RANK, :], io["w_lr_up"]).then_inc(s_small, 16)
                    sp.dma_start(wlr[RANK:RANK + 1, :], io["b_forget"]).then_inc(s_small, 16)
                    sp.dma_start(consts[:, :, :], io["consts"]).then_inc(s_consts, 16)
                    run(use, name, first, RING, 4 * RING)
                    sp.wait_ge(tab_sb, 1)
                    sp.dma_start(io["scratch"], flat(state[0:H_MOBA, 0, 0:2, :])).then_inc(tab_out, 16)
                    run(use, name, first, 4 * RING, 6 * RING)
                    sp.wait_ge(tab_out, 16)
                    sp.dma_start(brev[:, :, :], bass.AP(io["scratch"].tensor, 0, [[1, P], [512, H_MOBA], [1, T]]))\
                      .then_inc(brev_in, 16)
                    run(use, name, first, 6 * RING, count)
                    sp.wait_ge(sc_done, 3)
                    sp.dma_start(xctx[:, :, :], io["ctxT"]).then_inc(s_ctx, 16)
                    continue
                run(use, name, first, 0, count)
                if use == "pw1_ctx_b":
                    sp.wait_ge(br_drained, 2)
                    sp.dma_start(g_flat[:, late:late + 2 * T + 3 * P], io["tables"]).then_inc(s_late, 16)
            sp.wait_ge(out_ready, 1)
            sp.dma_start(io["out"], xlat[:, :, :]).then_inc(out_stored, 16)
            sp.wait_ge(out_stored, 16)

        @block.gpsimd
        def _(pool):
            pool.memset(ones[:, :], 1.0 / D).then_inc(s_memset, 1)
            pool.memset(epsc[:, :], EPS).then_inc(s_memset, 1)
            pool.memset(alr, 1.0).then_inc(s_memset, 1)

            def run(use, k0, k1):
                part = slice(SLAB - pool_words(use), SLAB)

                def lo(g):
                    pool.wait_ge(hi_done, g.number() + 1)
                    pool.tensor_tensor(wlo[:, g.slot, part], raw[:, g.slot, part], whi[:, g.slot, part].bitcast(F32),
                                       ALU.subtract).then_inc(lo2_done, 1)

                times = (k1 - k0) // RING
                if times > 1:
                    with pool.Fori(0, times) as j:
                        for k in range(RING):
                            lo(Slab(BASE[use] + k0 + k, 1, j))
                    k0 += RING * times
                for k in range(k0, k1):
                    lo(Slab(BASE[use] + k))

            masked_at = AT["mix", 8] + RING + 2
            run("lead", 0, masked_at)
            attn = bufA[:, 0:1024].rearrange("p (a i) -> p a i", i=P)
            pool.wait_ge(attn_sb, 1)
            pool.affine_select(out=attn, in_=attn, compare_op=ALU.is_ge, fill=0.0, base=0,
                               pattern=[[0, 8], [1, P]], channel_multiplier=-1).then_inc(pool_order, 1)
            pool.wait_ge(pool_order, 1)
            pool.memset(attn[0:CHUNK, :, CHUNK:P], 0.0).then_inc(attn_masked, 1)
            run("lead", masked_at, len(LEAD))
            for use, _, _, count in RUN_ORDER[1:]:
                run(use, 0, count)

        @block.scalar
        def _(act):
            order = Tally(act_order)

            def hi(g):
                if isinstance(g.j, int) and g.c >= TOTAL:
                    return
                act.wait_ge(landed[g.slot], g.landings())
                if g.c >= RING:
                    act.wait_ge(slab_done, (g + -RING).number() + 1)
                act.activation(whi[:, g.slot, :], raw[:, g.slot, :], ACT.Copy).then_inc(hi_done, 1)

            def squares(x, sq):
                for i in range(2):
                    act.activation(sq[:, 1024 * i:1024 * i + 1024], x[:, 4 * i:4 * i + 4, :], ACT.Square).then_inc(sq_done, 1)

            def root(n, bank=4):
                act.wait_ge(ms_done, n + 1)
                act.activation(rstd[:, 0, :], ps[:, bank, 0:T], ACT.Sqrt, bias=epsc[:, :]).then_inc(std_done, 1)

            def split_hi(n, y, out, shift=None, between=None):
                for t in range(0, KT, 2):
                    act.wait_ge(y_done, KT * n + t + 2)
                    if shift is None:
                        ins = act.activation(out[:, t:t + 2, :], y[:, t * T:t * T + 2 * T], ACT.Copy)
                    else:
                        for m in (t, t + 1):
                            ins = act.activation(out[:, m, :], y[:, m * T:m * T + T], ACT.Identity, bias=shift(m))
                    ins.then_inc(xhi_done, 1)
                    if between:
                        between(t // 2)

            def mod_row(i, g, bank):
                act.wait_ge(slab_done, g + 1)
                if i >= 2:
                    act.wait_ge(modT_done, i - 1)
                act.activation(modrow[:, i % 2, :], ps[0:4, bank, 0:SLABC], ACT.Copy).then_inc(row_done, 1)

            def ada_row(use, first, k):
                hi(Slab(BASE[use] + k + RING))
                mod_row(N_ADA + first + k, BASE[use] + k, k % 2)

            def glu(q, j, g):
                act.wait_ge(slab_done, g + 1)
                if j >= 2:
                    act.wait_ge(v_done, 4 * q + j - 1)
                for m in range(2):
                    ins = act.activation(cva[:, j % 2, m, :], ps[:, 2 * (j % 2) + 1, m * T:m * T + T], ACT.Sigmoid,
                                         bias=col("pw1_b", KT + 2 * j + m))
                ins.then_inc(sg_done, 1)

            def ln_squares(q):
                act.wait_ge(cen_done, q + 1)
                for i in range(2):
                    act.activation(ctx_sq[:, 1024 * i:1024 * i + 1024], acc[:, 4 * i:4 * i + 4, :], ACT.Square).then_inc(lsq_done, 1)

            def ln_root(q):
                act.wait_ge(var_done, q + 1)
                act.activation(lstd[:, 0, :], ps[:, 2, 0:T], ACT.Sqrt, bias=epsc[:, :]).then_inc(lstd_done, 1)

            def ln_silu(q, out):
                act.wait_ge(lnorm_done, q + 1)
                for t in range(KT):
                    act.activation(ctx_sq[:, t * T:t * T + T], acc[:, t, :], ACT.Silu,
                                   scale=col("ln_g", t), bias=col("ln_b", t)).then_inc(act_done, 1)
                for t in range(0, KT, 2):
                    act.wait_ge(act_done, KT * q + t + 2)
                    act.activation(out[:, t:t + 2, :], ctx_sq[:, t * T:t * T + 2 * T], ACT.Copy).then_inc(chi_done, 1)

            act.wait_ge(s_memset, 3)
            act.wait_ge(s_x, 16)
            squares(xlat, bufB)
            act.wait_ge(s_cols, 16)
            act.activation(tiny[:, 0:16], cols[:, COL["cond"][0]:COL["cond"][0] + 2 * KT], ACT.Silu).then_inc(cond_f, 1)
            act.wait_ge(cond_f, 1)
            act.wait_ge(cond_zero, 1)
            cnd4 = cnd[:, 0:4 * KT].rearrange("p (k f) -> p k f", f=4)
            for s in range(2):
                act.activation(cnd4[:, :, 2 * s], tiny[:, 8 * s:8 * s + 8], ACT.Copy).then_inc(cond_hi, 1)
            hi(Slab(0))
            root(0)
            hi(Slab(1))
            split_hi(0, bufA, h_hi)
            hi(Slab(2))

            def drain(n, out, func=ACT.Copy, scale=1.0, rows=P):
                bank = ps[0:rows, n % 4, 0:out.shape[-1] if len(out.shape) == 2 else 512]
                act.activation(out, bank, func, scale=scale).then_inc(mix_drained, 1)

            for n, (kind, g) in enumerate(LEAD):
                hi(Slab(n + RING))
                if kind == "ada":
                    mod_row(g, n, n % 4)
                    continue
                act.wait_ge(slab_done, n + 1)
                if g == 0:
                    drain(n, alr[0:RANK, :], rows=RANK)
                elif g < 3:
                    drain(n, ka[:, 2 * (g - 1):2 * g, :])
                elif g < 5:
                    drain(n, qa[:, 2 * (g - 3):2 * (g - 3) + 2, :], scale=DK ** -0.5)
                elif g < 9:
                    drain(n, va[:, :, (g - 5) * SLABC:(g - 4) * SLABC])
                elif g < 11:
                    drain(n, mqk[:, 1, 2 * (g - 9):2 * (g - 9) + 2, :])
                elif g < 13:
                    drain(n, mqk[:, 0, 2 * (g - 11):2 * (g - 11) + 2, :], scale=DH ** -0.5)
                elif g < 15:
                    drain(n, mv[:, :, (g - 13) * SLABC:(g - 12) * SLABC])
                elif g < 19:
                    if g == 15:
                        act.wait_ge(tab_done, 1)
                    drain(n, sra[:, 2 * (g - 15):2 * (g - 15) + 2, :], ACT.Silu)
                else:
                    if g == 19:
                        act.wait_ge(o_done, 1)
                    drain(n, gates[:, 2 * (g - 19):2 * (g - 19) + 2, :], ACT.Sigmoid)
                if g == 2:
                    act.wait_ge(z_done, 1)
                    lz = bufB[:, 0:1024]
                    order.mark(act.activation(lz, ps[:, 4:6, :], ACT.Abs))
                    act.wait_ge(act_order, order.value())
                    order.mark(act.activation(lz, lz, ACT.Exp, scale=-1.0))
                    act.wait_ge(act_order, order.value())
                    act.activation(lz, lz, ACT.Ln, bias=1.0).then_inc(la_done, 1)
                if g == 4:
                    act.wait_ge(blast, 2)
                    act.activation(bufA[:, 0:1024], ps[:, 6:8, :], ACT.Exp).then_inc(exps_done, 1)
                    act.activation(bufA[:, 1024:2048], ps[:, 6:8, :], ACT.Exp, scale=-1.0).then_inc(exps_done, 1)
                    act.activation(tiny[:, 16:32], tiny[:, 0:16], ACT.Exp).then_inc(exps_done, 1)
                    act.activation(bufB[:, 0:1024], bufB[:, 0:1024], ACT.Exp).then_inc(exps_done, 1)
                if g == 8:
                    act.wait_ge(attn_done, 1)
                    act.activation(bufA[:, 0:1024], ps[:, 4:6, :], ACT.Copy).then_inc(attn_sb, 1)
                    act.wait_ge(kteT_done, 1)
                    act.activation(bufB[:, 1024:2048], ps[:, 6:8, :], ACT.Copy).then_inc(kteT_sb, 1)
                if g == 13:
                    act.wait_ge(o_done, 1)
                    act.activation(bufB[:, :], ps[:, 4:8, :], ACT.Square).then_inc(o_sq, 1)
                if g == 14:
                    act.wait_ge(oms_done, 1)
                    act.activation(bufB[:, 0:1024], ps[:, 4:6, :], ACT.Sqrt, bias=epsc[:, :], scale=D / DV).then_inc(ostd_done, 1)
                if g == 19:
                    for i in range(2):
                        act.wait_ge(oa_done, KT)
                        act.activation(g_hi[:, 4 * i:4 * i + 4, :], bufA[:, 1024 * i:1024 * i + 1024], ACT.Copy)\
                           .then_inc(oahi_done, 1)
                if g in (17, 20, 23):
                    act.wait_ge(sub_done, (g - 17) // 3 + 1)
                    act.activation(state[:, 0, :, :], state[:, 0, :, :], ACT.Exp).then_inc(e_done, 1)
                if g in (18, 21, 24):
                    r = (g - 18) // 3
                    act.wait_ge(pt_done, r + 1)
                    if r == 2:
                        act.wait_ge(modT_done, N_ADA)
                    act.activation(pt_of(r), ps[:, 6:8, :], ACT.Copy).then_inc(pt_sb, 1)
            act.wait_ge(ob_done, 1)
            act.activation(m_hi[:, :, :, :], ps[:, 4:6, :], ACT.Copy).then_inc(obhi_done, 1)

            b0 = BASE["moba"]
            hi(Slab(b0 + RING))
            act.wait_ge(s_ctx, 16)
            squares(xctx, ctx_sq)
            hi(Slab(b0 + 1 + RING))
            b0 = BASE["gla"]
            hi(Slab(b0 + RING))
            root(1)
            hi(Slab(b0 + 1 + RING))
            act.wait_ge(slab_done, AT["mix", N_MIX - 1] + 1)
            split_hi(1, ctx_y, h_hi, shift_of(0, 0, 1))
            hi(Slab(b0 + 2 + RING))
            hi(Slab(b0 + 3 + RING))
            b0 = BASE["pw1_ctx_a"]
            hi(Slab(b0 + RING))
            act.wait_ge(slab_done, BASE["gla"] + 4)
            for k in range(4):
                act.wait_ge(mixed_done, k + 1)
                act.activation(g_hi[:, 2 * k:2 * k + 2, :], bufA[:, 512 * k:512 * k + 512], ACT.Copy).then_inc(mxhi_done, 1)
            hi(Slab(b0 + 1 + RING))
            glu(0, 0, b0 + 1)
            for i in range(4):
                hi(Slab(BASE["out"] + i + RING))

            def pw1_act(q, b1, n, x, sq, y, out, shift, ready):
                hi(Slab(b1 + RING))
                act.wait_ge(*ready)
                squares(x, sq)
                hi(Slab(b1 + 1 + RING))
                glu(q, 1, b1 + 1)
                root(n)
                hi(Slab(b1 + 2 + RING))
                split_hi(n, y, out, shift)
                hi(Slab(b1 + 3 + RING))
                glu(q, 2, b1 + 3)
                hi(Slab(b1 + 4 + RING))
                hi(Slab(b1 + 5 + RING))
                glu(q, 3, b1 + 5)

            pw1_act(0, BASE["pw1_ctx_b"], 2, xlat, bufB, bufA, g_hi, None, (x_ready, 4))
            ffn_act(act, hi, 0, "ffn0")

            act.wait_ge(x_ready, 8)
            squares(xlat, bufB)
            ln_squares(0)
            root(3)
            for k in range(3):
                ada_row("ada_a", 0, k)
            ln_root(0)
            act.wait_ge(y_done, KT * 4)
            squares(xlat, bufB)
            for k in range(3, 6):
                ada_row("ada_a", 0, k)
            ln_silu(0, g_hi)
            root(4)
            split_hi(4, bufA, h_hi, shift_of(0, 0, 0))
            for i in range(4):
                hi(Slab(BASE["pw2_ctx"] + i + RING))
            b0 = BASE["pw1_lat"]
            hi(Slab(b0 + RING))
            hi(Slab(b0 + 1 + RING))
            glu(1, 0, b0 + 1)
            pw1_act(1, b0 + 2, 5, xctx, ctx_sq, ctx_y, g_hi, shift_of(0, 3, 1), (x_ready, 12))
            ffn_act(act, hi, 1, "ffn_ctx")

            ln_squares(1)
            for k in range(3):
                ada_row("ada_b", 6, k)
            ln_root(1)
            for k in range(3, 6):
                ada_row("ada_b", 6, k)
            ln_silu(1, h_hi)
            for i in range(4):
                hi(Slab(BASE["pw2_lat"] + i + RING))
            act.wait_ge(x_ready, 20)
            squares(xlat, bufB)
            squares(xctx, ctx_sq)
            root(6)
            for k in range(2):
                ada_row("ada_c", 12, k)
            split_hi(6, bufA, g_hi, shift_of(0, 3, 0), between=lambda k: ada_row("ada_c", 12, 2 + k))
            root(7, bank=5)
            split_hi(7, ctx_y, h_hi, shift_of(1, 0, 1))
            act.wait_ge(modT_done, N_ADA + 18)
            ffn_act(act, hi, 2, "ffn_lat")

            act.wait_ge(x_ready, 24)
            squares(xlat, bufB)
            for k in range(2):
                ada_row("ada_d", 18, k)
            root(8)
            for k in range(2, 6):
                ada_row("ada_d", 18, k)
            split_hi(8, bufA, g_hi, shift_of(1, 0, 0))

            b0 = BASE["qkv"]
            for i in range(6):
                hi(Slab(b0 + i + RING))
                act.wait_ge(slab_done, b0 + i + 1)
                if i == 0:
                    act.activation(k_raw, ps[:, 0, :], ACT.Copy).then_inc(kv_sb, 1)
                    act.activation(k_all[:, :, T:2 * T], ps[:, 1, :].rearrange("p (a t) -> p a t", a=2), ACT.Copy).then_inc(kv_sb, 1)
                elif i == 1:
                    act.activation(v_all, ps[:, 2:4, :], ACT.Copy).then_inc(kv_sb, 1)
                else:
                    act.activation(q_raw[:, 2 * (i - 2):2 * (i - 2) + 2, :], ps[:, i - 2, :], ACT.Copy, scale=DH ** -0.5).then_inc(q_sb, 1)

            def turned(n):
                b = n % 2
                act.wait_ge(wt_done, n + 1)
                if n >= 2:
                    act.wait_ge(wo_done, n - 1)
                act.activation(bufB[:, 1024 * b:1024 * b + 1024], ps[:, 4:6, :], ACT.Copy).then_inc(wt_sb, 1)
                if n % 2:
                    act.wait_ge(wo_done, n + 1)
                    i = n // 2
                    act.activation(h_hi[:, i, :], ps[:, 6 + i % 2, 0:T], ACT.Copy).then_inc(wohi_done, 1)

            for n in range(H2):
                b = n % 2
                pr = bufA[:, 1024 * b:1024 * b + 1024].rearrange("p (s k) -> p s k", s=2)
                act.wait_ge(wmax_done, n + 1)
                if n >= 2:
                    act.wait_ge(wt_done, n - 1)
                for s in range(2):
                    act.activation(pr[:, s, :], ps[:, 2 * b + s, :], ACT.Exp, bias=tiny[:, 8 * b + 2 + s:8 * b + 3 + s],
                                   accum_out=tiny[:, 16 + 8 * b + s:17 + 8 * b + s])
                act.activation(tiny[:, 18 + 8 * b:20 + 8 * b], tiny[:, 8 * b + 4:8 * b + 6], ACT.Exp).then_inc(we_done, 1)
                if n >= 1:
                    turned(n - 1)
            turned(H2 - 1)
            for i in range(4):
                hi(Slab(BASE["wo"] + i + RING))
            act.wait_ge(x_ready, 28)
            squares(xlat, bufB)
            root(9)
            split_hi(9, bufA, g_hi, shift_of(1, 3, 0))
            ffn_act(act, hi, 3, "ffn2")
            act.wait_ge(x_ready, 32)
            squares(xlat, bufB)
            root(10)

        @block.vector
        def _(dve):
            order = Tally(dve_order)

            def lo(g):
                if isinstance(g.j, int) and g.c >= TOTAL:
                    return
                part = slice(0, SLAB - pool_words(use_of(g.c)))
                dve.wait_ge(hi_done, g.number() + 1)
                dve.tensor_tensor(wlo[:, g.slot, part], raw[:, g.slot, part], whi[:, g.slot, part].bitcast(F32), ALU.subtract)\
                   .then_inc(lo_done, 1)

            def scale(n, x, gains, y):
                dve.wait_ge(std_done, n + 1)
                order.mark(dve.reciprocal(rstd[:, 1, :], rstd[:, 0, :]))
                dve.wait_ge(dve_order, order.value())
                for t in range(KT):
                    dve.scalar_tensor_tensor(y[:, t * T:t * T + T], x[:, t, :], gains(t), rstd[:, 1, :],
                                             ALU.mult, ALU.mult).then_inc(y_done, 1)

            def split_lo(i, y, out, shift=None, between=None):
                for t in range(0, KT, 2):
                    dve.wait_ge(xhi_done, KT // 2 * i + t // 2 + 1)
                    if shift is None:
                        ins = dve.tensor_tensor(out[1][:, t:t + 2, :], y[:, t * T:t * T + 2 * T],
                                                out[0][:, t:t + 2, :].bitcast(F32), ALU.subtract)
                    else:
                        for m in (t, t + 1):
                            ins = dve.scalar_tensor_tensor(out[1][:, m, :], y[:, m * T:m * T + T], shift(m),
                                                           out[0][:, m, :].bitcast(F32), ALU.add, ALU.subtract)
                    ins.then_inc(xlo_done, 1)
                    if between:
                        between(t // 2)

            def mod_add(i, bank):
                layer, k = i // N_ADA, i % N_ADA
                c0 = COL[f"ada_b{layer}"][0] + 2 * k
                dve.wait_ge(modT_done, i + 1)
                dve.tensor_tensor(mod[:, layer, 2 * k:2 * k + 2, :], ps[:, bank, T:T + 4].rearrange("p (a s) -> p a s", s=2),
                                  cols[:, c0:c0 + 2, None].to_broadcast([P, 2, 2]), ALU.add).then_inc(mod_done, 1)

            def ada_add(use, first, k):
                lo(Slab(BASE[use] + k + RING))
                mod_add(N_ADA + first + k, k % 2)

            def modulated(i0, i1, ready):
                dve.wait_ge(mod_done, ready)
                for i in range(i0, i1):
                    layer, which, s, gain = MODULATED[i]
                    dve.scalar_tensor_tensor(amod[:, i, :], mod[:, layer, which * KT:which * KT + KT, s], 1.0,
                                             cols[:, COL[gain][0]:COL[gain][0] + KT], ALU.add, ALU.mult).then_inc(amod_done, 1)
                dve.wait_ge(amod_done, i1)

            def glu(q, j):
                dve.wait_ge(sg_done, 4 * q + j + 1)
                for m in range(2):
                    ins = dve.scalar_tensor_tensor(vpad[:, 2 * j + m, PADC:PADC + T], ps[:, 2 * (j % 2), m * T:m * T + T],
                                                   col("pw1_b", 2 * j + m), cva[:, j % 2, m, :], ALU.add, ALU.mult)
                ins.then_inc(v_done, 1)

            def pw1_dve(q, b1, n, i, x, gains, y, out, shift):
                lo(Slab(b1 + RING))
                lo(Slab(b1 + 1 + RING))
                glu(q, 1)
                scale(n, x, gains, y)
                lo(Slab(b1 + 2 + RING))
                split_lo(i, y, out, shift)
                lo(Slab(b1 + 3 + RING))
                glu(q, 2)
                lo(Slab(b1 + 4 + RING))
                lo(Slab(b1 + 5 + RING))
                glu(q, 3)

            def dwconv_first(q):
                dve.wait_ge(v_done, 4 * q + 4)
                dve.wait_ge(pads_done, 2)
                for t in range(KT):
                    order.mark(dve.tensor_scalar(acc[:, t, :], vpad[:, t, 0:T], col("dw_w", t), col("dw_b", t), ALU.mult, ALU.add))

            def dwconv(j, k):
                dve.wait_ge(dve_order, order.value())
                for t in range(KT):
                    w = cols[:, bass.ds(3 * KT * j + (COL["dw_w"][0] + KT * (k - 2) + t), 1)]
                    order.mark(dve.scalar_tensor_tensor(acc[:, t, :], vpad[:, t, bass.ds(3 * j + (k - 2), T)], w, acc[:, t, :],
                                                        ALU.mult, ALU.add))

            def wide(a):
                return a[:, None, :].to_broadcast([P, KT, T])

            def dwconv_end():
                dve.wait_ge(dve_order, order.value())
                dve.sem_inc(dw_done, 1)

            def ln_centre(q):
                dve.wait_ge(mu_done, q + 1)
                dve.tensor_tensor(acc[:, :, :], acc[:, :, :], wide(ps[:, 2, 0:T]), ALU.subtract).then_inc(cen_done, 1)

            def ln_scale(q):
                dve.wait_ge(lstd_done, q + 1)
                order.mark(dve.reciprocal(lstd[:, 1, :], lstd[:, 0, :]))
                dve.wait_ge(dve_order, order.value())
                dve.tensor_tensor(acc[:, :, :], acc[:, :, :], wide(lstd[:, 1, :]), ALU.mult).then_inc(lnorm_done, 1)

            def ln_lo(q, out):
                for t in range(0, KT, 2):
                    dve.wait_ge(chi_done, 4 * q + t // 2 + 1)
                    dve.tensor_tensor(out[1][:, t:t + 2, :], ctx_sq[:, t * T:t * T + 2 * T], out[0][:, t:t + 2, :].bitcast(F32),
                                      ALU.subtract).then_inc(clo_done, 1)

            def pw2_dve(use, x, gate):
                for i in range(4):
                    lo(Slab(BASE[use] + i + RING))
                    dve.wait_ge(slab_done, BASE[use] + i + 1)
                    for m in range(2):
                        t = 2 * i + m
                        order.mark(dve.tensor_scalar(bufA[:, t * T:t * T + T], ps[:, i, m * T:m * T + T], col("pw2_b", t), gate(t),
                                                     ALU.add, ALU.mult))
                    dve.wait_ge(dve_order, order.value())
                    dve.tensor_tensor(x[:, 2 * i:2 * i + 2, :], x[:, 2 * i:2 * i + 2, :], bufA[:, 512 * i:512 * i + 512], ALU.add)\
                       .then_inc(x_ready, 1)

            def gated_residual(use, x, gate):
                dve.wait_ge(slab_done, BASE[use] + 3 * NJ)
                for t in range(KT):
                    ins = dve.scalar_tensor_tensor(x[:, t, :], ps[:, 4 + t // 2, (t % 2) * T:(t % 2) * T + T], gate(t), x[:, t, :],
                                                   ALU.mult, ALU.add)
                    if t % 2:
                        ins.then_inc(x_ready, 1)

            H, G = (h_hi, h_lo), (g_hi, g_lo)
            dve.memset(cnd[:, :].bitcast(F32), 0.0).then_inc(cond_zero, 1)
            dve.memset(relb[BUCKETS:BUCKETS + 1, :], NEG).then_inc(s_relb, 1)
            cnd4 = cnd[:, 0:4 * KT].rearrange("p (k f) -> p k f", f=4)
            dve.wait_ge(cond_hi, 2)
            for s in range(2):
                dve.tensor_tensor(cnd4[:, :, 2 * s + 1], tiny[:, 8 * s:8 * s + 8], cnd4[:, :, 2 * s].bitcast(F32), ALU.subtract)\
                   .then_inc(cond_lo, 1)
            lo(Slab(0))
            scale(0, xlat, lambda t: col("norm_mix", t), bufA)
            lo(Slab(1))
            split_lo(0, bufA, H)
            lo(Slab(2))
            dve.wait_ge(tab_done, 1)
            dve.tensor_copy(state[0:H_MOBA, 0, 0:2, :], ps[0:H_MOBA, 5, :]).then_inc(tab_sb, 1)

            E1, E2, E3 = bufA[:, 0:1024], bufA[:, 1024:2048], bufB[:, 0:1024]
            heads = lambda a: a.rearrange("p (h t) -> p h t", t=T)
            for n, (kind, g) in enumerate(LEAD):
                lo(Slab(n + RING))
                if n and LEAD[n - 1][0] == "ada":
                    mod_add(LEAD[n - 1][1], (n - 1) % 4)
                if kind == "ada":
                    continue
                if g == 2:
                    dve.wait_ge(la_done, 1)
                    dve.scalar_tensor_tensor(bufB[:, 1024:2048], flat(ps[:, 4:6, :]), 0.0, bufB[:, 0:1024],
                                             ALU.min, ALU.subtract).then_inc(la_done, 1)
                if g == 4:
                    dve.wait_ge(b_done, 1)
                    bT = ps[:, 6:8, :].rearrange("p a (h c i) -> p (a h c) i", h=2, c=NCH)
                    dve.tensor_copy(tiny[:, 0:16], bT[:, :, CHUNK - 1]).then_inc(blast, 1)
                    dve.wait_ge(blast, 1)
                    dve.scalar_tensor_tensor(E3.rearrange("p (c i) -> p c i", i=CHUNK), bT, -1.0,
                                             tiny[:, 0:16, None].to_broadcast([P, 16, CHUNK]),
                                             ALU.mult, ALU.add).then_inc(blast, 1)
                    dve.wait_ge(exps_done, 1)
                    dve.tensor_tensor(qa, qa, heads(E1), ALU.mult).then_inc(dec_done, 1)
                    dve.wait_ge(exps_done, 2)
                    dve.tensor_tensor(heads(E2), ka, heads(E2), ALU.mult).then_inc(dec_done, 1)
                    dve.wait_ge(exps_done, 4)
                    dve.tensor_tensor(heads(E3), ka, heads(E3), ALU.mult).then_inc(dec_done, 1)
                if g == 10:
                    dve.wait_ge(tab_out, 16)
                    dve.wait_ge(kv_done, 1)
                    dve.tensor_copy(ka, ps[:, 4:6, :].rearrange("p a (h v) -> p (a h) v", v=DV)).then_inc(state_done, 1)
                    dve.wait_ge(state_done, 1)
                    for c in (1, 2):
                        if c == 2:
                            dve.wait_ge(kv_done, 2)
                        for h in range(H_GLA):
                            prev = ka[:, h, :] if c == 1 else state[:, 0, h, :]
                            bank = (6 if c == 1 else 4) + h // 2
                            if c == 2:
                                dve.wait_ge(state_done, 2 + h)
                            dec = 16 + h * NCH + c
                            dve.scalar_tensor_tensor(state[:, c - 1, h, :], prev, tiny[:, dec:dec + 1],
                                                     ps[:, bank, (h % 2) * DV:(h % 2) * DV + DV], ALU.mult, ALU.add)\
                               .then_inc(state_done, 1)
                if g == 13:
                    dve.wait_ge(o_sq, 1)
                    dve.tensor_copy(bufA[:, :], flat(ps[:, 4:8, :])).then_inc(o_sb, 1)
                if g == 14:
                    dve.wait_ge(ostd_done, 1)
                    order.mark(dve.reciprocal(bufB[:, 0:1024], bufB[:, 0:1024]))
                    dve.wait_ge(dve_order, order.value())
                    dve.wait_ge(o_sb, 1)
                    o = bufA[:, :].rearrange("p (h d t) -> p h d t", h=H_GLA, d=2)
                    order.mark(dve.tensor_tensor(
                        o, o, heads(bufB[:, 0:1024])[:, :, None, :].to_broadcast([P, H_GLA, 2, T]), ALU.mult))
                if g == 18:
                    dve.wait_ge(dve_order, order.value())
                    dve.wait_ge(mix_drained, 19)
                    for t in range(KT):
                        o = bufA[:, t * T:t * T + T]
                        dve.scalar_tensor_tensor(o, o, col("gla_out_norm", t), sra[:, t, :], ALU.mult, ALU.mult)\
                           .then_inc(oa_done, 1)
                if g == 19:
                    for i in range(2):
                        dve.wait_ge(oahi_done, i + 1)
                        dve.tensor_tensor(g_lo[:, 4 * i:4 * i + 4, :], bufA[:, 1024 * i:1024 * i + 1024],
                                          g_hi[:, 4 * i:4 * i + 4, :].bitcast(F32), ALU.subtract).then_inc(oalo_done, 1)
                if g in (16, 19, 22):
                    r = (g - 16) // 3
                    nb = 8 if r == 0 else 4
                    sc = ps[:, 4:6, :].rearrange("p a (h k) -> p (a h) k", h=nb // 2)
                    pr = flat(state[:, 0, :, :]).rearrange("p (h k) -> p h k", h=nb)
                    dve.wait_ge(sc_done, r + 1)
                    order.mark(dve.tensor_reduce(tiny[:, 32:32 + nb], sc, AX.X, ALU.max))
                    dve.wait_ge(dve_order, order.value())
                    if r:
                        dve.wait_ge(pt_done, r)
                    dve.tensor_tensor(pr, sc, tiny[:, 32:32 + nb, None].to_broadcast([P, nb, 1024 // nb]), ALU.subtract)\
                       .then_inc(sub_done, 1)
                if g in (17, 20, 23):
                    dve.wait_ge(e_done, r + 1)
                    order.mark(dve.tensor_reduce(tiny[:, 40:40 + nb], pr, AX.X, ALU.add))
                    dve.wait_ge(dve_order, order.value())
                    order.mark(dve.reciprocal(tiny[:, 48:48 + nb], tiny[:, 40:40 + nb]))
                    dve.wait_ge(dve_order, order.value())
                    dve.tensor_tensor(pr, pr, tiny[:, 48:48 + nb, None].to_broadcast([P, nb, 1024 // nb]), ALU.mult)\
                       .then_inc(p_done, 1)
                if g == 25:
                    modulated(0, 4, N_ADA)
            dve.wait_ge(obhi_done, 1)
            dve.tensor_tensor(flat(m_lo[:, :, :, :]), flat(ps[:, 4:6, :]), flat(m_hi[:, :, :, :].bitcast(F32)), ALU.subtract)\
               .then_inc(oblo_done, 1)

            for i in range(2):
                lo(Slab(BASE["moba"] + i + RING))
                dve.wait_ge(slab_done, BASE["moba"] + i + 1)
                dve.wait_ge(mix_drained, N_MIX)
                dve.tensor_tensor(bufB[:, 1024 * i:1024 * i + 1024], flat(ps[:, 2 * i:2 * i + 2, :]),
                                  flat(gates[:, KT + 4 * i:KT + 4 * i + 4, :]), ALU.mult).then_inc(br_drained, 1)
            scale(1, xctx, gain_of(0), ctx_y)
            for k in range(4):
                lo(Slab(BASE["gla"] + k + RING))
                dve.wait_ge(slab_done, BASE["gla"] + k + 1)
                mix = bufA[:, 512 * k:512 * k + 512]
                dve.tensor_tensor(mix, ps[:, k, :], flat(gates[:, 2 * k:2 * k + 2, :]), ALU.mult).then_inc(br_drained, 1)
                dve.wait_ge(br_drained, k + 3)
                dve.tensor_tensor(mix, mix, bufB[:, 512 * k:512 * k + 512], ALU.add).then_inc(mixed_done, 1)
                if k == 1:
                    split_lo(1, ctx_y, H, shift_of(0, 0, 1))
            dve.memset(vpad[:, :, 0:PADC], 0.0).then_inc(pads_done, 1)
            dve.memset(vpad[:, :, PADC + T:VP], 0.0).then_inc(pads_done, 1)
            b0 = BASE["pw1_ctx_a"]
            lo(Slab(b0 + RING))
            for k in range(4):
                dve.wait_ge(mxhi_done, k + 1)
                dve.tensor_tensor(flat(g_lo[:, 2 * k:2 * k + 2, :]), bufA[:, 512 * k:512 * k + 512],
                                  flat(g_hi[:, 2 * k:2 * k + 2, :].bitcast(F32)), ALU.subtract).then_inc(mxlo_done, 1)
            lo(Slab(b0 + 1 + RING))
            glu(0, 0)
            for k in range(4):
                lo(Slab(BASE["out"] + k + RING))
                dve.wait_ge(slab_done, BASE["out"] + k + 1)
                x = flat(xlat[:, 2 * k:2 * k + 2, :])
                dve.tensor_tensor(x, ps[:, 4 + k, :], x, ALU.add).then_inc(x_ready, 1)
            pw1_dve(0, BASE["pw1_ctx_b"], 2, 2, xlat, lambda t: col("norm_ffn", t), bufA, G, None)

            dwconv_first(0)
            ffn_dve(dve, lo, order, 0, "ffn0", dwconv)
            dwconv_end()
            dve.wait_ge(slab_done, BASE["ffn0"] + 3 * NJ)
            for q in range(4):
                x = flat(xlat[:, 2 * q:2 * q + 2, :])
                dve.tensor_tensor(x, ps[:, 4 + q, :], x, ALU.add).then_inc(x_ready, 1)
            ln_centre(0)
            scale(3, xlat, lambda t: col("norm_final", t), flat(xlat[:, :, :]))
            for k in range(3):
                ada_add("ada_a", 0, k)
            ln_scale(0)
            for k in range(3, 6):
                ada_add("ada_a", 0, k)
            ln_lo(0, G)
            scale(4, xlat, gain_of(2), bufA)
            split_lo(3, bufA, H, shift_of(0, 0, 0))
            dve.wait_ge(xlo_done, KT // 2 * 4)
            pw2_dve("pw2_ctx", xctx, shift_of(0, 2, 1))
            b0 = BASE["pw1_lat"]
            lo(Slab(b0 + RING))
            lo(Slab(b0 + 1 + RING))
            glu(1, 0)
            pw1_dve(1, b0 + 2, 5, 4, xctx, gain_of(1), ctx_y, G, shift_of(0, 3, 1))

            dwconv_first(1)
            ffn_dve(dve, lo, order, 1, "ffn_ctx", dwconv)
            dwconv_end()
            ln_centre(1)
            gated_residual("ffn_ctx", xctx, shift_of(0, 5, 1))
            for k in range(3):
                ada_add("ada_b", 6, k)
            ln_scale(1)
            for k in range(3, 6):
                ada_add("ada_b", 6, k)
            ln_lo(1, H)
            modulated(4, 6, N_ADA + 12)
            pw2_dve("pw2_lat", xlat, shift_of(0, 2, 0))
            scale(6, xlat, gain_of(3), bufA)
            for k in range(2):
                ada_add("ada_c", 12, k)
            split_lo(5, bufA, G, shift_of(0, 3, 0), between=lambda k: ada_add("ada_c", 12, 2 + k))
            scale(7, xctx, gain_of(4), ctx_y)
            split_lo(6, ctx_y, H, shift_of(1, 0, 1))
            ffn_dve(dve, lo, order, 2, "ffn_lat")
            gated_residual("ffn_lat", xlat, shift_of(0, 5, 0))
            for k in range(2):
                ada_add("ada_d", 18, k)
            scale(8, xlat, gain_of(5), bufA)
            for k in range(2, 6):
                ada_add("ada_d", 18, k)
            split_lo(7, bufA, G, shift_of(1, 0, 0))
            modulated(6, 7, 2 * N_ADA)

            b0 = BASE["qkv"]
            cos, sin = (rope_cs[:, i:i + 1, :].to_broadcast([P, 2, T]) for i in range(2))

            def rope(out, raw_, bank, done):
                order.mark(dve.tensor_tensor(out, ps[:, bank, :].rearrange("p (a t) -> p a t", a=2), sin, ALU.mult))
                order.mark(dve.tensor_tensor(raw_, raw_, cos, ALU.mult))
                dve.wait_ge(dve_order, order.value())
                dve.tensor_tensor(out, out, raw_, ALU.add).then_inc(done, 1)

            dve.wait_ge(s_late, 16)
            for i in range(6):
                lo(Slab(b0 + i + RING))
                if i == 1:
                    dve.wait_ge(krot_done, 1)
                    rope(k_all[:, :, 0:T], k_raw, 4, k_ready)
                if i >= 3:
                    dve.wait_ge(qrot_done, i - 2)
                    rope(q_rot[:, 2 * (i - 3):2 * (i - 3) + 2, :], q_raw[:, 2 * (i - 3):2 * (i - 3) + 2, :], 4 + (i - 2) % 4, q_ready)
            dve.wait_ge(qrot_done, 4)
            rope(q_rot[:, 6:8, :], q_raw[:, 6:8, :], 4, q_ready)

            def probs(n):
                b = n % 2
                c = 16 + 8 * b
                dve.wait_ge(we_done, n + 1)
                order.mark(dve.tensor_tensor(tiny[:, c + 4:c + 6], tiny[:, c:c + 2], tiny[:, c + 2:c + 4], ALU.add))
                dve.wait_ge(dve_order, order.value())
                order.mark(dve.reciprocal(tiny[:, c + 6:c + 8], tiny[:, c + 4:c + 6]))
                dve.wait_ge(dve_order, order.value())
                for s in range(2):
                    pr = bufA[:, 1024 * b + 512 * s:1024 * b + 512 * s + 512]
                    ins = dve.tensor_scalar(pr, pr, tiny[:, c + 6 + s:c + 7 + s], None, ALU.mult)
                ins.then_inc(wp_done, 1)

            def out_lo(i):
                dve.wait_ge(wohi_done, i + 1)
                dve.tensor_tensor(h_lo[:, i, :], ps[:, 6 + i % 2, 0:T], h_hi[:, i, :].bitcast(F32), ALU.subtract).then_inc(wolo_done, 1)

            for n in range(H2):
                b = n % 2
                c = 8 * b
                dve.wait_ge(ws_done, n + 1)
                if n >= 2:
                    dve.wait_ge(we_done, n - 1)
                order.mark(dve.tensor_reduce(tiny[:, c:c + 2], ps[:, 2 * b:2 * b + 2, :], AX.X, ALU.max))
                dve.wait_ge(dve_order, order.value())
                sink = col("sink", n)
                order.mark(dve.tensor_scalar(tiny[:, c + 2:c + 4], tiny[:, c:c + 2], sink, -1.0, ALU.max, ALU.mult))
                dve.wait_ge(dve_order, order.value())
                dve.tensor_scalar(tiny[:, c + 4:c + 6], tiny[:, c + 2:c + 4], sink, None, ALU.add).then_inc(wmax_done, 1)
                if n >= 1:
                    probs(n - 1)
                if n >= 4 and n % 2 == 0:
                    out_lo(n // 2 - 2)
            probs(H2 - 1)
            out_lo(6)
            out_lo(7)
            for i in range(4):
                lo(Slab(BASE["wo"] + i + RING))
                dve.wait_ge(slab_done, BASE["wo"] + i + 1)
                for m in range(2):
                    t = 2 * i + m
                    ins = dve.scalar_tensor_tensor(xlat[:, t, :], ps[:, i, m * T:m * T + T], mod[:, 1, 2 * KT + t, 0:1], xlat[:, t, :],
                                                   ALU.mult, ALU.add)
                ins.then_inc(x_ready, 1)
            scale(9, xlat, gain_of(6), bufA)
            split_lo(8, bufA, G, shift_of(1, 3, 0))
            ffn_dve(dve, lo, order, 3, "ffn2")
            gated_residual("ffn2", xlat, shift_of(1, 5, 0))
            scale(10, xlat, lambda t: col("final_g", t), flat(xlat[:, :, :]))
            dve.wait_ge(y_done, KT * 11)
            dve.sem_inc(out_ready, 1)

        @block.tensor
        def _(pe):
            def mm3(out, w, x, start=False, stop=False):
                pe.matmul(out, w[0], x[0], start=start, stop=False, skip_group_check=True)
                pe.matmul(out, w[0], x[1], start=False, stop=False, skip_group_check=True)
                return pe.matmul(out, w[1], x[0], start=False, stop=stop, skip_group_check=True)

            def weights(g, k):
                pe.wait_ge(lo_done, g.number() + 1)
                pe.wait_ge(lo2_done, g.number() + 1)
                return [a[:, g.slot, :].rearrange("p (k n) -> p k n", k=k) for a in (whi, wlo)]

            def features(g, bank, x, kts=KT, tiles=2, split=None):
                w = weights(g, kts)
                for m in range(tiles):
                    for k in range(kts):
                        if split is not None and m == 0 and k % 2 == 0:
                            pe.wait_ge(xlo_done, KT // 2 * split + k // 2 + 1)
                        ins = mm3(ps[:, bank + m // 2, (m % 2) * T:(m % 2) * T + T],
                                  [a[:, k, m * P:m * P + P] for a in w], [a[:, k, :] for a in x],
                                  start=(k == 0 and m % 2 == 0), stop=(k == kts - 1))
                ins.then_inc(slab_done, 1)

            def tokens(g, bank, x):
                w = weights(g, KT)
                for s in range(2):
                    for k in range(KT):
                        ins = mm3(ps[:, bank, s * T:s * T + T], [a[:, k, s * P:s * P + P] for a in x],
                                  [a[:, k, :] for a in w], start=(k == 0 and s == 0), stop=(k == KT - 1))
                ins.then_inc(slab_done, 1)

            def mean(x, bank, done, ready, first):
                for t in range(KT):
                    if t % 4 == 0:
                        pe.wait_ge(ready, first + (t // 4 if ready is not dw_done else 0) + 1)
                    ins = pe.matmul(ps[:, bank, 0:T], ones[:, :], x[:, t * T:t * T + T], start=(t == 0), stop=(t == KT - 1))
                ins.then_inc(done, 1)

            def means(n, sq, bank=4):
                mean(sq, bank, ms_done, sq_done, 2 * n)

            def ada(g, bank):
                w = weights(g, KT)
                for t in range(KT):
                    for part in range(2):
                        ins = pe.matmul(ps[:, bank, 0:SLABC], cnd[:, 4 * t:4 * t + P], w[part][:, t, :],
                                        start=(t == 0 and part == 0), stop=(t == KT - 1 and part == 1))
                ins.then_inc(slab_done, 1)

            def turn_row(i, bank):
                pe.wait_ge(row_done, i + 1)
                for m in range(2):
                    ins = pe.matmul(ps[:, bank, T + 2 * m:T + 2 * m + 2], modrow[:, i % 2, m * P:m * P + P], sel[:, :],
                                    start=(m == 0), stop=True, skip_group_check=True)
                ins.then_inc(modT_done, 1)

            def ada_group(use, first, k0, k1):
                for k in range(k0, k1):
                    i = N_ADA + first + k
                    if k >= 2:
                        pe.wait_ge(mod_done, i - 1)
                    ada(Slab(BASE[use] + k), k % 2)
                    if k > k0:
                        turn_row(i - 1, (k - 1) % 2)
                turn_row(i, k % 2)

            H, G = (h_hi, h_lo), (g_hi, g_lo)
            pe.wait_ge(s_memset, 3)
            means(0, bufB)
            pe.wait_ge(cond_lo, 2)

            for n, (kind, g) in enumerate(LEAD):
                if n >= 4:
                    was, i = LEAD[n - 4]
                    pe.wait_ge(*((mix_drained, i + 1) if was == "mix" else (mod_done, i + 1)))
                if kind == "ada":
                    ada(Slab(n), n % 4)
                elif 5 <= g < 9 or 13 <= g < 15:
                    tokens(Slab(n), n % 4, H)
                else:
                    features(Slab(n), n % 4, H, tiles=1 if g == 0 else 2, split=0 if g == 0 else None)
                if n == 0:
                    pe.wait_ge(s_relb, 1)
                    pe.wait_ge(s_small, 80)
                    pe.matmul(ps[0:H_MOBA, 5, :], relb[:, :], sra[0:BUCKETS + 1, 0:2, :], start=True, stop=True).then_inc(tab_done, 1)
                if n and LEAD[n - 1][0] == "ada":
                    turn_row(LEAD[n - 1][1], (n - 1) % 4)
                if kind == "ada":
                    continue
                if g == 2:
                    pe.wait_ge(mix_drained, 1)
                    pe.wait_ge(tab_sb, 1)
                    for s in range(2):
                        ins = pe.matmul(ps[:, 4 + s, :], alr[:, s * P:s * P + P], wlr, start=True, stop=True)
                    ins.then_inc(z_done, 1)
                if g == 4:
                    pe.wait_ge(s_consts, 16)
                    pe.wait_ge(la_done, 2)
                    for h in range(H_GLA):
                        for s in range(2):
                            la = bufB[:, 1024 + s * 512 + h * DK:1024 + s * 512 + h * DK + DK]
                            c = (h % 2) * T + s * P
                            ins = pe.matmul(ps[:, 6 + h // 2, c:c + P], la, cum, start=(h % 2 == 0 and s == 0),
                                            stop=True, skip_group_check=True)
                    ins.then_inc(b_done, 1)
                if g == 8:
                    pe.wait_ge(dec_done, 2)
                    for h in range(H_GLA):
                        for s in range(2):
                            a = h * 2 + s
                            ins = pe.matmul(ps[:, 4 + a // 4, (a % 4) * P:(a % 4) * P + P],
                                            bufA[:, 1024 + h * T + s * P:1024 + h * T + s * P + P],
                                            qa[:, h, s * P:s * P + P], start=(a % 4 == 0), stop=True, skip_group_check=True)
                    ins.then_inc(attn_done, 1)
                    pe.wait_ge(dec_done, 3)
                    for h in range(H_GLA):
                        for s in range(2):
                            ins = pe.transpose(ps[:, 6 + s, h * DK:h * DK + DK], bufB[:, h * T + s * P:h * T + s * P + P], eye)
                    ins.then_inc(kteT_done, 1)
                if g in (10, 11):
                    pe.wait_ge(attn_sb, 1)
                    pe.wait_ge(kteT_sb, 1)
                    if g == 11:
                        pe.wait_ge(state_done, 1)
                    for c in (0, 1) if g == 10 else (2,):
                        s, r0 = c // 2, (c % 2) * CHUNK
                        for h in range(H_GLA):
                            bank = (4, 6, 4)[c] + h // 2
                            k = bufB[r0:r0 + CHUNK, 1024 + s * 512 + h * DK:1024 + s * 512 + h * DK + DK]
                            ins = pe.matmul(ps[:, bank, (h % 2) * DV:(h % 2) * DV + DV], k,
                                            va[r0:r0 + CHUNK, s, h * DV:h * DV + DV],
                                            start=(h % 2 == 0), stop=True, skip_group_check=True)
                    ins.then_inc(kv_done, 1)
                if g == 12:
                    pe.wait_ge(attn_masked, 1)
                    pe.wait_ge(state_done, 9)
                    for h in range(H_GLA):
                        for d in range(2):
                            c = d * T
                            for s in range(2):
                                a = h * 2 + s
                                pe.matmul(ps[:, 4 + h, c + s * P:c + s * P + P],
                                          va[:, s, h * DV + d * P:h * DV + d * P + P], bufA[:, a * P:a * P + P],
                                          start=(d == 0 and s == 0), stop=False, skip_group_check=True)
                            for k in range(1, NCH):
                                S = ka[:, h, :] if k == 1 else state[:, k - 2, h, :]
                                ins = pe.matmul(ps[:, 4 + h, c + k * CHUNK:c + k * CHUNK + CHUNK], S[:, d * P:d * P + P],
                                                qa[:, h, k * CHUNK:k * CHUNK + CHUNK], start=False, stop=(k == NCH - 1),
                                                skip_group_check=True)
                    ins.then_inc(o_done, 1)
                if g == 14:
                    pe.wait_ge(o_sq, 1)
                    pe.wait_ge(o_sb, 1)
                    for h in range(H_GLA):
                        for d in range(2):
                            c = (h * 2 + d) * T
                            ins = pe.matmul(ps[:, 4 + h // 2, (h % 2) * T:(h % 2) * T + T], ones[:, :], bufB[:, c:c + T],
                                            start=(h % 2 == 0 and d == 0), stop=(d == 1), skip_group_check=True)
                    ins.then_inc(oms_done, 1)
                if g in (18, 21, 24):
                    r = (g - 18) // 3
                    pe.wait_ge(p_done, r + 1)
                    if r:
                        pe.wait_ge(pt_sb, r)
                    pr = flat(state[:, 0, :, :])
                    for a in range(8):
                        ins = pe.transpose(ps[:, 6 + a // 4, (a % 4) * P:(a % 4) * P + P], pr[:, a * P:a * P + P], eye)
                    ins.then_inc(pt_done, 1)
                if g in (15, 18, 21):
                    r = (g - 15) // 3
                    if r == 0:
                        pe.wait_ge(ostd_done, 1)
                        pe.wait_ge(brev_in, 16)
                        pe.wait_ge(mix_drained, 15)
                    else:
                        pe.wait_ge(sub_done, r)
                    nk = P if r == 0 else T
                    for h in range(8) if r == 0 else range(4 * r - 4, 4 * r):
                        i = place(h, r) * nk
                        out = ps[:, 4 + i // 512, i % 512:i % 512 + nk]
                        r0, q0 = (h % 2) * DH, 0 if r == 0 else P
                        pe.matmul(out, mqk[r0:r0 + DH, 0, h // 2, q0:q0 + P], mqk[r0:r0 + DH, 1, h // 2, 0:nk],
                                  start=(i % 512 == 0), stop=False, skip_group_check=True)
                        ins = pe.matmul(out, rev, brev[:, h, T - nk:T], start=False, stop=True, skip_group_check=True)
                    ins.then_inc(sc_done, 1)
                if g == 25:
                    pe.wait_ge(pt_sb, 3)
                    for h in range(H_MOBA):
                        r0, bank, c = (h % 2) * DH, 4 + h // 4, (h // 2 % 2) * T
                        for q in range(2):
                            out = ps[r0:r0 + DH, bank, c + q * P:c + q * P + P]
                            for k in range(q + 1):
                                a = place(h, 0) if q == 0 else place(h, 1) * 2 + k
                                pt = flat(pt_of(0) if q == 0 else pt_of(1 + h // 4))[:, a * P:a * P + P]
                                ins = pe.matmul(out, mv[:, k, h * DH:h * DH + DH], pt,
                                                start=(h % 4 < 2 and q == 0), stop=(k == q), skip_group_check=True)
                    ins.then_inc(ob_done, 1)

            M = [a[:, :, :, :].rearrange("p a b t -> p (a b) t") for a in (m_hi, m_lo)]
            pe.wait_ge(oblo_done, 1)
            pe.wait_ge(mix_drained, N_MIX)
            for i in range(2):
                features(Slab(BASE["moba"] + i), 2 * i, M, kts=4, tiles=4)
            means(1, ctx_sq)
            pe.wait_ge(oalo_done, 2)
            for i in range(4):
                pe.wait_ge(br_drained, 1 if i < 2 else 2)
                features(Slab(BASE["gla"] + i), i, G)
            pe.wait_ge(br_drained, 4)
            features(Slab(BASE["pw1_ctx_a"]), 0, H, split=1)
            features(Slab(BASE["pw1_ctx_a"] + 1), 1, H)
            pe.wait_ge(mxlo_done, 4)
            for i in range(4):
                features(Slab(BASE["out"] + i), 4 + i, G)

            def pw1_pe(q, b1, n, sq):
                for i in range(6):
                    if i >= 2:
                        pe.wait_ge(v_done, 4 * q + i // 2)
                    features(Slab(b1 + i), (2 + i) % 4, H)
                    if i == 1:
                        means(n, sq)

            pe.wait_ge(br_drained, 6)
            pw1_pe(0, BASE["pw1_ctx_b"], 2, bufB)
            ffn_pe(pe, features, mm3, 0, "ffn0", 2, [(v_done, 3), (v_done, 4)])

            acc_flat = flat(acc[:, :, :])
            mean(acc_flat, 2, mu_done, dw_done, 0)
            means(3, bufB)
            ada_group("ada_a", 0, 0, 3)
            mean(ctx_sq, 2, var_done, lsq_done, 0)
            ada_group("ada_a", 0, 3, 6)
            means(4, bufB)
            pe.wait_ge(mod_done, N_ADA + 6)
            pe.wait_ge(clo_done, 4)
            for i in range(4):
                features(Slab(BASE["pw2_ctx"] + i), i, G)
            b0 = BASE["pw1_lat"]
            pe.wait_ge(x_ready, 10)
            features(Slab(b0), 0, H, split=3)
            features(Slab(b0 + 1), 1, H)
            pe.wait_ge(x_ready, 12)
            pw1_pe(1, b0 + 2, 5, ctx_sq)
            ffn_pe(pe, features, mm3, 1, "ffn_ctx", 4, [(v_done, 7), (v_done, 8)])

            mean(acc_flat, 2, mu_done, dw_done, 1)
            ada_group("ada_b", 6, 0, 3)
            mean(ctx_sq, 2, var_done, lsq_done, 2)
            ada_group("ada_b", 6, 3, 6)
            pe.wait_ge(mod_done, N_ADA + 12)
            pe.wait_ge(clo_done, 8)
            for i in range(4):
                features(Slab(BASE["pw2_lat"] + i), i, H)
            means(6, bufB)
            means(7, ctx_sq, bank=5)
            ada_group("ada_c", 12, 0, 6)
            ffn_pe(pe, features, mm3, 2, "ffn_lat", 5, [(mod_done, N_ADA + 18), (x_ready, 20)])

            ada_group("ada_d", 18, 0, 2)
            means(8, bufB)
            ada_group("ada_d", 18, 2, 6)
            pe.wait_ge(mod_done, 2 * N_ADA)
            b0 = BASE["qkv"]
            wk, wv = weights(Slab(b0), KT), weights(Slab(b0 + 1), KT)

            def keys(bank, x):
                for m in range(2):
                    for k in range(KT):
                        ins = mm3(ps[:, bank, m * T:m * T + T], [a[:, k, m * P:m * P + P] for a in wk], [a[:, k, :] for a in x],
                                  start=(k == 0 and m == 0))
                return ins

            def values(bank, x):
                for s in range(2):
                    for k in range(KT):
                        ins = mm3(ps[:, bank, s * T:s * T + T], [a[:, k, s * P:s * P + P] for a in x], [a[:, k, :] for a in wv],
                                  start=(k == 0 and s == 0))
                return ins

            pe.wait_ge(xlo_done, KT // 2 * 7)
            keys(1, H)
            values(3, H)
            pe.wait_ge(xlo_done, KT // 2 * 8)
            keys(0, G).then_inc(slab_done, 1)
            values(2, G).then_inc(slab_done, 1)

            def turn(raw_, bank, done):
                for a in range(2):
                    ins = pe.matmul(ps[:, bank, a * T:a * T + T], rot, raw_[:, a, :], start=(a == 0), stop=True, skip_group_check=True)
                ins.then_inc(done, 1)

            pe.wait_ge(s_late, 16)
            pe.wait_ge(kv_sb, 1)
            turn(k_raw, 4, krot_done)
            for i in range(4):
                pe.wait_ge(kv_sb, 2 if i < 2 else 3)
                features(Slab(b0 + 2 + i), i, G)
                if i >= 1:
                    pe.wait_ge(q_sb, i)
                    turn(q_raw[:, 2 * i - 2:2 * i, :], 4 + i, qrot_done)
            pe.wait_ge(q_sb, 4)
            pe.wait_ge(k_ready, 1)
            turn(q_raw[:, 6:8, :], 4, qrot_done)

            def wscores(n):
                i, u, b = n // 2, n % 2, n % 2
                r0 = u * DH
                pe.wait_ge(q_ready, 4 if n == 0 else i // 2 + 1)
                if n >= 2:
                    pe.wait_ge(we_done, n - 1)
                for s in range(2):
                    pe.matmul(ps[:, 2 * b + s, :], q_rot[r0:r0 + DH, i, s * P:s * P + P], k_all[r0:r0 + DH, i // 4, :],
                              start=True, stop=False, skip_group_check=True)
                    c = P if s == 0 else 0
                    ins = pe.matmul(ps[:, 2 * b + s, c:c + P], eye, wmask[:, s, :], start=False, stop=True, skip_group_check=True)
                ins.then_inc(ws_done, 1)

            def wturn(n):
                b = n % 2
                pe.wait_ge(wp_done, n + 1)
                if n >= 1:
                    pe.wait_ge(wt_sb, n)
                for k in range(4):
                    for s in range(2):
                        a = 2 * k + s
                        ins = pe.transpose(ps[:, 4 + a // 4, (a % 4) * P:(a % 4) * P + P],
                                           bufA[:, 1024 * b + 512 * s + k * P:1024 * b + 512 * s + k * P + P], eye)
                ins.then_inc(wt_done, 1)

            def wout(n):
                i, u, b = n // 2, n % 2, n % 2
                kv = 2 * (i // 4) + u
                pe.wait_ge(wt_sb, n + 1)
                if n >= 4:
                    pe.wait_ge(wolo_done, i - 1)
                for k in range(4):
                    ins = pe.matmul(ps[u * DH:u * DH + DH, 6 + i % 2, 0:T], v_all[:, k, kv * DH:kv * DH + DH],
                                    bufB[:, 1024 * b + k * T:1024 * b + k * T + T], start=(k == 0), stop=(k == 3), skip_group_check=True)
                ins.then_inc(wo_done, 1)

            wscores(0)
            for n in range(H2):
                if n + 1 < H2:
                    wscores(n + 1)
                wturn(n)
                if n >= 1:
                    wout(n - 1)
            wout(H2 - 1)
            pe.wait_ge(wolo_done, KT)
            for i in range(4):
                features(Slab(BASE["wo"] + i), i, H)
            means(9, bufB)
            ffn_pe(pe, features, mm3, 3, "ffn2", 8, [(x_ready, 28), (x_ready, 28)])
            means(10, bufB)


def kernel(**inputs):
    import concourse.bacc as bacc
    from concourse.bass_utils import run_bass_kernel_spmd as run

    a = {k: np.asarray(v) for k, v in inputs.items()}
    COL, NCOL = columns()
    STORE, n_slabs = stored()

    def tiles(v):
        return np.ascontiguousarray(np.asarray(v).reshape(-1, P).T)

    w = np.zeros((n_slabs, P, SLAB), np.float32)

    def put(name, i, block):
        k = block.shape[0] // P
        w[STORE[name][0] + i] = block.reshape(k, P, -1).transpose(1, 0, 2).reshape(P, SLAB)

    def put_columns(name, i, mat, c0):
        put(name, i, mat[:, c0:c0 + SLABC])

    def put_ffn(name, up, down):
        ups = [0] + [3 * j - 1 for j in range(1, NJ)]
        for j, i in enumerate(ups):
            put_columns(name, i, up, j * SLABC)
            put_columns(name, i + 1, up, D_FF + j * SLABC)
            put(name, 3 * NJ - 1 if j == NJ - 1 else 3 * j + 4, down[j * SLABC:(j + 1) * SLABC])

    win = a["w_in"][0]
    o_qa, o_ka, o_va, o_ra = 0, GLA_W, 2 * GLA_W, 2 * GLA_W + V_W
    o_lr = o_ra + V_W
    o_qb = o_lr + RANK
    o_kb, o_vb, o_g = o_qb + MOBA_W, o_qb + 2 * MOBA_W, o_qb + 3 * MOBA_W
    lr = np.zeros((D, SLABC), np.float32)
    lr[:, 0:RANK] = win[:, o_lr:o_lr + RANK]
    put("lead", AT["mix", 0], lr)
    i = 1
    for c0, width in [(o_ka, GLA_W), (o_qa, GLA_W), (o_va, V_W), (o_kb, MOBA_W), (o_qb, MOBA_W), (o_vb, MOBA_W),
                      (o_ra, V_W), (o_g, 2 * D)]:
        for c in range(c0, c0 + width, SLABC):
            put_columns("lead", AT["mix", i], win, c)
            i += 1
    for i in range(2):
        put("moba", i, a["w_branch_moba"][0][:, i * 512:(i + 1) * 512])
    for i in range(4):
        put_columns("gla", i, a["w_branch_gla"][0], i * SLABC)
        put_columns("out", i, a["w_out"][0], i * SLABC)
    put_ffn("ffn0", a["w_up"][0], a["w_down"][0])
    for layer in range(2):
        for i in range(N_ADA):
            put_columns(*(("lead", AT["ada", i]) if layer == 0 else ("ada1", i)), a["ada_w_2"][layer], i * SLABC)
        put_ffn(f"ffn{layer + 1}", a["ffn_w_up_2"][layer], a["ffn_w_down_2"][layer])
    for j in range(4):
        put_columns("pw1", 2 * j, a["conv_w_pw1_2"][0], j * SLABC)
        put_columns("pw1", 2 * j + 1, a["conv_w_pw1_2"][0], D + j * SLABC)
        put_columns("pw2", j, a["conv_w_pw2_2"][0], j * SLABC)
    pairs = [(h, h + 4) for g in (0, 8) for h in range(g, g + 4)]
    by_pair = np.concatenate([np.arange(h * DH, (h + 1) * DH) for p in pairs for h in p])
    wqkv = a["attn_w_qkv_2"][0]
    put_columns("qkv", 0, wqkv, H2 * DH)
    put_columns("qkv", 1, wqkv, (H2 + HKV) * DH)
    wq, wo = wqkv[:, :H2 * DH][:, by_pair], a["attn_w_o_2"][0][by_pair]
    for i in range(4):
        put_columns("qkv", 2 + i, wq, i * SLABC)
        put_columns("wo", i, wo, i * SLABC)

    cols = np.zeros((P, NCOL), np.float32)

    def put_cols(name, v):
        c, k = COL[name]
        cols[:, c:c + k] = tiles(v)

    put_cols("norm_mix", a["norm_mix"][0])
    put_cols("gla_out_norm", a["gla_out_norm"][0])
    put_cols("norm_ffn", a["norm_ffn"][0])
    put_cols("norm_final", a["norm_final"])
    put_cols("ffn_w0", a["conv_w"][0])
    put_cols("ffn_b0", a["conv_b"][0])
    for layer in range(2):
        put_cols(f"ffn_w{layer + 1}", a["ffn_w_dw_2"][layer])
        put_cols(f"ffn_b{layer + 1}", a["ffn_b_dw_2"][layer])
        put_cols(f"norm1_{layer}", a["norm1_g_2"][layer])
        put_cols(f"norm2_{layer}", a["norm2_g_2"][layer])
        put_cols(f"ada_b{layer}", a["ada_b_2"][layer])
    put_cols("final_g", a["final_g_2"])
    for name, key in [("pw1_b", "conv_b_pw1_2"), ("dw_w", "conv_w_dw_2"), ("dw_b", "conv_b_dw_2"), ("ln_g", "conv_ln_g_2"),
                      ("ln_b", "conv_ln_b_2"), ("pw2_b", "conv_b_pw2_2")]:
        put_cols(name, a[key][0])
    put_cols("cond", np.concatenate([a["c_2"][0], a["c_ctx_2"]]))
    c, k = COL["sink"]
    cols[:, c:c + k] = a["attn_sink_2"][0][[h for p in pairs for h in p]][None, :]

    eye = np.eye(P, dtype=np.float32)
    tok = np.arange(P)
    cum = ((tok[:, None] <= tok[None, :]) & (tok[:, None] // CHUNK == tok[None, :] // CHUNK)) / TAU
    consts = np.stack([eye, eye[::-1], cum.astype(np.float32)], axis=1)
    dist = T - 1 - np.arange(2 * T)
    half = BUCKETS // 2
    far = half + (np.log(np.maximum(dist, 1).astype(np.float32) / half) / np.float32(np.log(MAX_DIST / half))
                  * (BUCKETS - half)).astype(np.int32)
    bucket = np.where(dist < half, dist, np.minimum(far, BUCKETS - 1))
    bucket = np.where(dist < 0, BUCKETS, bucket)
    onehot = (np.arange(BUCKETS + 1)[:, None] == bucket[None, :]).astype(np.float32)

    pos = np.arange(T)
    freqs = (np.float32(ROPE_BASE) ** (-np.arange(DH // 4, dtype=np.float32) / (DH // 4))).astype(np.float32)
    angle = np.concatenate([(pos // GRID_W).astype(np.float32)[:, None] * freqs, (pos % GRID_W).astype(np.float32)[:, None] * freqs], axis=1)
    rope = [np.tile(f(angle).T.astype(np.float32), (4, 1)) for f in (np.cos, np.sin)]
    rot = np.zeros((P, P), np.float32)
    for h in (0, DH):
        for d in range(DH // 2):
            rot[h + DH // 2 + d, h + d] = -1.0
            rot[h + d, h + DH // 2 + d] = 1.0
    outside = [np.where(tok[None, :] > tok[:, None], NEG, 0.0), np.where(tok[None, :] < tok[:, None], NEG, 0.0)]
    tables = np.concatenate(rope + [rot] + outside, axis=1).astype(np.float32)
    sel = np.array([[1, 0], [1, 0], [0, 1], [0, 1]], np.float32)

    arrays = {
        "tables": tables, "sel": sel,
        "ctxT": np.ascontiguousarray(a["ctx_2"][0].T.reshape(KT, P, T).transpose(1, 0, 2)),
        "w": w, "cols": cols, "consts": np.ascontiguousarray(consts), "onehot": onehot.reshape(BUCKETS + 1, 2, T),
        "xT": np.ascontiguousarray(a["x"][0].T.reshape(KT, P, T).transpose(1, 0, 2)),
        "rel_bias": a["rel_bias"], "w_lr_up": a["w_lr_up"][0], "b_forget": a["b_forget"],
    }
    arrays = {f"{k}_dram": np.ascontiguousarray(v) for k, v in arrays.items()}

    nc = bacc.Bacc("TRN2", target_bir_lowering=False, num_devices=1)
    io = {k[:-5]: nc.dram_tensor(k, v.shape, F32, kind="ExternalInput").ap() for k, v in arrays.items()}
    io["out"] = nc.dram_tensor("out_dram", (P, KT, T), F32, kind="ExternalOutput").ap()
    io["scratch"] = nc.dram_tensor("bias_rows", (H_MOBA, 512), F32, kind="Internal").ap()
    build(nc, io)
    got = run(nc, [arrays], core_ids=[0]).results[0]["out_dram"]
    return np.ascontiguousarray(got.transpose(2, 1, 0).reshape(1, T, D))
```

```python
from contextlib import ExitStack

import numpy as np

import concourse.bass as bass
from concourse import mybir

F32 = mybir.dt.float32
F32R = mybir.dt.float32r
BF16 = mybir.dt.bfloat16
ACT = mybir.ActivationFunctionType
ALU = mybir.AluOpType
AX = mybir.AxisListType

P = 128
T = 256
D = 1024
KT = D // P
EPS = 1e-6
SLAB = 2048
SLABC = 256
RING = 3

H_GLA, DK, DV, CHUNK, RANK, TAU = 4, 128, 256, 64, 16, 16.0
NCH = T // CHUNK
H_MOBA, DH = 8, 64
BUCKETS, MAX_DIST = 32, 128
NEG = -1e30
D_FF = 2816
NJ = D_FF // SLABC
FT = D_FF // P
TAPS = 3
CONV_TAPS = 31
PADC = (CONV_TAPS - 1) // 2
H2, HKV, WINDOW, GRID_W, ROPE_BASE = 16, 4, 128, 64, 10000.0
GLA_W, V_W, MOBA_W = H_GLA * DK, H_GLA * DV, H_MOBA * DH


def columns():
    at, n = {}, 0
    for name, k in [
        ("norm_mix", KT), ("gla_out_norm", KT), ("norm_ffn", KT), ("norm_final", KT),
        ("ffn_w0", TAPS * 2 * FT), ("ffn_w1", TAPS * 2 * FT), ("ffn_w2", TAPS * 2 * FT),
        ("ffn_b0", 2 * FT), ("ffn_b1", 2 * FT), ("ffn_b2", 2 * FT),
        ("norm1_0", KT), ("norm1_1", KT), ("norm2_0", KT), ("norm2_1", KT), ("final_g", KT),
        ("pw1_b", 2 * KT), ("dw_w", CONV_TAPS * KT), ("dw_b", KT), ("ln_g", KT), ("ln_b", KT), ("pw2_b", KT),
        ("ada_b0", 48), ("ada_b1", 48), ("cond", 2 * KT), ("sink", H2),
    ]:
        at[name] = (n, k)
        n += k
    return at, n


N_MIX, N_ADA = 27, 6 * D // SLABC

ADA_FIRST = 2
LEAD = [("ada", i) for i in range(ADA_FIRST)]
for _g in range(N_MIX):
    LEAD.append(("mix", _g))
    if ADA_FIRST + _g < N_ADA:
        LEAD.append(("ada", ADA_FIRST + _g))
AT = {item: n for n, item in enumerate(LEAD)}
MOST = 6


def ada_bank(i):
    return 3 - 2 * (i // MOST % 2)


RUN_ORDER = [
    ("lead", "lead", 0, len(LEAD)), ("gla", "gla", 0, 4), ("moba", "moba", 0, 2),
    ("pw1_ctx_a", "pw1", 0, 2), ("out", "out", 0, 4), ("pw1_ctx_b", "pw1", 2, 6),
    ("ffn0", "ffn0", 0, 3 * NJ - 1), ("ada_a", "ada1", 0, 3), ("ffn0_end", "ffn0", 3 * NJ - 1, 1), ("ada_a2", "ada1", 3, 3),
    ("pw2_ctx", "pw2", 0, 4), ("pw1_lat", "pw1", 0, 8),
    ("ffn_ctx", "ffn1", 0, 3 * NJ - 1), ("ada_b", "ada1", 6, 3), ("ffn_ctx_end", "ffn1", 3 * NJ - 1, 1), ("ada_b2", "ada1", 9, 3),
    ("pw2_lat", "pw2", 0, 4), ("ada_c", "ada1", 12, 4),
    ("ffn_lat", "ffn1", 0, 3 * NJ - 1), ("k_ctx", "qkv", 0, 1), ("ffn_lat_end", "ffn1", 3 * NJ - 1, 1), ("v_ctx", "qkv", 1, 1),
    ("ada_d", "ada1", 16, 4), ("qkv", "qkv", 0, 6), ("wo", "wo", 0, 4), ("ada_e", "ada1", 20, 4),
    ("ffn2", "ffn2", 0, 3 * NJ - 1), ("ffn2_end", "ffn2", 3 * NJ - 1, 1),
]

GROUP_BANKS = {"ada_a": (3, 2), "ada_b": (3, 2), "ada_c": (1, 6), "ada_d": (5, 6), "ada_e": (5, 7)}
GROUPS = list(GROUP_BANKS)


def stored():
    at, n = {}, 0
    for _, name, first, k in RUN_ORDER:
        at[name] = max(at.get(name, 0), first + k)
    out = {}
    for name, k in at.items():
        out[name] = (n, k)
        n += k
    return out, n


def stream():
    at, n = {}, 0
    for use, _, _, k in RUN_ORDER:
        at[use] = n
        n += k
    return at, n


def pool_words(use):
    return 1920 if use in ("ffn0", "ffn_ctx", "ada_a2", "ada_b2") else 1024


class Slab:

    def __init__(self, c, n=0, j=0):
        self.c, self.n, self.j = c, n, j

    def __add__(self, k):
        return Slab(self.c + k, self.n, self.j)

    @property
    def slot(self):
        return self.c % RING

    def number(self):
        return self.c + 3 * self.n * self.j

    def landings(self):
        return 16 * (self.c // RING + 1) + 16 * self.n * self.j


class Tally:

    def __init__(self, sem):
        self.sem, self.n, self.j, self.per, self.n0 = sem, 0, None, 0, 0

    def mark(self, ins):
        ins.then_inc(self.sem, 1)
        self.n += 1

    def value(self):
        return self.n if self.j is None else self.n + self.per * self.j

    def enter(self, j, per):
        self.j, self.per, self.n0 = j, per, self.n

    def leave(self, times):
        assert self.n - self.n0 == self.per, (self.n, self.n0, self.per)
        self.n, self.j = self.n0 + self.per * times, None


def build(nc, io):
    COL, NCOL = columns()
    STORE, _ = stored()
    BASE, TOTAL = stream()
    FIRST, COUNT = ({use: entry[i] for use, *entry in RUN_ORDER} for i in (1, 2))

    def group_slabs(use):
        return [BASE[u] + k for u in (use, use + "2") if u in BASE for k in range(COUNT[u])]

    ctx = ExitStack()
    with ctx:
        def sb(name, shape, dt=F32):
            return ctx.enter_context(nc.sbuf_tensor(name, shape, dt))

        def sem(name):
            return ctx.enter_context(nc.semaphore(name))

        ps = ctx.enter_context(nc.psum_tensor("ps", [P, 8, 512], F32))
        raw = sb("raw", [P, RING, SLAB])
        whi = sb("whi", [P, RING, SLAB], F32R)
        wlo = sb("wlo", [P, RING, SLAB], F32R)
        xlat = sb("xlat", [P, KT, T])
        h_hi = sb("h_hi", [P, KT, T], F32R)
        h_lo = sb("h_lo", [P, KT, T], F32R)
        g_hi = sb("g_hi", [P, KT, T], F32R)
        g_lo = sb("g_lo", [P, KT, T], F32R)
        m_hi = sb("m_hi", [P, 2, 2, T], F32R)
        m_lo = sb("m_lo", [P, 2, 2, T], F32R)
        cnd = sb("cnd", [P, 4 * MOST * KT + P], F32R)
        cnd_at = 4 * (MOST - 1)
        cnd4 = cnd[:, cnd_at:cnd_at + 4 * MOST * KT].rearrange("p (k f) -> p k f", f=4 * MOST)
        cva = sb("cva", [P, 2, 2, T])
        cvb = sb("cvb", [P, 2, 2, T])
        bufA = sb("bufA", [P, SLAB])
        bufB = sb("bufB", [P, SLAB])
        gates = sb("gates", [P, 2 * KT, T])
        sra = sb("sra", [P, KT, T])
        mqk = sb("mqk", [P, 2, 4, T])
        mv = sb("mv", [P, 2, MOBA_W])
        state = sb("state", [P, 2, H_GLA, DV])
        brev = sb("brev", [P, H_MOBA, T])
        cols = sb("cols", [P, NCOL])
        ones = sb("ones", [P, P])
        consts = sb("consts", [P, 3, P])
        rstd = sb("rstd", [P, 2, T])
        tiny = sb("tiny", [P, 64])
        relb = sb("relb", [BUCKETS + 1, H_MOBA])
        epsc = sb("epsc", [P, 1])
        eye_b = sb("eye_b", [P, P], BF16)
        wmask_b = sb("wmask_b", [P, 2, P], BF16)
        warm = sb("warm", [P, 1])
        mod = sb("mod", [P, 2, 6 * KT, 2])
        amod = sb("amod", [P, 7, KT])
        sel = sb("sel", [4 * MOST, 2 * MOST])

        def flat(a):
            names = "abc"[:len(a.shape) - 1]
            return a.rearrange(f"p {' '.join(names)} -> p ({' '.join(names)})")

        qa, ka = gates[:, 0:4, :], gates[:, 4:8, :]
        va = flat(gates[:, 8:16, :]).rearrange("p (s n) -> p s n", s=2)
        wlr, alr = mv[0:RANK + 1, 0, :], mv[0:RANK + 1, 1, 0:T]
        eye, rev, cum = (consts[:, i, :] for i in range(3))
        xctx = brev
        g_flat = flat(gates[:, :, :])
        VP = T + 2 * PADC
        vpad = g_flat[:, 0:KT * VP].rearrange("p (t n) -> p t n", t=KT)
        acc = sra
        late = KT * VP
        rope_cs = g_flat[:, late:late + 2 * T].rearrange("p (a t) -> p a t", a=2)
        rot = g_flat[:, late + 2 * T:late + 2 * T + P]
        wmask = g_flat[:, late + 2 * T + P:late + 2 * T + 3 * P].rearrange("p (a k) -> p a k", a=2)
        lstd = g_flat[:, late + 2 * T + 3 * P:late + 4 * T + 3 * P].rearrange("p (a t) -> p a t", a=2)
        modrow = cvb[0:4 * MOST, 1, :, :]
        late_rows = cvb[0:4 * MOST, 0, 0, :]
        ctx_sq, ctx_y = flat(mqk[:, :, :, :]), flat(sra[:, :, :])
        q_raw, q_rot = sra, mqk[:, :, :, :].rearrange("p a b t -> p (a b) t")
        k_raw = mv[:, 0, :].rearrange("p (a t) -> p a t", a=2)
        k_all = flat(state[:, 0, :, :]).rearrange("p (a n) -> p a n", a=2)
        k_hi, k_lo = (a[:, :, :, :].rearrange("p a b t -> p a (b t)") for a in (m_hi, m_lo))
        v_all = state[:, 1, :, :]

        def col(name, i=0):
            c = COL[name][0]
            return cols[:, c + i:c + i + 1]

        MODULATED = [(0, 1, 1, "norm1_0"), (0, 4, 1, "norm2_0"), (0, 1, 0, "norm1_0"), (0, 4, 0, "norm2_0"),
                     (1, 1, 1, "norm1_1"), (1, 1, 0, "norm1_1"), (1, 4, 0, "norm2_1")]

        def gain_of(i):
            return lambda t: amod[:, i, t:t + 1]

        def shift_of(layer, i, s):
            return lambda t: mod[:, layer, i * KT + t, s:s + 1]

        s_cols, s_consts, s_small, s_x = sem("cols_landed"), sem("consts_landed"), sem("small_landed"), sem("x_landed")
        s_ctx, s_late = sem("context_landed"), sem("tables_landed")
        s_memset, s_relb = sem("memsets_done"), sem("later_keys_set")
        landed = [sem(f"slab_landed{i}") for i in range(RING)]
        hi_done, slab_done = sem("slab_hi_done"), sem("slab_used")
        lo_done, lo2_done = sem("slab_lo_done_by_vector"), sem("slab_lo_done_by_gpsimd")
        dve_order, act_order, pool_order = sem("dve_order"), sem("act_order"), sem("pool_order")
        sq_done, fold_done = sem("squares_done"), sem("squares_folded")
        ms_done, std_done, y_done = sem("means_done"), sem("std_done"), sem("normed")
        xhi_done, xlo_done = sem("act_hi_done"), sem("act_lo_done")
        mix_drained = sem("mix_drained")
        z_done, la_done, b_done, blast = sem("z_done"), sem("la_done"), sem("b_done"), sem("blast_done")
        exps_done, dec_done = sem("exps_done"), sem("decayed_done")
        attn_done, attn_sb, attn_masked = sem("attn_done"), sem("attn_copied"), sem("attn_masked")
        kteT_done, kteT_sb = sem("kteT_done"), sem("kteT_copied")
        kv_done, state_done = sem("kv_done"), sem("state_done")
        o_done, o_sq, o_sb, oms_done, ostd_done = sem("o_done"), sem("o_squared"), sem("o_copied"), sem("o_means_done"), sem("o_std_done")
        oa_done, oahi_done, oalo_done = sem("oa_done"), sem("oa_hi_done"), sem("oa_lo_done")
        tab_done, tab_sb, tab_out, brev_in = sem("bias_row_done"), sem("bias_row_copied"), sem("bias_row_stored"), sem("bias_landed")
        sc_done, sub_done, e_done, p_done = sem("scores_done"), sem("scores_less_max"), sem("exp_done"), sem("probs_done")
        pt_done, pt_sb, ob_done, obhi_done, oblo_done = sem("probsT_done"), sem("probsT_copied"), sem("ob_done"), sem("ob_hi_done"), sem("ob_lo_done")
        br_drained, mixed_done, mxhi_done, mxlo_done = sem("branch_drained"), sem("mixed_done"), sem("mixed_hi_done"), sem("mixed_lo_done")
        bank_done = sem("output_bank_done")
        x_ready = sem("residual_ready")
        tap0, conv_out, silu_done, mid_f, mid_hi, mid_lo = sem("tap0_done"), sem("conv_done"), sem("silu_done"), sem("mid_done"), sem("mid_hi_done"), sem("mid_lo_done")
        cond_f, cond_zero, cond_hi, cond_lo = sem("cond_done"), sem("cond_cleared"), sem("cond_hi_done"), sem("cond_lo_done")
        row_done, modT_done, mod_done, amod_done = sem("mod_rows_done"), sem("mod_turned"), sem("mod_done"), sem("amod_done")
        rows_done, rowsT_done, mod2_done = sem("group_rows_done"), sem("group_turned"), sem("group_mod_done")
        sg_done, v_done, pads_done, dw_done = sem("sigmoid_done"), sem("glu_done"), sem("pads_cleared"), sem("dwconv_folded")
        mu_done, cen_done, lsq_done, var_done = sem("ln_mean_done"), sem("ln_centred"), sem("ln_squared"), sem("ln_var_done")
        lfold_done = sem("ln_folded")
        lstd_done, lnorm_done, act_done = sem("ln_std_done"), sem("ln_normed"), sem("ln_silu_done")
        chi_done, clo_done = sem("conv_act_hi_done"), sem("conv_act_lo_done")
        kv_sb, krot_done, k_ready = sem("kv_copied"), sem("k_turned"), sem("k_roped")
        khi_done, klo_done, qhi_done, qlo_done = sem("k_hi_done"), sem("k_lo_done"), sem("q_hi_done"), sem("q_lo_done")
        wmask_ready = sem("masks_ready")
        q_sb, qrot_done, q_ready = sem("q_copied"), sem("q_turned"), sem("q_roped")
        ws_done, wmax_done, we_done, wp_done = sem("window_scores"), sem("window_max"), sem("window_exp"), sem("window_probs")
        wt_done, wt_sb, wo_done, wohi_done, wolo_done = (sem("window_probsT"), sem("window_probsT_copied"), sem("window_out"),
                                                        sem("window_out_hi"), sem("window_out_lo"))
        out_stored = sem("out_stored")

        def place(h, r):
            return h % 2 * 4 + h // 2 if r == 0 else h % 2 * 2 + h % 4 // 2

        def pt_of(r):
            return [state[:, 1, :, :], cva[:, :, :, :], cvb[:, :, :, :]][r]

        def down_slab(b0, j):
            return b0 + 3 * j + 4

        def use_of(c):
            return [use for use, _, _, _ in RUN_ORDER if BASE[use] <= c][-1]

        def ffn_v(f):
            return (0, 1, 1, 2)[f]

        block = ctx.enter_context(nc.Block())

        def ffn_act(act, hi, f, use, tail=None):
            b0 = BASE[use]
            centre = 2 if f == 0 else 1
            c, b = COL[f"ffn_w{ffn_v(f)}"][0] + centre * 2 * FT, COL[f"ffn_b{ffn_v(f)}"][0]

            def tap(half, j, par):
                buf = (cva, cvb)[half]
                for m in range(2):
                    t = 2 * j + (m + half * FT)
                    ins = act.activation(buf[:, par, m, :], ps[:, 2 * par + half, m * T:m * T + T], ACT.Identity,
                                         scale=cols[:, bass.ds(t + c, 1)], bias=cols[:, bass.ds(t + b, 1)])
                ins.then_inc(tap0, 1)

            def up(g, j, par, first):
                hi(g + RING)
                act.wait_ge(slab_done, g.number() + 1)
                if not first:
                    act.wait_ge(mid_f, j + (f * NJ - 1))
                tap(0, j, par)
                hi(g + (RING + 1))
                act.wait_ge(slab_done, g.number() + 2)
                if not first:
                    act.wait_ge(mid_lo, j + (f * NJ - 1))
                tap(1, j, par)
                act.wait_ge(conv_out, 2 * j + (f * 2 * NJ + 1))
                act.activation(cva[:, par, :, :], cva[:, par, :, :], ACT.Silu).then_inc(silu_done, 1)

            def split(j, par, first):
                act.wait_ge(mid_f, j + (f * NJ + 1))
                if not first:
                    act.wait_ge(slab_done, down_slab(b0, j - 2) + 1)
                act.activation(m_hi[:, par, :, :], cvb[:, par, :, :], ACT.Copy).then_inc(mid_hi, 1)

            up(Slab(b0), 0, 0, True)
            split(0, 0, True)
            up(Slab(b0 + 2), 1, 1, True)
            hi(Slab(b0 + 4 + RING))
            split(1, 1, True)
            with act.Fori(0, 4) as jj:
                for u in range(2):
                    g = Slab(b0 + 5 + 3 * u, 2, jj)
                    up(g, 2 * jj + (2 + u), u, False)
                    hi(g + (2 + RING))
                    split(2 * jj + (2 + u), u, False)
            g = Slab(b0 + 3 * NJ - 4)
            up(g, NJ - 1, 0, False)
            others = BASE[use + "_end"] - BASE[use] - COUNT[use]
            hi(g + (2 + RING))
            if others == RING:
                hi(g + (3 + RING))
            split(NJ - 1, 0, False)
            for k in range(1 if others == RING else 0, others):
                hi(g + (3 + k + RING))
            if tail:
                tail()
            hi(g + (3 + others + RING))

        def ffn_dve(dve, lo, order, f, use, host=None, tail=None):
            b0 = BASE[use]
            shifted = [(0, 2, -2), (1, 1, -1)] if f == 0 else [(0, 1, -1), (2, 0, 1)]
            c0 = COL[f"ffn_w{ffn_v(f)}"][0]
            others = BASE[use + "_end"] - BASE[use] - COUNT[use]

            def taps(half, j, par):
                buf = (cva, cvb)[half]
                dve.wait_ge(tap0, 2 * j + (f * 2 * NJ + half + 1))
                for i, (k, first, shift) in enumerate(shifted):
                    n = T - abs(shift)
                    src = first + shift
                    for m in range(2):
                        w = cols[:, bass.ds(2 * j + (c0 + k * 2 * FT + half * FT + m), 1)]
                        out = buf[:, par, m, first:first + n]
                        ins = dve.scalar_tensor_tensor(out, ps[:, 2 * par + half, m * T + src:m * T + src + n], w, out,
                                                       ALU.mult, ALU.add)
                        if i == 0:
                            order.mark(ins)
                    if i == 0:
                        dve.wait_ge(dve_order, order.value())
                ins.then_inc(conv_out, 1)

            def pair(g, j, par, down, beside):
                lo(g + RING)
                taps(0, j, par)
                if beside and down:
                    beside(0)
                lo(g + (RING + 1))
                taps(1, j, par)
                dve.wait_ge(silu_done, j + (f * NJ + 1))
                dve.wait_ge(conv_out, 2 * j + (f * 2 * NJ + 2))
                dve.tensor_tensor(cvb[:, par, :, :], cva[:, par, :, :], cvb[:, par, :, :], ALU.mult).then_inc(mid_f, 1)
                if beside and down:
                    beside(1)
                if down:
                    lo(g + (2 + RING))
                if isinstance(j, int) and j == NJ - 1 and others == RING:
                    lo(g + (3 + RING))
                dve.wait_ge(mid_hi, j + (f * NJ + 1))
                dve.tensor_tensor(m_lo[:, par, :, :], cvb[:, par, :, :], m_hi[:, par, :, :].bitcast(F32), ALU.subtract)\
                   .then_inc(mid_lo, 1)
                if beside:
                    for k in (2,) if down else (0, 1, 2):
                        beside(k)

            def hosted(j):
                return (lambda k: host(j, k)) if host else None

            pair(Slab(b0), 0, 0, False, hosted(0))
            pair(Slab(b0 + 2), 1, 1, True, hosted(1))
            with dve.Fori(0, 4) as jj:
                order.enter(jj, 8 + (6 * KT if host else 0))
                for u in range(2):
                    pair(Slab(b0 + 5 + 3 * u, 2, jj), 2 * jj + (2 + u), u, True, hosted(2 * jj + (2 + u)))
                order.leave(4)
            g = Slab(b0 + 3 * NJ - 4)
            pair(g, NJ - 1, 0, True, tail)
            for k in range(1 if others == RING else 0, others):
                lo(g + (3 + k + RING))
            if tail:
                tail(3)
            lo(g + (3 + others + RING))

        def ffn_pe(pe, features, mm3, f, use, x, split, free, tail=None, early=None, before_end=None):
            b0 = BASE[use]

            def up(g, j, par, first):
                for half in range(2):
                    if not first:
                        pe.wait_ge(conv_out, 2 * j + (f * 2 * NJ + half - 3))
                    features(g + half, 2 * par + half, x, split=split if first and j == 0 and half == 0 else None)
                    if early and first and j == 0 and half == 0:
                        early()

            def down(g, j, par, first=False, last=False, halfway=None):
                pe.wait_ge(lo_done, g.number() + 1)
                pe.wait_ge(lo2_done, g.number() + 1)
                pe.wait_ge(mid_lo, j + (f * NJ + 1))
                w = [a[:, g.slot, :].rearrange("p (k n) -> p k n", k=2) for a in (whi, wlo)]
                for m in range(KT):
                    if halfway and m == KT // 2:
                        halfway()
                    for k in range(2):
                        ins = mm3(ps[:, 4 + m // 2, (m % 2) * T:(m % 2) * T + T], [a[:, k, m * P:m * P + P] for a in w],
                                  [m_hi[:, par, k, :], m_lo[:, par, k, :]], start=(first and k == 0 and m % 2 == 0))
                    if last and m % 2 and m < KT - 1:
                        ins.then_inc(bank_done, 1)
                ins.then_inc(slab_done, 1)

            pe.wait_ge(*free[0])
            up(Slab(b0), 0, 0, True)
            pe.wait_ge(*free[1])
            up(Slab(b0 + 2), 1, 1, True)
            down(Slab(b0 + 4), 0, 0, True)
            with pe.Fori(0, 4) as jj:
                for u in range(2):
                    g = Slab(b0 + 5 + 3 * u, 2, jj)
                    up(g, 2 * jj + (2 + u), u, False)
                    down(g + 2, 2 * jj + (1 + u), 1 - u)
            up(Slab(b0 + 3 * NJ - 4), NJ - 1, 0, False)
            down(Slab(b0 + 3 * NJ - 2), NJ - 2, 1)
            if before_end:
                pe.wait_ge(conv_out, 2 * NJ * f + 2 * (NJ - 1))
                before_end()
            down(Slab(BASE[use + "_end"]), NJ - 1, 0, last=True, halfway=tail)

        @block.sync
        def _(sp):
            def load(name, first, g):
                if g.c >= RING:
                    sp.wait_ge(lo_done, (g + -RING).number() + 1)
                    sp.wait_ge(lo2_done, (g + -RING).number() + 1)
                sp.dma_start(raw[:, g.slot, :], io["w"][bass.ds(STORE[name][0] + first, 1)]).then_inc(landed[g.slot], 16)

            def run(use, name, first, k0, k1):
                times = (k1 - k0) // RING
                if times > 1:
                    with sp.Fori(0, times) as j:
                        for k in range(RING):
                            load(name, 3 * j + (first + k0 + k), Slab(BASE[use] + k0 + k, 1, j))
                    k0 += RING * times
                for k in range(k0, k1):
                    load(name, first + k, Slab(BASE[use] + k))

            sp.dma_start(xlat[:, :, :], io["xT"]).then_inc(s_x, 16)
            sp.dma_start(cols[:, :], io["cols"]).then_inc(s_cols, 16)
            for use, name, first, count in RUN_ORDER:
                if use == "lead":
                    run(use, name, first, 0, RING)
                    sp.dma_start(relb[0:BUCKETS, :], io["rel_bias"]).then_inc(s_small, 16)
                    sp.dma_start(sra[0:BUCKETS + 1, 0:2, :], io["onehot"]).then_inc(s_small, 16)
                    sp.dma_start(sel[:, :], io["sel"]).then_inc(s_small, 16)
                    sp.dma_start(wlr[0:RANK, :], io["w_lr_up"]).then_inc(s_small, 16)
                    sp.dma_start(wlr[RANK:RANK + 1, :], io["b_forget"]).then_inc(s_small, 16)
                    sp.dma_start(consts[:, :, :], io["consts"]).then_inc(s_consts, 16)
                    run(use, name, first, RING, 4 * RING)
                    sp.wait_ge(tab_sb, 1)
                    sp.dma_start(io["scratch"], flat(state[0:H_MOBA, 0, 0:2, :])).then_inc(tab_out, 16)
                    run(use, name, first, 4 * RING, 6 * RING)
                    sp.wait_ge(tab_out, 16)
                    sp.dma_start(brev[:, :, :], bass.AP(io["scratch"].tensor, 0, [[1, P], [512, H_MOBA], [1, T]]))\
                      .then_inc(brev_in, 16)
                    run(use, name, first, 6 * RING, count)
                    sp.wait_ge(sc_done, 3)
                    sp.dma_start(xctx[:, :, :], io["ctxT"]).then_inc(s_ctx, 16)
                    continue
                run(use, name, first, 0, count)
                if use == "pw1_ctx_b":
                    sp.wait_ge(br_drained, 6)
                    sp.dma_start(g_flat[:, late:late + 2 * T + 3 * P], io["tables"]).then_inc(s_late, 16)
            for k in range(0, KT, 2):
                sp.wait_ge(y_done, KT * 10 + k + 2)
                sp.dma_start(io["out"][:, k:k + 2, :], xlat[:, k:k + 2, :]).then_inc(out_stored, 16)
            sp.wait_ge(out_stored, 16 * KT // 2)

        @block.gpsimd
        def _(pool):
            pool.memset(ones[:, :], 1.0 / D).then_inc(s_memset, 1)
            pool.memset(epsc[:, :], EPS).then_inc(s_memset, 1)
            pool.memset(alr, 1.0).then_inc(s_memset, 1)

            def run(use, k0, k1):
                part = slice(SLAB - pool_words(use), SLAB)

                def lo(g):
                    pool.wait_ge(hi_done, g.number() + 1)
                    pool.tensor_tensor(wlo[:, g.slot, part], raw[:, g.slot, part], whi[:, g.slot, part].bitcast(F32),
                                       ALU.subtract).then_inc(lo2_done, 1)

                times = (k1 - k0) // RING
                if times > 1:
                    with pool.Fori(0, times) as j:
                        for k in range(RING):
                            lo(Slab(BASE[use] + k0 + k, 1, j))
                    k0 += RING * times
                for k in range(k0, k1):
                    lo(Slab(BASE[use] + k))

            masked_at = AT["mix", 8] + RING + 2
            run("lead", 0, masked_at)
            attn = bufA[:, 0:1024].rearrange("p (a i) -> p a i", i=P)
            pool.wait_ge(attn_sb, 1)
            pool.affine_select(out=attn, in_=attn, compare_op=ALU.is_ge, fill=0.0, base=0,
                               pattern=[[0, 8], [1, P]], channel_multiplier=-1).then_inc(pool_order, 1)
            pool.wait_ge(pool_order, 1)
            pool.memset(attn[0:CHUNK, :, CHUNK:P], 0.0).then_inc(attn_masked, 1)
            run("lead", masked_at, len(LEAD))
            for use, _, _, count in RUN_ORDER[1:]:
                run(use, 0, count)

        @block.scalar
        def _(act):
            order = Tally(act_order)

            def hi(g):
                if isinstance(g.j, int) and g.c >= TOTAL:
                    return
                act.wait_ge(landed[g.slot], g.landings())
                if g.c >= RING:
                    act.wait_ge(slab_done, (g + -RING).number() + 1)
                act.activation(whi[:, g.slot, :], raw[:, g.slot, :], ACT.Copy).then_inc(hi_done, 1)

            def squares(x, sq, preload=False, ready=None):
                for i in range(2):
                    if ready is not None:
                        act.wait_ge(x_ready, ready + 2 * i + 2)
                    act.activation(sq[:, 1024 * i:1024 * i + 1024], x[:, 4 * i:4 * i + 4, :], ACT.Square).then_inc(sq_done, 1)
                if preload:
                    act.wait_ge(act_order, order.value())
                    order.mark(act.activation(warm[:, :], epsc[:, :], ACT.Sqrt))

            def root(n, bank=4):
                act.wait_ge(ms_done, n + 1)
                act.activation(rstd[:, 0, :], ps[:, bank, 0:T], ACT.Sqrt, bias=epsc[:, :]).then_inc(std_done, 1)

            def split_hi(n, y, out, shift=None, between=None):
                for t in range(0, KT, 2):
                    act.wait_ge(y_done, KT * n + t + 2)
                    if shift is None:
                        ins = act.activation(out[:, t:t + 2, :], y[:, t * T:t * T + 2 * T], ACT.Copy)
                    else:
                        for m in (t, t + 1):
                            ins = act.activation(out[:, m, :], y[:, m * T:m * T + T], ACT.Identity, bias=shift(m))
                    ins.then_inc(xhi_done, 1)
                    if between:
                        between(t // 2)

            def mod_rows(i, g):
                q = i // MOST
                act.wait_ge(slab_done, g + 1)
                if q >= 2:
                    act.wait_ge(modT_done, q - 1)
                act.activation(modrow[:, q % 2, :], ps[0:4 * MOST, ada_bank(i), 0:SLABC], ACT.Copy).then_inc(row_done, 1)

            def hi_ahead(use, k0, k1):
                for k in range(k0, k1):
                    hi(Slab(BASE[use] + k + RING))

            def group_rows(use):
                slabs = group_slabs(use)
                n = len(slabs)
                act.wait_ge(slab_done, slabs[-1] + 1)
                act.activation(late_rows[0:4 * n, :], ps[0:4 * n, GROUP_BANKS[use][0], 0:SLABC], ACT.Copy).then_inc(rows_done, 1)

            def glu(q, j, g):
                act.wait_ge(slab_done, g + 1)
                if j >= 2:
                    act.wait_ge(v_done, 4 * q + j - 1)
                for m in range(2):
                    ins = act.activation(cva[:, j % 2, m, :], ps[:, 2 * (j % 2) + 1, m * T:m * T + T], ACT.Sigmoid,
                                         bias=col("pw1_b", KT + 2 * j + m))
                ins.then_inc(sg_done, 1)

            def ln_squares(q):
                act.wait_ge(cen_done, q + 1)
                for i in range(2):
                    act.activation(ctx_sq[:, 1024 * i:1024 * i + 1024], acc[:, 4 * i:4 * i + 4, :], ACT.Square).then_inc(lsq_done, 1)

            def ln_root(q):
                act.wait_ge(var_done, q + 1)
                act.activation(lstd[:, 0, :], ps[:, 0, 0:T], ACT.Sqrt, bias=epsc[:, :]).then_inc(lstd_done, 1)

            def ln_silu(q, out):
                def upper(t):
                    act.wait_ge(act_done, KT * q + t + 2)
                    act.activation(out[:, t:t + 2, :], ctx_sq[:, t * T:t * T + 2 * T], ACT.Copy).then_inc(chi_done, 1)

                for t in range(KT):
                    act.wait_ge(lnorm_done, 2 * q + 1 + t // (KT // 2))
                    act.activation(ctx_sq[:, t * T:t * T + T], acc[:, t, :], ACT.Silu,
                                   scale=col("ln_g", t), bias=col("ln_b", t)).then_inc(act_done, 1)
                    if t % 2 and t > 1:
                        upper(t - 3)
                upper(KT - 2)

            act.wait_ge(s_memset, 3)
            act.wait_ge(s_x, 16)
            squares(xlat, bufB)
            act.wait_ge(s_cols, 16)
            act.activation(tiny[:, 0:16], cols[:, COL["cond"][0]:COL["cond"][0] + 2 * KT], ACT.Silu).then_inc(cond_f, 1)
            act.wait_ge(cond_f, 1)
            act.wait_ge(cond_zero, 1)
            for s in range(2):
                act.activation(cnd4[:, :, 2 * s], tiny[:, 8 * s:8 * s + 8], ACT.Copy).then_inc(cond_hi, 1)
            root(0)
            hi(Slab(0))
            hi(Slab(1))
            split_hi(0, bufA, h_hi)
            hi(Slab(2))

            def drain(n, out, func=ACT.Copy, scale=1.0, rows=P):
                bank = ps[0:rows, n % 4, 0:out.shape[-1] if len(out.shape) == 2 else 512]
                act.activation(out, bank, func, scale=scale).then_inc(mix_drained, 1)

            for n, (kind, g) in enumerate(LEAD):
                hi(Slab(n + RING))
                if kind == "ada":
                    if g % MOST == MOST - 1:
                        mod_rows(g, n)
                    continue
                act.wait_ge(slab_done, n + 1)
                if g == 0:
                    drain(n, alr[0:RANK, :], rows=RANK)
                elif g < 3:
                    drain(n, ka[:, 2 * (g - 1):2 * g, :])
                elif g < 5:
                    drain(n, qa[:, 2 * (g - 3):2 * (g - 3) + 2, :], scale=DK ** -0.5)
                elif g < 9:
                    drain(n, va[:, :, (g - 5) * SLABC:(g - 4) * SLABC])
                elif g < 11:
                    drain(n, mqk[:, 1, 2 * (g - 9):2 * (g - 9) + 2, :])
                elif g < 13:
                    drain(n, mqk[:, 0, 2 * (g - 11):2 * (g - 11) + 2, :], scale=DH ** -0.5)
                elif g < 15:
                    drain(n, mv[:, :, (g - 13) * SLABC:(g - 12) * SLABC])
                elif g < 19:
                    if g == 15:
                        act.wait_ge(tab_done, 1)
                    drain(n, sra[:, 2 * (g - 15):2 * (g - 15) + 2, :], ACT.Silu)
                else:
                    if g == 19:
                        act.wait_ge(o_done, 1)
                    drain(n, gates[:, 2 * (g - 19):2 * (g - 19) + 2, :], ACT.Sigmoid)
                if g == 2:
                    act.wait_ge(z_done, 1)
                    lz = bufB[:, 0:1024]
                    order.mark(act.activation(lz, ps[:, 4:6, :], ACT.Abs))
                    act.wait_ge(act_order, order.value())
                    order.mark(act.activation(lz, lz, ACT.Exp, scale=-1.0))
                    act.wait_ge(act_order, order.value())
                    act.activation(lz, lz, ACT.Ln, bias=1.0).then_inc(la_done, 1)
                if g == 4:
                    act.wait_ge(blast, 2)
                    act.activation(bufA[:, 0:1024], ps[:, 6:8, :], ACT.Exp).then_inc(exps_done, 1)
                    act.activation(bufA[:, 1024:2048], ps[:, 6:8, :], ACT.Exp, scale=-1.0).then_inc(exps_done, 1)
                    act.activation(tiny[:, 16:32], tiny[:, 0:16], ACT.Exp).then_inc(exps_done, 1)
                    act.activation(bufB[:, 0:1024], bufB[:, 0:1024], ACT.Exp).then_inc(exps_done, 1)
                if g == 8:
                    act.wait_ge(attn_done, 1)
                    act.activation(bufA[:, 0:1024], ps[:, 4:6, :], ACT.Copy).then_inc(attn_sb, 1)
                    act.wait_ge(kteT_done, 1)
                    act.activation(bufB[:, 1024:2048], ps[:, 6:8, :], ACT.Copy).then_inc(kteT_sb, 1)
                if g == 13:
                    act.wait_ge(o_done, 1)
                    act.activation(bufB[:, :], ps[:, 4:8, :], ACT.Square).then_inc(o_sq, 1)
                if g == 14:
                    act.wait_ge(oms_done, 1)
                    act.activation(bufB[:, 0:1024], ps[:, 4:6, :], ACT.Sqrt, bias=epsc[:, :], scale=D / DV).then_inc(ostd_done, 1)
                if g == 19:
                    for i in range(2):
                        act.wait_ge(oa_done, KT)
                        act.activation(g_hi[:, 4 * i:4 * i + 4, :], bufA[:, 1024 * i:1024 * i + 1024], ACT.Copy)\
                           .then_inc(oahi_done, 1)
                if g in (17, 20, 23):
                    act.wait_ge(sub_done, (g - 17) // 3 + 1)
                    act.activation(state[:, 0, :, :], state[:, 0, :, :], ACT.Exp).then_inc(e_done, 1)
                if g in (18, 21, 24):
                    r = (g - 18) // 3
                    act.wait_ge(pt_done, r + 1)
                    if r == 2:
                        act.wait_ge(modT_done, N_ADA // MOST)
                    act.activation(pt_of(r), ps[:, 6:8, :], ACT.Copy).then_inc(pt_sb, 1)
            act.wait_ge(ob_done, 1)
            act.activation(m_hi[:, :, :, :], ps[:, 4:6, :], ACT.Copy).then_inc(obhi_done, 1)

            b0 = BASE["gla"]
            hi(Slab(b0 + RING))
            act.wait_ge(s_ctx, 16)
            squares(xctx, ctx_sq)
            hi(Slab(b0 + 1 + RING))
            root(1, bank=6)
            hi(Slab(b0 + 2 + RING))
            act.wait_ge(slab_done, AT["mix", N_MIX - 1] + 1)
            split_hi(1, ctx_y, h_hi, shift_of(0, 0, 1))
            hi(Slab(b0 + 3 + RING))
            b0 = BASE["moba"]
            hi(Slab(b0 + RING))
            hi(Slab(b0 + 1 + RING))
            b0 = BASE["pw1_ctx_a"]
            hi(Slab(b0 + RING))
            act.wait_ge(slab_done, BASE["gla"] + 4)
            for k in range(4):
                act.wait_ge(mixed_done, k + 1)
                act.activation(g_hi[:, 2 * k:2 * k + 2, :], bufA[:, 512 * k:512 * k + 512], ACT.Copy).then_inc(mxhi_done, 1)
            hi(Slab(b0 + 1 + RING))
            glu(0, 0, b0 + 1)
            hi_ahead("out", 0, 4)

            def pw1_act(q, b1, n, x, sq, y, out, shift, ready):
                hi(Slab(b1 + RING))
                act.wait_ge(*ready)
                squares(x, sq)
                hi(Slab(b1 + 1 + RING))
                glu(q, 1, b1 + 1)
                root(n)
                hi(Slab(b1 + 2 + RING))
                split_hi(n, y, out, shift)
                hi(Slab(b1 + 3 + RING))
                glu(q, 2, b1 + 3)
                hi(Slab(b1 + 4 + RING))
                hi(Slab(b1 + 5 + RING))
                glu(q, 3, b1 + 5)

            pw1_act(0, BASE["pw1_ctx_b"], 2, xlat, bufB, bufA, g_hi, None, (x_ready, 4))
            ffn_act(act, hi, 0, "ffn0", lambda: ln_squares(0))

            ln_root(0)
            squares(xlat, bufB, ready=4)
            hi_ahead("ada_a2", 0, 1)
            ln_silu(0, h_hi)
            root(3, bank=0)
            hi_ahead("ada_a2", 1, 2)
            group_rows("ada_a")
            hi_ahead("ada_a2", 2, 3)
            act.wait_ge(y_done, KT * 4)
            squares(xlat, bufB, preload=True)
            hi_ahead("pw2_ctx", 0, 1)
            root(4, bank=0)
            hi_ahead("pw2_ctx", 1, 2)
            split_hi(4, bufA, g_hi, shift_of(0, 0, 0))
            hi_ahead("pw2_ctx", 2, 4)
            b0 = BASE["pw1_lat"]
            hi(Slab(b0 + RING))
            hi(Slab(b0 + 1 + RING))
            glu(1, 0, b0 + 1)
            pw1_act(1, b0 + 2, 5, xctx, ctx_sq, ctx_y, h_hi, shift_of(0, 3, 1), (x_ready, 12))
            ffn_act(act, hi, 1, "ffn_ctx", lambda: ln_squares(1))

            ln_root(1)
            hi_ahead("ada_b2", 0, 1)
            ln_silu(1, g_hi)
            hi_ahead("ada_b2", 1, 2)
            group_rows("ada_b")
            hi_ahead("ada_b2", 2, 3)
            squares(xctx, bufB, ready=12)
            hi_ahead("pw2_lat", 0, 1)
            root(6, bank=0)
            hi_ahead("pw2_lat", 1, 4)
            hi_ahead("ada_c", 0, 1)
            squares(xlat, bufB, preload=True, ready=16)
            hi_ahead("ada_c", 1, 2)
            root(7, bank=0)
            hi_ahead("ada_c", 2, 3)
            split_hi(7, bufA, h_hi, shift_of(0, 3, 0))
            hi_ahead("ada_c", 3, 4)
            group_rows("ada_c")
            split_hi(6, ctx_y, g_hi, shift_of(1, 0, 1))
            ffn_act(act, hi, 2, "ffn_lat", lambda: squares(xlat, bufB, preload=True, ready=20))

            act.wait_ge(slab_done, BASE["ffn_lat_end"] + 1)
            act.activation(k_hi[:, :, T:2 * T], ps[:, 2, :].rearrange("p (a t) -> p a t", a=2), ACT.Copy).then_inc(khi_done, 1)
            root(8)
            hi_ahead("v_ctx", 0, 1)
            act.wait_ge(slab_done, BASE["v_ctx"] + 1)
            act.activation(v_all[:, 2:4, :], ps[:, 3, :].rearrange("p (a n) -> p a n", a=2), ACT.Copy).then_inc(kv_sb, 1)
            hi_ahead("ada_d", 0, 2)
            split_hi(8, bufA, h_hi, shift_of(1, 0, 0))
            hi_ahead("ada_d", 2, 4)
            group_rows("ada_d")

            def q_hi(j):
                act.wait_ge(q_ready, j + 1)
                act.activation(g_hi[:, 2 * j:2 * j + 2, :], q_rot[:, 2 * j:2 * j + 2, :], ACT.Copy).then_inc(qhi_done, 1)

            b0 = BASE["qkv"]
            for i in range(6):
                hi(Slab(b0 + i + RING))
                act.wait_ge(slab_done, b0 + i + 1)
                if i == 0:
                    act.activation(k_raw, ps[:, 0, :], ACT.Copy).then_inc(kv_sb, 1)
                elif i == 1:
                    act.activation(v_all[:, 0:2, :], ps[:, 1, :].rearrange("p (a n) -> p a n", a=2), ACT.Copy).then_inc(kv_sb, 1)
                else:
                    act.activation(q_raw[:, 2 * (i - 2):2 * (i - 2) + 2, :], ps[:, i - 2, :], ACT.Copy, scale=DH ** -0.5).then_inc(q_sb, 1)
                if i == 3:
                    act.wait_ge(k_ready, 1)
                    act.activation(k_hi[:, :, 0:T], k_all[:, :, 0:T], ACT.Copy).then_inc(khi_done, 1)
                if i >= 4:
                    q_hi(i - 4)

            def turned(n):
                b = n % 2
                act.wait_ge(wt_done, n + 1)
                if n >= 2:
                    act.wait_ge(wo_done, n // 2)
                act.activation(bufB[:, 1024 * b:1024 * b + 1024], ps[:, 4:6, :], ACT.Copy).then_inc(wt_sb, 1)

            def out_hi(i):
                act.wait_ge(wo_done, i + 1)
                act.activation(g_hi[:, i, :], ps[:, 6 + i % 2, 0:T], ACT.Copy).then_inc(wohi_done, 1)

            for n in range(H2):
                b = n % 2
                pr = bufA[:, 1024 * b:1024 * b + 1024].rearrange("p (s k) -> p s k", s=2)
                if n >= 4 and n % 2 == 0:
                    out_hi(n // 2 - 2)
                act.wait_ge(wmax_done, n + 1)
                if n >= 2:
                    act.wait_ge(wt_done, n - 1)
                for s in range(2):
                    act.activation(pr[:, s, :], ps[:, 2 * b + s, :], ACT.Exp, bias=tiny[:, 8 * b + 2 + s:8 * b + 3 + s],
                                   accum_out=tiny[:, 16 + 8 * b + s:17 + 8 * b + s])
                act.activation(tiny[:, 18 + 8 * b:20 + 8 * b], tiny[:, 8 * b + 4:8 * b + 6], ACT.Exp).then_inc(we_done, 1)
                if n >= 1:
                    turned(n - 1)
                if n in (1, 2):
                    q_hi(n + 1)
            turned(H2 - 1)
            out_hi(H2 // 2 - 2)
            out_hi(H2 // 2 - 1)
            for i in range(4):
                hi(Slab(BASE["wo"] + i + RING))
            squares(xlat, bufB, preload=True, ready=24)
            hi_ahead("ada_e", 0, 1)
            root(9)
            hi_ahead("ada_e", 1, 2)
            split_hi(9, bufA, h_hi, shift_of(1, 3, 0))
            hi_ahead("ada_e", 2, 4)
            group_rows("ada_e")
            ffn_act(act, hi, 3, "ffn2", lambda: squares(xlat, bufB, preload=True, ready=28))
            root(10)

        @block.vector
        def _(dve):
            order = Tally(dve_order)

            def lo(g):
                if isinstance(g.j, int) and g.c >= TOTAL:
                    return
                part = slice(0, SLAB - pool_words(use_of(g.c)))
                dve.wait_ge(hi_done, g.number() + 1)
                dve.tensor_tensor(wlo[:, g.slot, part], raw[:, g.slot, part], whi[:, g.slot, part].bitcast(F32), ALU.subtract)\
                   .then_inc(lo_done, 1)

            def fold(n, sq):
                if n:
                    dve.wait_ge(y_done, KT * n)
                for i in range(2):
                    dve.wait_ge(sq_done, 2 * n + i + 1)
                    dve.tensor_reduce(rstd[:, i, :], sq[:, 1024 * i:1024 * i + 1024].rearrange("p (t n) -> p n t", n=T), AX.X, ALU.add)\
                       .then_inc(fold_done, 1)

            def scale(n, x, gains, y, first=None):
                dve.wait_ge(std_done, n + 1)
                order.mark(dve.reciprocal(rstd[:, 1, :], rstd[:, 0, :]))
                if first:
                    first()
                dve.wait_ge(dve_order, order.value())
                for t in range(KT):
                    dve.scalar_tensor_tensor(y[:, t * T:t * T + T], x[:, t, :], gains(t), rstd[:, 1, :],
                                             ALU.mult, ALU.mult).then_inc(y_done, 1)

            def scale_split(n, x, gains, i, y, out, shift, first=None, second=None):
                dve.wait_ge(std_done, n + 1)
                order.mark(dve.reciprocal(rstd[:, 1, :], rstd[:, 0, :]))
                if first:
                    first()
                dve.wait_ge(dve_order, order.value())
                for t in range(0, KT, 2):
                    for m in (t, t + 1):
                        dve.scalar_tensor_tensor(y[:, m * T:m * T + T], x[:, m, :], gains(m), rstd[:, 1, :],
                                                 ALU.mult, ALU.mult).then_inc(y_done, 1)
                    if t == 2 and second:
                        second()
                    if t >= 2:
                        split_lo(i, y, out, shift, tiles=(t - 2, t))
                split_lo(i, y, out, shift, tiles=(KT - 2, KT))

            def split_lo(i, y, out, shift=None, between=None, tiles=(0, KT)):
                for t in range(*tiles, 2):
                    dve.wait_ge(xhi_done, KT // 2 * i + t // 2 + 1)
                    if shift is None:
                        ins = dve.tensor_tensor(out[1][:, t:t + 2, :], y[:, t * T:t * T + 2 * T],
                                                out[0][:, t:t + 2, :].bitcast(F32), ALU.subtract)
                    else:
                        for m in (t, t + 1):
                            ins = dve.scalar_tensor_tensor(out[1][:, m, :], y[:, m * T:m * T + T], shift(m),
                                                           out[0][:, m, :].bitcast(F32), ALU.add, ALU.subtract)
                    ins.then_inc(xlo_done, 1)
                    if between:
                        between(t // 2)

            def mod_add(layer, k0, n, bank, done, *ready):
                c0 = COL[f"ada_b{layer}"][0] + k0
                dve.wait_ge(*ready)
                for m in range(2):
                    ins = dve.tensor_tensor(mod[:, layer, k0 + m:k0 + n:2, :],
                                            ps[:, bank, T + n * m:T + n * m + n].rearrange("p (k s) -> p k s", s=2),
                                            cols[:, c0 + m:c0 + n:2, None].to_broadcast([P, n // 2, 2]), ALU.add)
                ins.then_inc(done, 1)

            def lo_ahead(use, k0, k1):
                for k in range(k0, k1):
                    lo(Slab(BASE[use] + k + RING))

            def group_add(use):
                mod_add(1, 2 * FIRST[use], 2 * len(group_slabs(use)), GROUP_BANKS[use][1], mod2_done,
                        rowsT_done, GROUPS.index(use) + 1)

            def modulated(i0, i1, *ready):
                dve.wait_ge(*ready)
                for i in range(i0, i1):
                    layer, which, s, gain = MODULATED[i]
                    dve.scalar_tensor_tensor(amod[:, i, :], mod[:, layer, which * KT:which * KT + KT, s], 1.0,
                                             cols[:, COL[gain][0]:COL[gain][0] + KT], ALU.add, ALU.mult).then_inc(amod_done, 1)
                dve.wait_ge(amod_done, i1)

            def glu(q, j):
                dve.wait_ge(sg_done, 4 * q + j + 1)
                for m in range(2):
                    ins = dve.scalar_tensor_tensor(vpad[:, 2 * j + m, PADC:PADC + T], ps[:, 2 * (j % 2), m * T:m * T + T],
                                                   col("pw1_b", 2 * j + m), cva[:, j % 2, m, :], ALU.add, ALU.mult)
                ins.then_inc(v_done, 1)

            def pw1_dve(q, b1, n, i, x, sq, gains, y, out, shift):
                lo(Slab(b1 + RING))
                fold(n, sq)
                lo(Slab(b1 + 1 + RING))
                glu(q, 1)
                scale(n, x, gains, y)
                lo(Slab(b1 + 2 + RING))
                split_lo(i, y, out, shift)
                lo(Slab(b1 + 3 + RING))
                glu(q, 2)
                lo(Slab(b1 + 4 + RING))
                lo(Slab(b1 + 5 + RING))
                glu(q, 3)

            def dwconv_first(q):
                dve.wait_ge(v_done, 4 * q + 4)
                dve.wait_ge(pads_done, 2)
                for t in range(KT):
                    order.mark(dve.tensor_scalar(acc[:, t, :], vpad[:, t, 0:T], col("dw_w", t), col("dw_b", t), ALU.mult, ALU.add))

            def dwconv(j, k):
                dve.wait_ge(dve_order, order.value())
                for t in range(KT):
                    w = cols[:, bass.ds(3 * KT * j + (COL["dw_w"][0] + KT * (k + 1) + t), 1)]
                    order.mark(dve.scalar_tensor_tensor(acc[:, t, :], vpad[:, t, bass.ds(3 * j + (k + 1), T)], w, acc[:, t, :],
                                                        ALU.mult, ALU.add))

            def wide(a, n=KT):
                return a[:, None, :].to_broadcast([P, n, T])

            def ln_sum(q):
                dve.wait_ge(dve_order, order.value())
                if q:
                    dve.wait_ge(lnorm_done, 2 * q)
                dve.tensor_reduce(lstd[:, 0, :], acc[:, :, :].rearrange("p t n -> p n t"), AX.X, ALU.add).then_inc(dw_done, 1)

            def ln_fold(q):
                for i in range(2):
                    dve.wait_ge(lsq_done, 2 * q + i + 1)
                    dve.tensor_reduce(lstd[:, i, :], ctx_sq[:, 1024 * i:1024 * i + 1024].rearrange("p (t n) -> p n t", n=T),
                                      AX.X, ALU.add).then_inc(lfold_done, 1)

            def ln_tail(q, residual):
                def tail(k):
                    if k == 2:
                        ln_sum(q)
                        ln_centre(q)
                    if k == 3:
                        ln_fold(q)
                        residual()
                return tail

            def ln_centre(q):
                dve.wait_ge(mu_done, q + 1)
                dve.tensor_tensor(acc[:, :, :], acc[:, :, :], wide(ps[:, 0, 0:T]), ALU.subtract).then_inc(cen_done, 1)

            def ln_scale(q):
                dve.wait_ge(lstd_done, q + 1)
                order.mark(dve.reciprocal(lstd[:, 1, :], lstd[:, 0, :]))
                dve.wait_ge(dve_order, order.value())
                for t in (0, KT // 2):
                    half = acc[:, t:t + KT // 2, :]
                    dve.tensor_tensor(half, half, wide(lstd[:, 1, :], KT // 2), ALU.mult).then_inc(lnorm_done, 1)

            def ln_lo(q, out):
                for t in range(0, KT, 2):
                    dve.wait_ge(chi_done, 4 * q + t // 2 + 1)
                    dve.tensor_tensor(out[1][:, t:t + 2, :], ctx_sq[:, t * T:t * T + 2 * T], out[0][:, t:t + 2, :].bitcast(F32),
                                      ALU.subtract).then_inc(clo_done, 1)

            def pw2_dve(use, x, gate, between=None, ahead=0):
                for i in range(4):
                    if between and i == 1:
                        between()
                    lo_ahead(use, max(i, ahead), i + 1)
                    dve.wait_ge(slab_done, BASE[use] + i + 1)
                    for m in range(2):
                        t = 2 * i + m
                        order.mark(dve.tensor_scalar(bufA[:, t * T:t * T + T], ps[:, 4 + i, m * T:m * T + T], col("pw2_b", t), gate(t),
                                                     ALU.add, ALU.mult))
                    dve.wait_ge(dve_order, order.value())
                    dve.tensor_tensor(x[:, 2 * i:2 * i + 2, :], x[:, 2 * i:2 * i + 2, :], bufA[:, 512 * i:512 * i + 512], ALU.add)\
                       .then_inc(x_ready, 1)

            def outputs(f, use, q):
                if q < 3:
                    dve.wait_ge(bank_done, 3 * f + q + 1)
                else:
                    dve.wait_ge(slab_done, BASE[use + "_end"] + 1)

            def gated_residual(f, use, x, gate):
                for t in range(KT):
                    if t % 2 == 0:
                        outputs(f, use, t // 2)
                    ins = dve.scalar_tensor_tensor(x[:, t, :], ps[:, 4 + t // 2, (t % 2) * T:(t % 2) * T + T], gate(t), x[:, t, :],
                                                   ALU.mult, ALU.add)
                    if t % 2:
                        ins.then_inc(x_ready, 1)

            H, G = (h_hi, h_lo), (g_hi, g_lo)
            dve.memset(cnd[:, :].bitcast(F32), 0.0).then_inc(cond_zero, 1)
            dve.memset(relb[BUCKETS:BUCKETS + 1, :], NEG).then_inc(s_relb, 1)
            fold(0, bufB)
            dve.wait_ge(cond_hi, 2)
            for s in range(2):
                dve.tensor_tensor(cnd4[:, :, 2 * s + 1], tiny[:, 8 * s:8 * s + 8], cnd4[:, :, 2 * s].bitcast(F32), ALU.subtract)\
                   .then_inc(cond_lo, 1)
            scale_split(0, xlat, lambda t: col("norm_mix", t), 0, bufA, H, None, first=lambda: lo(Slab(0)), second=lambda: lo(Slab(1)))
            lo(Slab(2))
            dve.wait_ge(tab_done, 1)
            dve.tensor_copy(state[0:H_MOBA, 0, 0:2, :], ps[0:H_MOBA, 5, :]).then_inc(tab_sb, 1)

            E1, E2, E3 = bufA[:, 0:1024], bufA[:, 1024:2048], bufB[:, 0:1024]
            heads = lambda a: a.rearrange("p (h t) -> p h t", t=T)
            for n, (kind, g) in enumerate(LEAD):
                lo(Slab(n + RING))
                was, i = LEAD[n - 1] if n else ("", 0)
                if was == "ada" and i % MOST == MOST - 1:
                    mod_add(0, 2 * (i + 1 - MOST), 2 * MOST, ada_bank(i), mod_done, modT_done, i // MOST + 1)
                if kind == "ada":
                    continue
                if g == 2:
                    dve.wait_ge(la_done, 1)
                    dve.scalar_tensor_tensor(bufB[:, 1024:2048], flat(ps[:, 4:6, :]), 0.0, bufB[:, 0:1024],
                                             ALU.min, ALU.subtract).then_inc(la_done, 1)
                if g == 4:
                    dve.wait_ge(b_done, 1)
                    bT = ps[:, 6:8, :].rearrange("p a (h c i) -> p (a h c) i", h=2, c=NCH)
                    dve.tensor_copy(tiny[:, 0:16], bT[:, :, CHUNK - 1]).then_inc(blast, 1)
                    dve.wait_ge(blast, 1)
                    dve.scalar_tensor_tensor(E3.rearrange("p (c i) -> p c i", i=CHUNK), bT, -1.0,
                                             tiny[:, 0:16, None].to_broadcast([P, 16, CHUNK]),
                                             ALU.mult, ALU.add).then_inc(blast, 1)
                    dve.wait_ge(exps_done, 1)
                    dve.tensor_tensor(qa, qa, heads(E1), ALU.mult).then_inc(dec_done, 1)
                    dve.wait_ge(exps_done, 2)
                    dve.tensor_tensor(heads(E2), ka, heads(E2), ALU.mult).then_inc(dec_done, 1)
                    dve.wait_ge(exps_done, 4)
                    dve.tensor_tensor(heads(E3), ka, heads(E3), ALU.mult).then_inc(dec_done, 1)
                if g == 10:
                    dve.wait_ge(tab_out, 16)
                    dve.wait_ge(kv_done, 1)
                    dve.tensor_copy(ka, ps[:, 4:6, :].rearrange("p a (h v) -> p (a h) v", v=DV)).then_inc(state_done, 1)
                    dve.wait_ge(state_done, 1)
                    for c in (1, 2):
                        if c == 2:
                            dve.wait_ge(kv_done, 2)
                        for h in range(H_GLA):
                            prev = ka[:, h, :] if c == 1 else state[:, 0, h, :]
                            bank = (6 if c == 1 else 4) + h // 2
                            if c == 2:
                                dve.wait_ge(state_done, 2 + h)
                            dec = 16 + h * NCH + c
                            dve.scalar_tensor_tensor(state[:, c - 1, h, :], prev, tiny[:, dec:dec + 1],
                                                     ps[:, bank, (h % 2) * DV:(h % 2) * DV + DV], ALU.mult, ALU.add)\
                               .then_inc(state_done, 1)
                if g == 13:
                    dve.wait_ge(o_sq, 1)
                    dve.tensor_copy(bufA[:, :], flat(ps[:, 4:8, :])).then_inc(o_sb, 1)
                if g == 14:
                    dve.wait_ge(ostd_done, 1)
                    order.mark(dve.reciprocal(bufB[:, 0:1024], bufB[:, 0:1024]))
                    dve.wait_ge(dve_order, order.value())
                    dve.wait_ge(o_sb, 1)
                    o = bufA[:, :].rearrange("p (h d t) -> p h d t", h=H_GLA, d=2)
                    order.mark(dve.tensor_tensor(
                        o, o, heads(bufB[:, 0:1024])[:, :, None, :].to_broadcast([P, H_GLA, 2, T]), ALU.mult))
                if g == 18:
                    dve.wait_ge(dve_order, order.value())
                    dve.wait_ge(mix_drained, 19)
                    for t in range(KT):
                        o = bufA[:, t * T:t * T + T]
                        dve.scalar_tensor_tensor(o, o, col("gla_out_norm", t), sra[:, t, :], ALU.mult, ALU.mult)\
                           .then_inc(oa_done, 1)
                if g == 19:
                    for i in range(2):
                        dve.wait_ge(oahi_done, i + 1)
                        dve.tensor_tensor(g_lo[:, 4 * i:4 * i + 4, :], bufA[:, 1024 * i:1024 * i + 1024],
                                          g_hi[:, 4 * i:4 * i + 4, :].bitcast(F32), ALU.subtract).then_inc(oalo_done, 1)
                if g in (16, 19, 22):
                    r = (g - 16) // 3
                    nb = 8 if r == 0 else 4
                    sc = ps[:, 4:6, :].rearrange("p a (h k) -> p (a h) k", h=nb // 2)
                    pr = flat(state[:, 0, :, :]).rearrange("p (h k) -> p h k", h=nb)
                    dve.wait_ge(sc_done, r + 1)
                    order.mark(dve.tensor_reduce(tiny[:, 32:32 + nb], sc, AX.X, ALU.max))
                    dve.wait_ge(dve_order, order.value())
                    if r:
                        dve.wait_ge(pt_done, r)
                    dve.tensor_tensor(pr, sc, tiny[:, 32:32 + nb, None].to_broadcast([P, nb, 1024 // nb]), ALU.subtract)\
                       .then_inc(sub_done, 1)
                if g in (17, 20, 23):
                    dve.wait_ge(e_done, r + 1)
                    order.mark(dve.tensor_reduce(tiny[:, 40:40 + nb], pr, AX.X, ALU.add))
                    dve.wait_ge(dve_order, order.value())
                    order.mark(dve.reciprocal(tiny[:, 48:48 + nb], tiny[:, 40:40 + nb]))
                    dve.wait_ge(dve_order, order.value())
                    dve.tensor_tensor(pr, pr, tiny[:, 48:48 + nb, None].to_broadcast([P, nb, 1024 // nb]), ALU.mult)\
                       .then_inc(p_done, 1)
                if g == 25:
                    modulated(0, 4, mod_done, N_ADA // MOST)
            dve.wait_ge(obhi_done, 1)
            dve.tensor_tensor(flat(m_lo[:, :, :, :]), flat(ps[:, 4:6, :]), flat(m_hi[:, :, :, :].bitcast(F32)), ALU.subtract)\
               .then_inc(oblo_done, 1)

            fold(1, ctx_sq)
            dve.wait_ge(oalo_done, 2)
            for k in range(4):
                lo(Slab(BASE["gla"] + k + RING))
                if k == 2:
                    scale(1, xctx, gain_of(0), ctx_y)
                dve.wait_ge(slab_done, BASE["gla"] + k + 1)
                dve.wait_ge(mix_drained, N_MIX)
                dve.tensor_tensor(bufA[:, 512 * k:512 * k + 512], ps[:, k, :], flat(gates[:, 2 * k:2 * k + 2, :]), ALU.mult)\
                   .then_inc(br_drained, 1)
            split_lo(1, ctx_y, H, shift_of(0, 0, 1))
            for i in range(2):
                lo(Slab(BASE["moba"] + i + RING))
                dve.wait_ge(slab_done, BASE["moba"] + i + 1)
                dve.tensor_tensor(bufB[:, 1024 * i:1024 * i + 1024], flat(ps[:, 4 + 2 * i:6 + 2 * i, :]),
                                  flat(gates[:, KT + 4 * i:KT + 4 * i + 4, :]), ALU.mult).then_inc(br_drained, 1)
                dve.wait_ge(br_drained, 5 + i)
                for k in (2 * i, 2 * i + 1):
                    mix = bufA[:, 512 * k:512 * k + 512]
                    dve.tensor_tensor(mix, mix, bufB[:, 512 * k:512 * k + 512], ALU.add).then_inc(mixed_done, 1)
            dve.memset(vpad[:, :, 0:PADC], 0.0).then_inc(pads_done, 1)
            dve.memset(vpad[:, :, PADC + T:VP], 0.0).then_inc(pads_done, 1)
            b0 = BASE["pw1_ctx_a"]
            lo(Slab(b0 + RING))
            for k in range(4):
                dve.wait_ge(mxhi_done, k + 1)
                dve.tensor_tensor(flat(g_lo[:, 2 * k:2 * k + 2, :]), bufA[:, 512 * k:512 * k + 512],
                                  flat(g_hi[:, 2 * k:2 * k + 2, :].bitcast(F32)), ALU.subtract).then_inc(mxlo_done, 1)
            lo(Slab(b0 + 1 + RING))
            glu(0, 0)
            for k in range(4):
                lo(Slab(BASE["out"] + k + RING))
                dve.wait_ge(slab_done, BASE["out"] + k + 1)
                x = flat(xlat[:, 2 * k:2 * k + 2, :])
                dve.tensor_tensor(x, ps[:, 4 + k, :], x, ALU.add).then_inc(x_ready, 1)
            pw1_dve(0, BASE["pw1_ctx_b"], 2, 2, xlat, bufB, lambda t: col("norm_ffn", t), bufA, G, None)

            dwconv_first(0)
            def residual():
                for q in range(4):
                    x = flat(xlat[:, 2 * q:2 * q + 2, :])
                    outputs(0, "ffn0", q)
                    dve.tensor_tensor(x, ps[:, 4 + q, :], x, ALU.add).then_inc(x_ready, 1)

            ffn_dve(dve, lo, order, 0, "ffn0", dwconv, ln_tail(0, residual))
            ln_scale(0)
            fold(3, bufB)
            lo_ahead("ada_a2", 0, 1)
            ln_lo(0, H)
            scale(3, xlat, lambda t: col("norm_final", t), flat(xlat[:, :, :]), first=lambda: lo_ahead("ada_a2", 1, 2))
            lo_ahead("ada_a2", 2, 3)
            fold(4, bufB)
            lo_ahead("pw2_ctx", 0, 1)
            scale(4, xlat, gain_of(2), bufA)
            split_lo(3, bufA, G, shift_of(0, 0, 0))
            group_add("ada_a")
            dve.wait_ge(xlo_done, KT // 2 * 4)
            pw2_dve("pw2_ctx", xctx, shift_of(0, 2, 1), ahead=1)
            b0 = BASE["pw1_lat"]
            lo(Slab(b0 + RING))
            lo(Slab(b0 + 1 + RING))
            glu(1, 0)
            pw1_dve(1, b0 + 2, 5, 4, xctx, ctx_sq, gain_of(1), ctx_y, H, shift_of(0, 3, 1))

            dwconv_first(1)
            ffn_dve(dve, lo, order, 1, "ffn_ctx", dwconv, ln_tail(1, lambda: gated_residual(1, "ffn_ctx", xctx, shift_of(0, 5, 1))))
            ln_scale(1)
            lo_ahead("ada_b2", 0, 1)
            ln_lo(1, G)
            lo_ahead("ada_b2", 1, 3)
            fold(6, bufB)
            group_add("ada_b")
            modulated(4, 6, mod2_done, GROUPS.index("ada_b") + 1)
            pw2_dve("pw2_lat", xlat, shift_of(0, 2, 0), between=lambda: scale(6, xctx, gain_of(4), ctx_y))
            lo_ahead("ada_c", 0, 1)
            fold(7, bufB)
            lo_ahead("ada_c", 1, 2)
            scale_split(7, xlat, gain_of(3), 5, bufA, H, shift_of(0, 3, 0))
            lo_ahead("ada_c", 2, 4)
            split_lo(6, ctx_y, G, shift_of(1, 0, 1))
            group_add("ada_c")
            def gated(f, use, gate):
                def tail(k):
                    if k == 3:
                        gated_residual(f, use, xlat, gate)
                        fold(8 if f == 2 else 10, bufB)
                return tail

            ffn_dve(dve, lo, order, 2, "ffn_lat", tail=gated(2, "ffn_lat", shift_of(0, 5, 0)))
            dve.wait_ge(khi_done, 1)
            dve.tensor_tensor(k_lo[:, :, T:2 * T], ps[:, 2, :].rearrange("p (a t) -> p a t", a=2), k_hi[:, :, T:2 * T].bitcast(F32),
                              ALU.subtract).then_inc(klo_done, 1)
            scale_split(8, xlat, gain_of(5), 7, bufA, H, shift_of(1, 0, 0), first=lambda: lo_ahead("v_ctx", 0, 1),
                        second=lambda: lo_ahead("ada_d", 0, 2))
            lo_ahead("ada_d", 2, 4)
            group_add("ada_d")
            modulated(6, 7, mod2_done, GROUPS.index("ada_d") + 1)

            b0 = BASE["qkv"]
            cos, sin = (rope_cs[:, i:i + 1, :].to_broadcast([P, 2, T]) for i in range(2))

            def rope(out, raw_, bank, done):
                order.mark(dve.tensor_tensor(out, ps[:, bank, :].rearrange("p (a t) -> p a t", a=2), sin, ALU.mult))
                order.mark(dve.tensor_tensor(raw_, raw_, cos, ALU.mult))
                dve.wait_ge(dve_order, order.value())
                dve.tensor_tensor(out, out, raw_, ALU.add).then_inc(done, 1)

            def q_lo(j):
                dve.wait_ge(qhi_done, j + 1)
                dve.tensor_tensor(g_lo[:, 2 * j:2 * j + 2, :], q_rot[:, 2 * j:2 * j + 2, :], g_hi[:, 2 * j:2 * j + 2, :].bitcast(F32),
                                  ALU.subtract).then_inc(qlo_done, 1)

            def scores_max(n):
                b = n % 2
                c = 8 * b
                dve.wait_ge(ws_done, n + 1)
                if n >= 2:
                    dve.wait_ge(we_done, n - 1)
                order.mark(dve.tensor_reduce(tiny[:, c:c + 2], ps[:, 2 * b:2 * b + 2, :], AX.X, ALU.max))
                dve.wait_ge(dve_order, order.value())
                sink = col("sink", n)
                order.mark(dve.tensor_scalar(tiny[:, c + 2:c + 4], tiny[:, c:c + 2], sink, -1.0, ALU.max, ALU.mult))
                dve.wait_ge(dve_order, order.value())
                dve.tensor_scalar(tiny[:, c + 4:c + 6], tiny[:, c + 2:c + 4], sink, None, ALU.add).then_inc(wmax_done, 1)

            dve.wait_ge(s_late, 16)
            dve.wait_ge(s_consts, 16)
            dve.tensor_copy(eye_b[:, :], eye).then_inc(wmask_ready, 1)
            dve.tensor_copy(wmask_b[:, :, :], wmask).then_inc(wmask_ready, 1)
            for i in range(6):
                lo(Slab(b0 + i + RING))
                if i == 1:
                    dve.wait_ge(krot_done, 1)
                    rope(k_all[:, :, 0:T], k_raw, 4, k_ready)
                if i == 5:
                    scores_max(0)
                if i >= 3:
                    dve.wait_ge(qrot_done, i - 2)
                    rope(q_rot[:, 2 * (i - 3):2 * (i - 3) + 2, :], q_raw[:, 2 * (i - 3):2 * (i - 3) + 2, :], 4 + (i - 2) % 4, q_ready)
                if i == 4:
                    dve.wait_ge(khi_done, 2)
                    dve.tensor_tensor(k_lo[:, :, 0:T], k_all[:, :, 0:T], k_hi[:, :, 0:T].bitcast(F32), ALU.subtract).then_inc(klo_done, 1)
                if i >= 4:
                    q_lo(i - 4)

            def probs(n):
                b = n % 2
                c = 16 + 8 * b
                dve.wait_ge(we_done, n + 1)
                order.mark(dve.tensor_tensor(tiny[:, c + 4:c + 6], tiny[:, c:c + 2], tiny[:, c + 2:c + 4], ALU.add))
                dve.wait_ge(dve_order, order.value())
                order.mark(dve.reciprocal(tiny[:, c + 6:c + 8], tiny[:, c + 4:c + 6]))
                dve.wait_ge(dve_order, order.value())
                for s in range(2):
                    pr = bufA[:, 1024 * b + 512 * s:1024 * b + 512 * s + 512]
                    ins = dve.tensor_scalar(pr, pr, tiny[:, c + 6 + s:c + 7 + s], None, ALU.mult)
                ins.then_inc(wp_done, 1)

            def out_lo(i):
                dve.wait_ge(wohi_done, i + 1)
                dve.tensor_tensor(g_lo[:, i, :], ps[:, 6 + i % 2, 0:T], g_hi[:, i, :].bitcast(F32), ALU.subtract).then_inc(wolo_done, 1)

            for n in range(H2):
                if n >= 5 and n % 2:
                    out_lo((n - 5) // 2)
                if n >= 1:
                    scores_max(n)
                    probs(n - 1)
                if n == 1:
                    dve.wait_ge(qrot_done, 4)
                    rope(q_rot[:, 6:8, :], q_raw[:, 6:8, :], 6, q_ready)
                if n in (2, 3):
                    q_lo(n)
            probs(H2 - 1)
            out_lo(6)
            out_lo(7)
            for i in range(4):
                dve.wait_ge(slab_done, BASE["wo"] + i + 1)
                for m in range(2):
                    t = 2 * i + m
                    ins = dve.scalar_tensor_tensor(xlat[:, t, :], ps[:, i, m * T:m * T + T], mod[:, 1, 2 * KT + t, 0:1], xlat[:, t, :],
                                                   ALU.mult, ALU.add)
                ins.then_inc(x_ready, 1)
                lo(Slab(BASE["wo"] + i + RING))
            fold(9, bufB)
            lo_ahead("ada_e", 0, 1)
            scale_split(9, xlat, gain_of(6), 8, bufA, H, shift_of(1, 3, 0), second=lambda: lo_ahead("ada_e", 1, 2))
            lo_ahead("ada_e", 2, 4)
            group_add("ada_e")
            ffn_dve(dve, lo, order, 3, "ffn2", tail=gated(3, "ffn2", shift_of(1, 5, 0)))
            scale(10, xlat, lambda t: col("final_g", t), flat(xlat[:, :, :]))

        @block.tensor
        def _(pe):
            def mm3(out, w, x, start=False, stop=False):
                pe.matmul(out, w[0], x[0], start=start, stop=False, skip_group_check=True)
                pe.matmul(out, w[0], x[1], start=False, stop=False, skip_group_check=True)
                return pe.matmul(out, w[1], x[0], start=False, stop=stop, skip_group_check=True)

            def weights(g, k):
                pe.wait_ge(lo_done, g.number() + 1)
                pe.wait_ge(lo2_done, g.number() + 1)
                return [a[:, g.slot, :].rearrange("p (k n) -> p k n", k=k) for a in (whi, wlo)]

            def features(g, bank, x, kts=KT, tiles=2, split=None, lo_sem=xlo_done):
                w = weights(g, kts)
                for m in range(tiles):
                    for k in range(kts):
                        if split is not None and m == 0 and k % 2 == 0:
                            pe.wait_ge(lo_sem, KT // 2 * split + k // 2 + 1)
                        ins = mm3(ps[:, bank + m // 2, (m % 2) * T:(m % 2) * T + T],
                                  [a[:, k, m * P:m * P + P] for a in w], [a[:, k, :] for a in x],
                                  start=(k == 0 and m % 2 == 0), stop=(k == kts - 1))
                ins.then_inc(slab_done, 1)

            def tokens(g, bank, x):
                w = weights(g, KT)
                for s in range(2):
                    for k in range(KT):
                        ins = mm3(ps[:, bank, s * T:s * T + T], [a[:, k, s * P:s * P + P] for a in x],
                                  [a[:, k, :] for a in w], start=(k == 0 and s == 0), stop=(k == KT - 1))
                ins.then_inc(slab_done, 1)

            def mean(sums, bank, done, ready, first):
                for i, s in enumerate(sums):
                    pe.wait_ge(ready, first + i + 1)
                    ins = pe.matmul(ps[:, bank, 0:T], ones[:, :], s, start=(i == 0), stop=(i == len(sums) - 1))
                ins.then_inc(done, 1)

            def means(n, bank=4):
                mean([rstd[:, 0, :], rstd[:, 1, :]], bank, ms_done, fold_done, 2 * n)

            def ln_mean(q):
                mean([lstd[:, 0, :]], 0, mu_done, dw_done, q)

            def ln_var(q):
                mean([lstd[:, 0, :], lstd[:, 1, :]], 0, var_done, lfold_done, 2 * q)

            def ada(g, bank, k=0, n=1):
                w = weights(g, KT)
                for t in range(KT):
                    for part in range(2):
                        c = cnd_at + 4 * MOST * t - 4 * k
                        ins = pe.matmul(ps[:, bank, 0:SLABC], cnd[:, c:c + P], w[part][:, t, :],
                                        start=(t == 0 and part == 0 and k == 0), stop=(t == KT - 1 and part == 1 and k == n - 1),
                                        skip_group_check=True)
                ins.then_inc(slab_done, 1)

            def turn_rows(rows, n, bank, done, *ready):
                pe.wait_ge(*ready)
                for m in range(2):
                    c = T + 2 * n * m
                    ins = pe.matmul(ps[:, bank, c:c + 2 * n], rows[0:4 * n, m * P:m * P + P], sel[0:4 * n, 0:2 * n],
                                    start=(m == 0), stop=True, skip_group_check=True)
                ins.then_inc(done, 1)

            def ada_group(use, k0, k1):
                for k in range(k0, k1):
                    ada(Slab(group_slabs(use)[k]), GROUP_BANKS[use][0], k, len(group_slabs(use)))

            def turn_group(use):
                turn_rows(late_rows, len(group_slabs(use)), GROUP_BANKS[use][1], rowsT_done, rows_done, GROUPS.index(use) + 1)

            H, G = (h_hi, h_lo), (g_hi, g_lo)
            pe.wait_ge(s_memset, 3)
            means(0)
            pe.wait_ge(cond_lo, 2)

            for n, (kind, g) in enumerate(LEAD):
                if kind == "ada":
                    if g % MOST == 0 and g >= 2 * MOST:
                        pe.wait_ge(mod_done, g // MOST - 1)
                    ada(Slab(n), ada_bank(g), g % MOST, MOST)
                else:
                    if n >= 4 and LEAD[n - 4][0] == "mix":
                        pe.wait_ge(mix_drained, LEAD[n - 4][1] + 1)
                    elif n % 2:
                        pe.wait_ge(mod_done, N_ADA // MOST - n % 4 // 2)
                    if 5 <= g < 9 or 13 <= g < 15:
                        tokens(Slab(n), n % 4, H)
                    else:
                        features(Slab(n), n % 4, H, tiles=1 if g == 0 else 2, split=0 if g == 0 else None)
                if n == 0:
                    pe.wait_ge(s_relb, 1)
                    pe.wait_ge(s_small, 80)
                    pe.matmul(ps[0:H_MOBA, 5, :], relb[:, :], sra[0:BUCKETS + 1, 0:2, :], start=True, stop=True).then_inc(tab_done, 1)
                was, i = LEAD[n - 1] if n else ("", 0)
                if was == "ada" and i % MOST == MOST - 1:
                    q = i // MOST
                    turn_rows(modrow[:, q % 2, :], MOST, ada_bank(i), modT_done, row_done, q + 1)
                if kind == "ada":
                    continue
                if g == 2:
                    pe.wait_ge(mix_drained, 1)
                    pe.wait_ge(tab_sb, 1)
                    for s in range(2):
                        ins = pe.matmul(ps[:, 4 + s, :], alr[:, s * P:s * P + P], wlr, start=True, stop=True)
                    ins.then_inc(z_done, 1)
                if g == 4:
                    pe.wait_ge(s_consts, 16)
                    pe.wait_ge(la_done, 2)
                    for h in range(H_GLA):
                        for s in range(2):
                            la = bufB[:, 1024 + s * 512 + h * DK:1024 + s * 512 + h * DK + DK]
                            c = (h % 2) * T + s * P
                            ins = pe.matmul(ps[:, 6 + h // 2, c:c + P], la, cum, start=(h % 2 == 0 and s == 0),
                                            stop=True, skip_group_check=True)
                    ins.then_inc(b_done, 1)
                if g == 8:
                    pe.wait_ge(dec_done, 2)
                    for h in range(H_GLA):
                        for s in range(2):
                            a = h * 2 + s
                            ins = pe.matmul(ps[:, 4 + a // 4, (a % 4) * P:(a % 4) * P + P],
                                            bufA[:, 1024 + h * T + s * P:1024 + h * T + s * P + P],
                                            qa[:, h, s * P:s * P + P], start=(a % 4 == 0), stop=True, skip_group_check=True)
                    ins.then_inc(attn_done, 1)
                    pe.wait_ge(dec_done, 3)
                    for h in range(H_GLA):
                        for s in range(2):
                            ins = pe.transpose(ps[:, 6 + s, h * DK:h * DK + DK], bufB[:, h * T + s * P:h * T + s * P + P], eye)
                    ins.then_inc(kteT_done, 1)
                if g in (10, 11):
                    pe.wait_ge(attn_sb, 1)
                    pe.wait_ge(kteT_sb, 1)
                    if g == 11:
                        pe.wait_ge(state_done, 1)
                    for c in (0, 1) if g == 10 else (2,):
                        s, r0 = c // 2, (c % 2) * CHUNK
                        for h in range(H_GLA):
                            bank = (4, 6, 4)[c] + h // 2
                            k = bufB[r0:r0 + CHUNK, 1024 + s * 512 + h * DK:1024 + s * 512 + h * DK + DK]
                            ins = pe.matmul(ps[:, bank, (h % 2) * DV:(h % 2) * DV + DV], k,
                                            va[r0:r0 + CHUNK, s, h * DV:h * DV + DV],
                                            start=(h % 2 == 0), stop=True, skip_group_check=True)
                    ins.then_inc(kv_done, 1)
                if g == 12:
                    pe.wait_ge(attn_masked, 1)
                    pe.wait_ge(state_done, 9)
                    for h in range(H_GLA):
                        for d in range(2):
                            c = d * T
                            for s in range(2):
                                a = h * 2 + s
                                pe.matmul(ps[:, 4 + h, c + s * P:c + s * P + P],
                                          va[:, s, h * DV + d * P:h * DV + d * P + P], bufA[:, a * P:a * P + P],
                                          start=(d == 0 and s == 0), stop=False, skip_group_check=True)
                            for k in range(1, NCH):
                                S = ka[:, h, :] if k == 1 else state[:, k - 2, h, :]
                                ins = pe.matmul(ps[:, 4 + h, c + k * CHUNK:c + k * CHUNK + CHUNK], S[:, d * P:d * P + P],
                                                qa[:, h, k * CHUNK:k * CHUNK + CHUNK], start=False, stop=(k == NCH - 1),
                                                skip_group_check=True)
                    ins.then_inc(o_done, 1)
                if g == 14:
                    pe.wait_ge(o_sq, 1)
                    pe.wait_ge(o_sb, 1)
                    for h in range(H_GLA):
                        for d in range(2):
                            c = (h * 2 + d) * T
                            ins = pe.matmul(ps[:, 4 + h // 2, (h % 2) * T:(h % 2) * T + T], ones[:, :], bufB[:, c:c + T],
                                            start=(h % 2 == 0 and d == 0), stop=(d == 1), skip_group_check=True)
                    ins.then_inc(oms_done, 1)
                if g in (18, 21, 24):
                    r = (g - 18) // 3
                    pe.wait_ge(p_done, r + 1)
                    if r:
                        pe.wait_ge(pt_sb, r)
                    pr = flat(state[:, 0, :, :])
                    for a in range(8):
                        ins = pe.transpose(ps[:, 6 + a // 4, (a % 4) * P:(a % 4) * P + P], pr[:, a * P:a * P + P], eye)
                    ins.then_inc(pt_done, 1)
                if g in (15, 18, 21):
                    r = (g - 15) // 3
                    if r == 0:
                        pe.wait_ge(ostd_done, 1)
                        pe.wait_ge(brev_in, 16)
                        pe.wait_ge(mix_drained, 15)
                    else:
                        pe.wait_ge(sub_done, r)
                    nk = P if r == 0 else T
                    for h in range(8) if r == 0 else range(4 * r - 4, 4 * r):
                        i = place(h, r) * nk
                        out = ps[:, 4 + i // 512, i % 512:i % 512 + nk]
                        r0, q0 = (h % 2) * DH, 0 if r == 0 else P
                        pe.matmul(out, mqk[r0:r0 + DH, 0, h // 2, q0:q0 + P], mqk[r0:r0 + DH, 1, h // 2, 0:nk],
                                  start=(i % 512 == 0), stop=False, skip_group_check=True)
                        ins = pe.matmul(out, rev, brev[:, h, T - nk:T], start=False, stop=True, skip_group_check=True)
                    ins.then_inc(sc_done, 1)
                if g == 25:
                    pe.wait_ge(pt_sb, 3)
                    for h in range(H_MOBA):
                        r0, bank, c = (h % 2) * DH, 4 + h // 4, (h // 2 % 2) * T
                        for q in range(2):
                            out = ps[r0:r0 + DH, bank, c + q * P:c + q * P + P]
                            for k in range(q + 1):
                                a = place(h, 0) if q == 0 else place(h, 1) * 2 + k
                                pt = flat(pt_of(0) if q == 0 else pt_of(1 + h // 4))[:, a * P:a * P + P]
                                ins = pe.matmul(out, mv[:, k, h * DH:h * DH + DH], pt,
                                                start=(h % 4 < 2 and q == 0), stop=(k == q), skip_group_check=True)
                    ins.then_inc(ob_done, 1)

            M = [a[:, :, :, :].rearrange("p a b t -> p (a b) t") for a in (m_hi, m_lo)]
            pe.wait_ge(oalo_done, 2)
            for i in range(4):
                last = max(n for n in range(len(LEAD)) if n % 4 == i)
                pe.wait_ge(mix_drained, LEAD[last][1] + 1)
                features(Slab(BASE["gla"] + i), i, G)
                if i == 1:
                    means(1, bank=6)
            pe.wait_ge(oblo_done, 1)
            pe.wait_ge(std_done, 2)
            for i in range(2):
                features(Slab(BASE["moba"] + i), 4 + 2 * i, M, kts=4, tiles=4)
            pe.wait_ge(br_drained, 4)
            features(Slab(BASE["pw1_ctx_a"]), 0, H, split=1)
            features(Slab(BASE["pw1_ctx_a"] + 1), 1, H)
            pe.wait_ge(mxlo_done, 4)
            for i in range(4):
                features(Slab(BASE["out"] + i), 4 + i, G)

            def pw1_pe(q, b1, n, x):
                for i in range(6):
                    if i >= 2:
                        pe.wait_ge(v_done, 4 * q + i // 2)
                    features(Slab(b1 + i), (2 + i) % 4, x)
                    if i == 1:
                        means(n)

            pw1_pe(0, BASE["pw1_ctx_b"], 2, H)
            ffn_pe(pe, features, mm3, 0, "ffn0", G, 2, [(v_done, 3), (v_done, 4)], tail=lambda: ln_mean(0),
                   before_end=lambda: ada_group("ada_a", 0, 3))

            ada_group("ada_a", 3, 4)
            ln_var(0)
            ada_group("ada_a", 4, 6)
            pe.wait_ge(lstd_done, 1)
            means(3, bank=0)
            for i in range(4):
                features(Slab(BASE["pw2_ctx"] + i), 4 + i, H, split=None if i else 0, lo_sem=clo_done)
                if i == 0:
                    turn_group("ada_a")
                if i == 1:
                    pe.wait_ge(std_done, 4)
                    means(4, bank=0)
            b0 = BASE["pw1_lat"]
            pe.wait_ge(mod2_done, GROUPS.index("ada_a") + 1)
            features(Slab(b0), 0, G, split=3)
            features(Slab(b0 + 1), 1, G)
            pe.wait_ge(x_ready, 12)
            pw1_pe(1, b0 + 2, 5, G)
            ffn_pe(pe, features, mm3, 1, "ffn_ctx", H, 4, [(v_done, 7), (v_done, 8)], tail=lambda: ln_mean(1),
                   before_end=lambda: ada_group("ada_b", 0, 3))

            ada_group("ada_b", 3, 4)
            ln_var(1)
            ada_group("ada_b", 4, 6)
            pe.wait_ge(lstd_done, 2)
            pe.wait_ge(x_ready, 16)
            for i in range(4):
                features(Slab(BASE["pw2_lat"] + i), 4 + i, G, split=None if i else 1, lo_sem=clo_done)
                if i == 0:
                    means(6, bank=0)
                    turn_group("ada_b")
            ada_group("ada_c", 0, 3)
            means(7, bank=0)
            ada_group("ada_c", 3, 4)
            pe.wait_ge(mod2_done, GROUPS.index("ada_b") + 1)
            def k_of_context():
                pe.wait_ge(xlo_done, KT // 2 * 7)
                features(Slab(BASE["k_ctx"]), 2, G)

            ffn_pe(pe, features, mm3, 2, "ffn_lat", H, 5, [(x_ready, 20), (x_ready, 20)], early=lambda: turn_group("ada_c"),
                   before_end=k_of_context)

            tokens(Slab(BASE["v_ctx"]), 3, G)
            means(8)
            ada_group("ada_d", 0, 4)
            b0 = BASE["qkv"]
            features(Slab(b0), 0, H, split=7)
            turn_group("ada_d")
            tokens(Slab(b0 + 1), 1, H)
            pe.wait_ge(mod2_done, GROUPS.index("ada_d") + 1)

            def turn(raw_, bank, done):
                for a in range(2):
                    ins = pe.matmul(ps[:, bank, a * T:a * T + T], rot, raw_[:, a, :], start=(a == 0), stop=True, skip_group_check=True)
                ins.then_inc(done, 1)

            pe.wait_ge(s_late, 16)
            pe.wait_ge(kv_sb, 2)
            turn(k_raw, 4, krot_done)
            for i in range(4):
                if i == 1:
                    pe.wait_ge(kv_sb, 3)
                if i == 2:
                    pe.wait_ge(klo_done, 1)
                features(Slab(b0 + 2 + i), i, H)
                if i >= 1:
                    pe.wait_ge(q_sb, i)
                    turn(q_raw[:, 2 * i - 2:2 * i, :], 4 + i, qrot_done)

            def wscores(n):
                i, u, b = n // 2, n % 2, n % 2
                r0 = u * DH
                pe.wait_ge(qlo_done, i // 2 + 1)
                if n >= 2:
                    pe.wait_ge(we_done, n - 1)
                for s in range(2):
                    mm3(ps[:, 2 * b + s, :], [a[r0:r0 + DH, i, s * P:s * P + P] for a in G],
                        [a[r0:r0 + DH, i // 4, :] for a in (k_hi, k_lo)], start=True)
                    c = P if s == 0 else 0
                    ins = pe.matmul(ps[:, 2 * b + s, c:c + P], eye_b[:, :], wmask_b[:, s, :], start=False, stop=True,
                                    skip_group_check=True)
                ins.then_inc(ws_done, 1)

            def wturn(n):
                b = n % 2
                pe.wait_ge(wp_done, n + 1)
                if n >= 1:
                    pe.wait_ge(wt_sb, n)
                for k in range(4):
                    for s in range(2):
                        a = 2 * k + s
                        ins = pe.transpose(ps[:, 4 + a // 4, (a % 4) * P:(a % 4) * P + P],
                                           bufA[:, 1024 * b + 512 * s + k * P:1024 * b + 512 * s + k * P + P], eye)
                ins.then_inc(wt_done, 1)

            def wout(i):
                pe.wait_ge(wt_sb, 2 * i + 2)
                if i >= 2:
                    pe.wait_ge(wolo_done, i - 1)
                for k in range(4):
                    for u in range(2):
                        kv = 2 * (i // 4) + u
                        ins = pe.matmul(ps[u * DH:u * DH + DH, 6 + i % 2, 0:T], v_all[:, k, kv * DH:kv * DH + DH],
                                        bufB[:, 1024 * u + k * T:1024 * u + k * T + T], start=(k == 0), stop=(k == 3),
                                        skip_group_check=True)
                ins.then_inc(wo_done, 1)

            def wo_first(k0, k1):
                w = weights(Slab(BASE["wo"]), KT)
                pe.wait_ge(wolo_done, k1)
                for m in range(2):
                    for k in range(k0, k1):
                        ins = mm3(ps[:, 0, m * T:m * T + T], [a[:, k, m * P:m * P + P] for a in w], [a[:, k, :] for a in G],
                                  start=(k == 0 and m == 0), stop=(k == KT - 1))
                return ins

            pe.wait_ge(wmask_ready, 2)
            pe.wait_ge(klo_done, 2)
            wscores(0)
            pe.wait_ge(q_sb, 4)
            pe.wait_ge(q_ready, 2)
            turn(q_raw[:, 6:8, :], 6, qrot_done)
            wscores(1)
            for n in range(H2):
                if n + 2 < H2:
                    wscores(n + 2)
                if n == H2 - 1:
                    wo_first(0, KT - 2)
                wturn(n)
                if n >= 2 and n % 2 == 0:
                    wout(n // 2 - 1)
            wout(H2 // 2 - 1)
            wo_first(KT - 2, KT).then_inc(slab_done, 1)
            for i in range(1, 4):
                features(Slab(BASE["wo"] + i), i, G)
            ada_group("ada_e", 0, 1)
            means(9)
            ada_group("ada_e", 1, 4)
            ffn_pe(pe, features, mm3, 3, "ffn2", H, 8, [(x_ready, 28), (x_ready, 28)], early=lambda: turn_group("ada_e"))
            means(10)


def kernel(**inputs):
    import concourse.bacc as bacc
    from concourse.bass_utils import run_bass_kernel_spmd as run

    a = {k: np.asarray(v) for k, v in inputs.items()}
    COL, NCOL = columns()
    STORE, n_slabs = stored()

    def tiles(v):
        return np.ascontiguousarray(np.asarray(v).reshape(-1, P).T)

    w = np.zeros((n_slabs, P, SLAB), np.float32)

    def put(name, i, block):
        k = block.shape[0] // P
        w[STORE[name][0] + i] = block.reshape(k, P, -1).transpose(1, 0, 2).reshape(P, SLAB)

    def put_columns(name, i, mat, c0):
        put(name, i, mat[:, c0:c0 + SLABC])

    def put_ffn(name, up, down):
        ups = [0] + [3 * j - 1 for j in range(1, NJ)]
        for j, i in enumerate(ups):
            put_columns(name, i, up, j * SLABC)
            put_columns(name, i + 1, up, D_FF + j * SLABC)
            put(name, 3 * NJ - 1 if j == NJ - 1 else 3 * j + 4, down[j * SLABC:(j + 1) * SLABC])

    win = a["w_in"][0]
    o_qa, o_ka, o_va, o_ra = 0, GLA_W, 2 * GLA_W, 2 * GLA_W + V_W
    o_lr = o_ra + V_W
    o_qb = o_lr + RANK
    o_kb, o_vb, o_g = o_qb + MOBA_W, o_qb + 2 * MOBA_W, o_qb + 3 * MOBA_W
    lr = np.zeros((D, SLABC), np.float32)
    lr[:, 0:RANK] = win[:, o_lr:o_lr + RANK]
    put("lead", AT["mix", 0], lr)
    i = 1
    for c0, width in [(o_ka, GLA_W), (o_qa, GLA_W), (o_va, V_W), (o_kb, MOBA_W), (o_qb, MOBA_W), (o_vb, MOBA_W),
                      (o_ra, V_W), (o_g, 2 * D)]:
        for c in range(c0, c0 + width, SLABC):
            put_columns("lead", AT["mix", i], win, c)
            i += 1
    for i in range(2):
        put("moba", i, a["w_branch_moba"][0][:, i * 512:(i + 1) * 512])
    for i in range(4):
        put_columns("gla", i, a["w_branch_gla"][0], i * SLABC)
        put_columns("out", i, a["w_out"][0], i * SLABC)
    put_ffn("ffn0", a["w_up"][0], a["w_down"][0])
    for layer in range(2):
        for i in range(N_ADA):
            put_columns(*(("lead", AT["ada", i]) if layer == 0 else ("ada1", i)), a["ada_w_2"][layer], i * SLABC)
        put_ffn(f"ffn{layer + 1}", a["ffn_w_up_2"][layer], a["ffn_w_down_2"][layer])
    for j in range(4):
        put_columns("pw1", 2 * j, a["conv_w_pw1_2"][0], j * SLABC)
        put_columns("pw1", 2 * j + 1, a["conv_w_pw1_2"][0], D + j * SLABC)
        put_columns("pw2", j, a["conv_w_pw2_2"][0], j * SLABC)
    pairs = [(h, h + 4) for g in (0, 8) for h in range(g, g + 4)]
    by_pair = np.concatenate([np.arange(h * DH, (h + 1) * DH) for p in pairs for h in p])
    wqkv = a["attn_w_qkv_2"][0]
    put_columns("qkv", 0, wqkv, H2 * DH)
    put_columns("qkv", 1, wqkv, (H2 + HKV) * DH)
    wq, wo = wqkv[:, :H2 * DH][:, by_pair], a["attn_w_o_2"][0][by_pair]
    for i in range(4):
        put_columns("qkv", 2 + i, wq, i * SLABC)
        put_columns("wo", i, wo, i * SLABC)

    cols = np.zeros((P, NCOL), np.float32)

    def put_cols(name, v):
        c, k = COL[name]
        cols[:, c:c + k] = tiles(v)

    put_cols("norm_mix", a["norm_mix"][0])
    put_cols("gla_out_norm", a["gla_out_norm"][0])
    put_cols("norm_ffn", a["norm_ffn"][0])
    put_cols("norm_final", a["norm_final"])
    put_cols("ffn_w0", a["conv_w"][0])
    put_cols("ffn_b0", a["conv_b"][0])
    for layer in range(2):
        put_cols(f"ffn_w{layer + 1}", a["ffn_w_dw_2"][layer])
        put_cols(f"ffn_b{layer + 1}", a["ffn_b_dw_2"][layer])
        put_cols(f"norm1_{layer}", a["norm1_g_2"][layer])
        put_cols(f"norm2_{layer}", a["norm2_g_2"][layer])
        put_cols(f"ada_b{layer}", a["ada_b_2"][layer])
    put_cols("final_g", a["final_g_2"])
    for name, key in [("pw1_b", "conv_b_pw1_2"), ("dw_w", "conv_w_dw_2"), ("dw_b", "conv_b_dw_2"), ("ln_g", "conv_ln_g_2"),
                      ("ln_b", "conv_ln_b_2"), ("pw2_b", "conv_b_pw2_2")]:
        put_cols(name, a[key][0])
    put_cols("cond", np.concatenate([a["c_2"][0], a["c_ctx_2"]]))
    c, k = COL["sink"]
    cols[:, c:c + k] = a["attn_sink_2"][0][[h for p in pairs for h in p]][None, :]

    eye = np.eye(P, dtype=np.float32)
    tok = np.arange(P)
    cum = ((tok[:, None] <= tok[None, :]) & (tok[:, None] // CHUNK == tok[None, :] // CHUNK)) / TAU
    consts = np.stack([eye, eye[::-1], cum.astype(np.float32)], axis=1)
    dist = T - 1 - np.arange(2 * T)
    half = BUCKETS // 2
    far = half + (np.log(np.maximum(dist, 1).astype(np.float32) / half) / np.float32(np.log(MAX_DIST / half))
                  * (BUCKETS - half)).astype(np.int32)
    bucket = np.where(dist < half, dist, np.minimum(far, BUCKETS - 1))
    bucket = np.where(dist < 0, BUCKETS, bucket)
    onehot = (np.arange(BUCKETS + 1)[:, None] == bucket[None, :]).astype(np.float32)

    pos = np.arange(T)
    freqs = (np.float32(ROPE_BASE) ** (-np.arange(DH // 4, dtype=np.float32) / (DH // 4))).astype(np.float32)
    angle = np.concatenate([(pos // GRID_W).astype(np.float32)[:, None] * freqs, (pos % GRID_W).astype(np.float32)[:, None] * freqs], axis=1)
    rope = [np.tile(f(angle).T.astype(np.float32), (4, 1)) for f in (np.cos, np.sin)]
    rot = np.zeros((P, P), np.float32)
    for h in (0, DH):
        for d in range(DH // 2):
            rot[h + DH // 2 + d, h + d] = -1.0
            rot[h + d, h + DH // 2 + d] = 1.0
    outside = [np.where(tok[None, :] > tok[:, None], NEG, 0.0), np.where(tok[None, :] < tok[:, None], NEG, 0.0)]
    tables = np.concatenate(rope + [rot] + outside, axis=1).astype(np.float32)
    sel = np.kron(np.eye(2 * MOST, dtype=np.float32), np.ones((2, 1), np.float32))

    arrays = {
        "tables": tables, "sel": sel,
        "ctxT": np.ascontiguousarray(a["ctx_2"][0].T.reshape(KT, P, T).transpose(1, 0, 2)),
        "w": w, "cols": cols, "consts": np.ascontiguousarray(consts), "onehot": onehot.reshape(BUCKETS + 1, 2, T),
        "xT": np.ascontiguousarray(a["x"][0].T.reshape(KT, P, T).transpose(1, 0, 2)),
        "rel_bias": a["rel_bias"], "w_lr_up": a["w_lr_up"][0], "b_forget": a["b_forget"],
    }
    arrays = {f"{k}_dram": np.ascontiguousarray(v) for k, v in arrays.items()}

    nc = bacc.Bacc("TRN2", target_bir_lowering=False, num_devices=1)
    io = {k[:-5]: nc.dram_tensor(k, v.shape, F32, kind="ExternalInput").ap() for k, v in arrays.items()}
    io["out"] = nc.dram_tensor("out_dram", (P, KT, T), F32, kind="ExternalOutput").ap()
    io["scratch"] = nc.dram_tensor("bias_rows", (H_MOBA, 512), F32, kind="Internal").ap()
    build(nc, io)
    got = run(nc, [arrays], core_ids=[0]).results[0]["out_dram"]
    return np.ascontiguousarray(got.transpose(2, 1, 0).reshape(1, T, D))
```
